# Optimizing a Trainium2 kernel written in Bass

```python
import jax, jax.numpy as jnp
from jax import lax
import numpy as np
import math

D_MODEL = 1024
BATCH = 1
SEQ = 1024
DEPTH = 1

CHUNK = 64
PLE_DIM = 256
EPS = 1e-6
A_HEADS = 4
A_DK = 128
A_DV = 128
A_WIDTH = A_HEADS * A_DV
B_HEADS = 8
B_HD = 64
B_WIDTH = B_HEADS * B_HD
B_LEFT_CHUNKS = 8
B_BAND = (B_LEFT_CHUNKS + 1) * CHUNK
MAX_REL = 128
N_REL = 2 * MAX_REL + 1
D_FF = ((8 * D_MODEL // 3 + 255) // 256) * 256
IN_SIZES = (A_HEADS * A_DK, A_HEADS * A_DK, A_WIDTH, A_WIDTH,
            B_WIDTH, B_WIDTH, B_WIDTH,
            D_MODEL, D_MODEL)
D_IN = sum(IN_SIZES)


def rmsnorm(x, g):
    x32 = x.astype(jnp.float32)
    y = x32 * lax.rsqrt(jnp.mean(x32 * x32, axis=-1, keepdims=True) + EPS)
    return (y * g.astype(jnp.float32)).astype(x.dtype)

def head_rms(t, g):
    t32 = t.astype(jnp.float32)
    return t32 * lax.rsqrt(jnp.mean(t32 * t32, axis=-1, keepdims=True) + EPS) * g.astype(jnp.float32)

def hgrn2_mixer(q, f_logit, i, g, lb, onorm_g):
    f32 = jnp.float32
    bsz, seq, _ = q.shape
    nc = seq // CHUNK
    lb32 = lb.astype(f32)
    logf = jnp.logaddexp(jnp.log(lb32), jnp.log1p(-lb32) + jax.nn.log_sigmoid(f_logit.astype(f32)))
    k = 1.0 - jnp.exp(logf)

    def heads(t, d):
        return t.astype(f32).reshape(bsz, nc, CHUNK, A_HEADS, d).transpose(1, 0, 3, 2, 4)

    qc = heads(q, A_DK) * (A_DK ** -0.5)
    kc = heads(k, A_DK)
    lfc = heads(logf, A_DK)
    ic = heads(i, A_DV)
    causal = jnp.tril(jnp.ones((CHUNK, CHUNK), dtype=bool))

    def step(state, inp):
        qt, kt, lft, it = inp
        b = jnp.cumsum(lft, axis=-2)
        o_inter = jnp.einsum('bhtk,bhkv->bhtv', qt * jnp.exp(b), state)
        diff = b[..., :, None, :] - b[..., None, :, :]
        dec = jnp.exp(jnp.where(causal[:, :, None], diff, -jnp.inf))
        attn = jnp.einsum('bhtk,bhsk,bhtsk->bhts', qt, kt, dec)
        o = o_inter + jnp.einsum('bhts,bhsv->bhtv', attn, it)
        b_last = b[..., -1:, :]
        new_state = (jnp.exp(b_last[..., 0, :])[..., None] * state
                     + jnp.einsum('bhsk,bhsv->bhkv', kt * jnp.exp(b_last - b), it))
        return new_state, o

    s0 = jnp.zeros((bsz, A_HEADS, A_DK, A_DV), f32)
    _, o = lax.scan(step, s0, (qc, kc, lfc, ic))
    o = o.transpose(1, 0, 3, 2, 4).reshape(bsz, seq, A_HEADS, A_DV)
    o = head_rms(o, onorm_g).reshape(bsz, seq, A_WIDTH) * jax.nn.silu(g.astype(f32))
    return o.astype(q.dtype)

def band_attention(q, k, v, qn_g, kn_g, rel_bias):
    f32 = jnp.float32
    bsz, seq, _ = q.shape
    nc = seq // CHUNK
    qh = head_rms(q.reshape(bsz, seq, B_HEADS, B_HD), qn_g)
    kh = head_rms(k.reshape(bsz, seq, B_HEADS, B_HD), kn_g)
    vh = v.reshape(bsz, seq, B_HEADS, B_HD).astype(f32)
    pad = B_LEFT_CHUNKS * CHUNK
    kp = jnp.pad(kh, ((0, 0), (pad, 0), (0, 0), (0, 0)))
    vp = jnp.pad(vh, ((0, 0), (pad, 0), (0, 0), (0, 0)))
    band_idx = (jnp.arange(nc) * CHUNK)[:, None] + jnp.arange(B_BAND)[None, :]
    kb = kp[:, band_idx]
    vb = vp[:, band_idx]
    qc = qh.reshape(bsz, nc, CHUNK, B_HEADS, B_HD)
    scores = jnp.einsum('bnqhd,bnkhd->bnhqk', qc, kb) * (B_HD ** -0.5)
    rel = (pad + jnp.arange(CHUNK))[:, None] - jnp.arange(B_BAND)[None, :]
    bias = rel_bias.astype(f32)[:, jnp.clip(rel, -MAX_REL, MAX_REL) + MAX_REL]
    valid = band_idx >= pad
    scores = jnp.where(valid[None, :, None, None, :], scores + bias[None, None], -1e30)
    probs = jax.nn.softmax(scores, axis=-1)
    o = jnp.einsum('bnhqk,bnkhd->bnqhd', probs, vb)
    return o.reshape(bsz, seq, B_WIDTH).astype(q.dtype)

def first_inputs(seed: int = 0) -> dict:
    key = jax.random.key(seed)
    ks = jax.random.split(key, 24)
    f32 = jnp.float32

    def nrm(k, shape, scale):
        return jax.random.normal(k, shape, f32) * scale

    def gain(k, shape):
        return 1.0 + 0.02 * jax.random.normal(k, shape, f32)

    return {
        "x": nrm(ks[0], (BATCH, SEQ, D_MODEL), 1.0),
        "p": nrm(ks[1], (DEPTH, BATCH, SEQ, PLE_DIM), 1.0),
        "norm_mix_g": gain(ks[2], (DEPTH, D_MODEL)),
        "w_in": nrm(ks[3], (DEPTH, D_MODEL, D_IN), D_MODEL ** -0.5),
        "hgrn_lb_logits": nrm(ks[4], (DEPTH, A_HEADS * A_DK), 0.5),
        "hgrn_onorm_g": gain(ks[5], (DEPTH, A_DV)),
        "attn_qnorm_g": gain(ks[6], (DEPTH, B_HD)),
        "attn_knorm_g": gain(ks[7], (DEPTH, B_HD)),
        "attn_rel_bias": nrm(ks[8], (DEPTH, B_HEADS, N_REL), 0.3),
        "w_branch_a": nrm(ks[9], (DEPTH, A_WIDTH, D_MODEL), A_WIDTH ** -0.5),
        "w_branch_b": nrm(ks[10], (DEPTH, B_WIDTH, D_MODEL), B_WIDTH ** -0.5),
        "w_out": nrm(ks[11], (DEPTH, D_MODEL, D_MODEL), 0.5 * D_MODEL ** -0.5),
        "norm_ffn_g": gain(ks[12], (DEPTH, D_MODEL)),
        "w_ffn_gate": nrm(ks[13], (DEPTH, D_MODEL, D_FF), D_MODEL ** -0.5),
        "w_ffn_up": nrm(ks[14], (DEPTH, D_MODEL, D_FF), D_MODEL ** -0.5),
        "w_ffn_down": nrm(ks[15], (DEPTH, D_FF, D_MODEL), 0.5 * D_FF ** -0.5),
        "norm_ple_g": gain(ks[16], (DEPTH, D_MODEL)),
        "w_ple_gate": nrm(ks[17], (DEPTH, D_MODEL, D_MODEL), D_MODEL ** -0.5),
        "w_ple_proj": nrm(ks[18], (DEPTH, PLE_DIM, D_MODEL), 0.5 * PLE_DIM ** -0.5),
    }

def first_block(x, p, norm_mix_g, w_in, hgrn_lb_logits, hgrn_onorm_g, attn_qnorm_g, attn_knorm_g,
              attn_rel_bias, w_branch_a, w_branch_b, w_out, norm_ffn_g, w_ffn_gate, w_ffn_up,
              w_ffn_down, norm_ple_g, w_ple_gate, w_ple_proj):
    lb_soft = jax.nn.softmax(hgrn_lb_logits.astype(jnp.float32), axis=0)
    lb_cum = jnp.cumsum(lb_soft, axis=0)
    lower_bounds = lb_cum - lb_cum[0:1]
    split_at = [int(s) for s in np.cumsum(IN_SIZES)[:-1]]

    for li in range(DEPTH):
        h = rmsnorm(x, norm_mix_g[li])
        z = h @ w_in[li]
        qa, fa, ia, ga, qb, kb, vb, gate_a, gate_b = jnp.split(z, split_at, axis=-1)
        oa = hgrn2_mixer(qa, fa, ia, ga, lower_bounds[li], hgrn_onorm_g[li])
        ob = band_attention(qb, kb, vb, attn_qnorm_g[li], attn_knorm_g[li], attn_rel_bias[li])
        merged = (jax.nn.sigmoid(gate_a) * (oa @ w_branch_a[li])
                  + jax.nn.sigmoid(gate_b) * (ob @ w_branch_b[li]))
        x = x + merged @ w_out[li]
        h2 = rmsnorm(x, norm_ffn_g[li])
        x = x + (jax.nn.silu(h2 @ w_ffn_gate[li]) * (h2 @ w_ffn_up[li])) @ w_ffn_down[li]
        h3 = rmsnorm(x, norm_ple_g[li])
        x = x + jax.nn.sigmoid(h3 @ w_ple_gate[li]) * (p[li].astype(x.dtype) @ w_ple_proj[li])
    return x


DEPTH_2 = 2

N_A = max(1, DEPTH_2 // 2)
N_B = DEPTH_2 - N_A

D_RNN = 1280
RNN_BLOCKS = 10
RNN_BW = D_RNN // RNN_BLOCKS
CONV_WIDTH = 4
LRU_C = 8.0

N_HEADS = 8
QK_NOPE = 128
QK_ROPE = 64
V_DIM = 128
KV_RANK = 256
Q_RANK = 384
ROPE_THETA = 10000.0
Q_BLOCK = 128
ATTN_SCALE = (QK_NOPE + QK_ROPE) ** -0.5


def rms_norm(x, g):
    xf = x.astype(jnp.float32)
    y = xf * lax.rsqrt(jnp.mean(xf * xf, axis=-1, keepdims=True) + EPS)
    return (y * g.astype(jnp.float32)).astype(x.dtype)

def rope_tables(seq_len):
    pos = jnp.arange(seq_len, dtype=jnp.float32)
    inv = ROPE_THETA ** (-jnp.arange(0, QK_ROPE, 2, dtype=jnp.float32) / QK_ROPE)
    ang = pos[:, None] * inv[None, :]
    return jnp.cos(ang), jnp.sin(ang)

def apply_rope(x, cos, sin):
    xf = x.astype(jnp.float32)
    x1, x2 = jnp.split(xf, 2, axis=-1)
    out = jnp.concatenate([x1 * cos - x2 * sin, x2 * cos + x1 * sin], axis=-1)
    return out.astype(x.dtype)

def causal_depthwise_conv(x, w, b):
    c = x.shape[-1]
    y = lax.conv_general_dilated(
        x, w[:, None, :].astype(x.dtype), window_strides=(1,),
        padding=[(CONV_WIDTH - 1, 0)], dimension_numbers=("NWC", "WIO", "NWC"),
        feature_group_count=c)
    return y + b

def _lin_combine(left, right):
    a1, b1 = left
    a2, b2 = right
    return a1 * a2, a2 * b1 + b2

def rglru_layer(x, norm_g, w_in, conv_w, conv_b, w_rg, b_rg, w_ig, b_ig, lam, w_out):
    bsz, seq, _ = x.shape
    h = rms_norm(x, norm_g)
    u = h @ w_in
    xb, gate = u[..., :D_RNN], u[..., D_RNN:]
    xb = causal_depthwise_conv(xb, conv_w, conv_b)
    xblk = xb.reshape(bsz, seq, RNN_BLOCKS, RNN_BW)
    r = jax.nn.sigmoid(jnp.einsum("bsnc,ncd->bsnd", xblk, w_rg).reshape(bsz, seq, D_RNN) + b_rg)
    i = jax.nn.sigmoid(jnp.einsum("bsnc,ncd->bsnd", xblk, w_ig).reshape(bsz, seq, D_RNN) + b_ig)
    log_a = -LRU_C * r.astype(jnp.float32) * jax.nn.softplus(-lam.astype(jnp.float32))
    a = jnp.exp(log_a)
    bterm = jnp.sqrt(-jnp.expm1(2.0 * log_a)) * (i * xb).astype(jnp.float32)
    _, hs = lax.associative_scan(_lin_combine, (a, bterm), axis=1)
    y = hs.astype(x.dtype) * jax.nn.silu(gate)
    return y @ w_out

def mla_shared_kv(x_stream, norm_kv, w_dkv, kv_norm, w_uk, w_uv, cos, sin):
    h = rms_norm(x_stream, norm_kv)
    ckr = h @ w_dkv
    c_kv = rms_norm(ckr[..., :KV_RANK], kv_norm)
    k_rope = apply_rope(ckr[..., KV_RANK:], cos[None], sin[None])
    k_nope = jnp.einsum("bsc,chd->bshd", c_kv, w_uk)
    v = jnp.einsum("bsc,chd->bshd", c_kv, w_uv)
    return k_nope, k_rope, v

def causal_block_attention(q_nope, q_rope, k_nope, k_rope, v):
    bsz, seq, nh, _ = q_nope.shape
    nb = seq // Q_BLOCK
    qn = q_nope.reshape(bsz, nb, Q_BLOCK, nh, QK_NOPE).transpose(1, 0, 2, 3, 4)
    qr = q_rope.reshape(bsz, nb, Q_BLOCK, nh, QK_ROPE).transpose(1, 0, 2, 3, 4)
    kpos = jnp.arange(seq)

    def one_block(args):
        qn_b, qr_b, bi = args
        s = jnp.einsum("bqhd,bkhd->bhqk", qn_b, k_nope, preferred_element_type=jnp.float32)
        s = s + jnp.einsum("bqhr,bkr->bhqk", qr_b, k_rope, preferred_element_type=jnp.float32)
        s = s * ATTN_SCALE
        qpos = bi * Q_BLOCK + jnp.arange(Q_BLOCK)
        mask = kpos[None, :] <= qpos[:, None]
        s = jnp.where(mask[None, None], s, -jnp.inf)
        p = jax.nn.softmax(s, axis=-1)
        return jnp.einsum("bhqk,bkhd->bqhd", p.astype(v.dtype), v)

    o = lax.map(one_block, (qn, qr, jnp.arange(nb)))
    return o.transpose(1, 0, 2, 3, 4).reshape(bsz, seq, nh, V_DIM)

def mla_layer(x, norm_g, w_in, q_norm, w_uq, w_out, k_nope, k_rope, v, cos, sin):
    bsz, seq, _ = x.shape
    h = rms_norm(x, norm_g)
    u = h @ w_in
    c_q = rms_norm(u[..., :Q_RANK], q_norm)
    gate = u[..., Q_RANK:]
    q = jnp.einsum("bsc,chd->bshd", c_q, w_uq)
    q_nope = q[..., :QK_NOPE]
    q_rope = apply_rope(q[..., QK_NOPE:], cos[None, :, None], sin[None, :, None])
    o = causal_block_attention(q_nope, q_rope, k_nope, k_rope, v)
    y = o.reshape(bsz, seq, N_HEADS * V_DIM) * jax.nn.silu(gate)
    return y @ w_out

def second_inputs(seed: int = 0) -> dict:
    key = jax.random.key(seed)
    ks = jax.random.split(key, 24)
    f32 = jnp.float32
    nrm = lambda k, shape, fan_in: jax.random.normal(k, shape, f32) * (fan_in ** -0.5)
    gain = lambda k, shape: 1.0 + 0.02 * jax.random.normal(k, shape, f32)
    small = lambda k, shape: 0.01 * jax.random.normal(k, shape, f32)

    u = jax.random.uniform(ks[8], (N_A, D_RNN), f32, 0.9, 0.999)
    a0 = u ** (1.0 / LRU_C)
    lam = jnp.log(a0) - jnp.log1p(-a0)

    return {
        "x": jax.random.normal(ks[0], (BATCH, SEQ, D_MODEL), f32),
        "norm_a": gain(ks[1], (N_A, D_MODEL)),
        "w_in_a": nrm(ks[2], (N_A, D_MODEL, 2 * D_RNN), D_MODEL),
        "conv_w": nrm(ks[3], (N_A, CONV_WIDTH, D_RNN), CONV_WIDTH),
        "conv_b": small(ks[4], (N_A, D_RNN)),
        "w_rg": nrm(ks[5], (N_A, RNN_BLOCKS, RNN_BW, RNN_BW), RNN_BW),
        "b_rg": small(ks[6], (N_A, D_RNN)),
        "w_ig": nrm(ks[7], (N_A, RNN_BLOCKS, RNN_BW, RNN_BW), RNN_BW),
        "b_ig": small(ks[9], (N_A, D_RNN)),
        "lru_lambda": lam,
        "w_out_a": nrm(ks[10], (N_A, D_RNN, D_MODEL), D_RNN),
        "norm_kv": gain(ks[11], (D_MODEL,)),
        "w_dkv": nrm(ks[12], (D_MODEL, KV_RANK + QK_ROPE), D_MODEL),
        "kv_norm": gain(ks[13], (KV_RANK,)),
        "w_uk": nrm(ks[14], (KV_RANK, N_HEADS, QK_NOPE), KV_RANK),
        "w_uv": nrm(ks[15], (KV_RANK, N_HEADS, V_DIM), KV_RANK),
        "norm_b": gain(ks[16], (N_B, D_MODEL)),
        "w_in_b": nrm(ks[17], (N_B, D_MODEL, Q_RANK + N_HEADS * V_DIM), D_MODEL),
        "q_norm": gain(ks[18], (N_B, Q_RANK)),
        "w_uq": nrm(ks[19], (N_B, Q_RANK, N_HEADS, QK_NOPE + QK_ROPE), Q_RANK),
        "w_out_b": nrm(ks[20], (N_B, N_HEADS * V_DIM, D_MODEL), N_HEADS * V_DIM),
        "final_norm": gain(ks[21], (D_MODEL,)),
    }

def second_block(x, norm_a, w_in_a, conv_w, conv_b, w_rg, b_rg, w_ig, b_ig, lru_lambda, w_out_a,
              norm_kv, w_dkv, kv_norm, w_uk, w_uv,
              norm_b, w_in_b, q_norm, w_uq, w_out_b, final_norm):
    seq = x.shape[1]
    cos, sin = rope_tables(seq)
    k_nope = k_rope = v = None
    for layer in range(DEPTH_2):
        if layer < N_A:
            x = x + rglru_layer(x, norm_a[layer], w_in_a[layer], conv_w[layer], conv_b[layer],
                                w_rg[layer], b_rg[layer], w_ig[layer], b_ig[layer],
                                lru_lambda[layer], w_out_a[layer])
        else:
            if layer == N_A:
                k_nope, k_rope, v = mla_shared_kv(x, norm_kv, w_dkv, kv_norm, w_uk, w_uv, cos, sin)
            j = layer - N_A
            x = x + mla_layer(x, norm_b[j], w_in_b[j], q_norm[j], w_uq[j], w_out_b[j],
                              k_nope, k_rope, v, cos, sin)
    return rms_norm(x, final_norm)


def setup_inputs(seed=0):
    out = dict(first_inputs(seed))
    for name, value in second_inputs(seed + 1).items():
        if name != "x":
            out[name + "_2"] = value
    return out


def reference(
    x, p, norm_mix_g, w_in, hgrn_lb_logits, hgrn_onorm_g, attn_qnorm_g, attn_knorm_g,
    attn_rel_bias, w_branch_a, w_branch_b, w_out, norm_ffn_g, w_ffn_gate, w_ffn_up, w_ffn_down,
    norm_ple_g, w_ple_gate, w_ple_proj, norm_a_2, w_in_a_2, conv_w_2, conv_b_2, w_rg_2, b_rg_2,
    w_ig_2, b_ig_2, lru_lambda_2, w_out_a_2, norm_kv_2, w_dkv_2, kv_norm_2, w_uk_2, w_uv_2,
    norm_b_2, w_in_b_2, q_norm_2, w_uq_2, w_out_b_2, final_norm_2,
):
    x = first_block(
        x, p, norm_mix_g, w_in, hgrn_lb_logits, hgrn_onorm_g, attn_qnorm_g, attn_knorm_g,
        attn_rel_bias, w_branch_a, w_branch_b, w_out, norm_ffn_g, w_ffn_gate, w_ffn_up,
        w_ffn_down, norm_ple_g, w_ple_gate, w_ple_proj,
    )
    return second_block(
        x, norm_a_2, w_in_a_2, conv_w_2, conv_b_2, w_rg_2, b_rg_2, w_ig_2, b_ig_2, lru_lambda_2,
        w_out_a_2, norm_kv_2, w_dkv_2, kv_norm_2, w_uk_2, w_uv_2, norm_b_2, w_in_b_2, q_norm_2,
        w_uq_2, w_out_b_2, final_norm_2,
    )


_drawn_inputs = setup_inputs


def setup_inputs(seed=0):
    import zlib

    import numpy as np

    out = dict(_drawn_inputs(seed))
    spreads = {}
    factors = {'norm_mix_g': 6.799,
     'hgrn_onorm_g': 8.0,
     'attn_qnorm_g': 8.0,
     'attn_knorm_g': 8.0,
     'attn_rel_bias': 6.69,
     'norm_ffn_g': 6.873,
     'norm_ple_g': 8.0,
     'norm_a_2': 6.205,
     'b_rg_2': 8.0,
     'b_ig_2': 8.0,
     'norm_kv_2': 8.0,
     'kv_norm_2': 8.0,
     'norm_b_2': 8.0,
     'q_norm_2': 8.0,
     'final_norm_2': 2.838}
    for name, (base, spread) in spreads.items():
        noise = np.random.default_rng([zlib.crc32(name.encode()), seed]).standard_normal(out[name].shape)
        drawn = base * np.exp(spread * noise) if base else spread * noise
        out[name] = __import__('jax').numpy.asarray(drawn.astype(out[name].dtype))
    for name, factor in factors.items():
        out[name] = (out[name] * factor).astype(out[name].dtype)
    return out
```

```python
import numpy as np
from contextlib import ExitStack
import concourse.bass as bass
from concourse import mybir

F32 = mybir.dt.float32
F32R = mybir.dt.float32r
ACT = mybir.ActivationFunctionType
ALU = mybir.AluOpType
AX = mybir.AxisListType

P = 128
D = 1024
S = 1024
HALF = 512
EPS = 1e-6
DC = D // P
A_HEADS = 4
HEADS_B = 8
HD_B = 64
D_FF = 2816
FF_GROUPS = (8, 8, 6)
RNN = 1280
RB = RNN // P
HEADS_C = 8
SCALE_C = float((128 + 64) ** -0.5)
NEG = -1e30
LEVELS = (64, 32, 16, 8, 4, 2, 1)
NT = S // P

G_MIX, G_FFN, G_PLE, G_A, G_KV, G_B, G_FIN = 0, 8, 16, 24, 32, 40, 48
V_ONORM, V_QN, V_KN = 56, 57, 58
V_CB, V_LAM, V_BR, V_BI, V_CW = 59, 69, 79, 89, 99
V_KVN, V_CQN, V_EPS, V_CFAR, V_ONE = 139, 141, 144, 145, 153
NVEC = 154

STREAM = [
    ("gates", 16, 1, 8), ("zb", 12, 1, 8), ("za", 16, 1, 8), ("merge", 8, 2, 4), ("wout", 8, 1, 8),
    ("gu0", 16, 1, 8), ("dn0", 8, 1, 8), ("gu1", 16, 1, 8), ("dn1", 8, 1, 8), ("gu2", 12, 1, 8), ("dn2", 8, 1, 6),
    ("proj", 2, 4, 2), ("pleg", 8, 1, 8), ("xg", 2 * RB, 1, 8),
    ("wo1", 8, 1, 5), ("wo2", 8, 1, 5), ("dkv", 3, 1, 8), ("cq", 3, 1, 8), ("cgate", 8, 1, 8),
    ("uk", 2, 4, 2), ("uv", 2, 4, 2), ("uq0", 3, 2, 3), ("uq1", 3, 2, 3), ("wob", 8, 1, 8),
]
STAGE = {}
_u = _t = 0
for _name, _n, _T, _C in STREAM:
    STAGE[_name] = (_u, _t, _n, _T, _C)
    _u += _n
    _t += _n * _T
UNITS = _u
MM_PER_UNIT = 16


def half_of(h):
    return slice(h * HALF, (h + 1) * HALF)


def items_of(eng, n, body):
    for j in range(min(2, n)):
        body(0, j)
    pairs = n // 2
    if pairs == 2:
        for j in range(2):
            body(1, j)
    elif pairs > 2:
        with eng.Fori(1, pairs) as i:
            for j in range(2):
                body(i, j)
    if n % 2 and n > 2:
        body(n // 2, 0)


def chunk_of(t, m):
    return t[:, m] if isinstance(m, int) else t[:, bass.ds(m, 1)]


def await_at_least(eng, semaphore, count):
    if not isinstance(count, int) or count > 0:
        eng.wait_ge(semaphore, count)


def fused_kernel(nc, a):
    ctx = ExitStack()
    with ctx:
        def sem(name):
            return ctx.enter_context(nc.semaphore(name))

        BASE = (nc.sbuf_base + 31) // 32 * 32
        REG = 32768

        def at(name, shape, off, dt=F32):
            return nc.alloc_sbuf_tensor_at(name, shape, dt, offset=BASE + off)

        def R(r, kib=0):
            return r * REG + kib * 1024

        RING = R(5)
        w_staged = at("w_staged", [P, 2, 1024], RING)
        w_high = at("w_high", [P, 2, 1024], RING + 8192, F32R)
        w_low = at("w_low", [P, 2, 1024], RING + 16384, F32R)
        MISC = RING + 24576
        rstd = at("rstd", [P, S], MISC)
        sq = at("squares", [P, 2, S], MISC + 4096)
        acc = at("square_sum", [P, S], MISC + 12288)
        tmp = at("tmp", [P, S], MISC + 16384)
        ident = at("identity", [P, P], MISC + 20480)
        ones = at("ones", [P, P], MISC + 20992)
        vec = at("vectors", [P, NVEC], MISC + 21504)
        derived = at("derived_vectors", [P, 80], MISC + 21504 + 640)
        stat = at("softmax_stats", [P, 16], MISC + 21504 + 960)

        def V(c, n=1):
            return vec[:, c:c + n]

        eps = V(V_EPS)
        q_gain_scaled = derived[:, 0:1]

        def full(name, region, dt=F32, kib=0, chunks=8):
            return at(name, [P, chunks, S], R(region, kib), dt)

        def f32(t):
            return t.bitcast(F32)

        ps = ctx.enter_context(nc.psum_tensor("ps", [P, 8, HALF], F32))

        x1 = full("x_in", 0)
        h1H, h1L = full("h_mix_high", 1, F32R), full("h_mix_low", 2, F32R)
        zb = full("z_band", 3, chunks=12)
        qk_b, v_raw = zb[:, 0:8], zb[:, 8:12]
        v_tok = at("v_band_by_token", [P, NT, HEADS_B * HD_B], R(4, 16))
        bias = at("band_bias", [P, HEADS_B, 256], R(4, 0))
        o_tok = at("o_band_by_token", [P, 2, HEADS_B * HD_B], R(4, 8))
        head_ones = at("head_ones", [P, P], MISC + 22528)
        far_mask = at("far_mask", [P, 64], MISC + 23040)
        probs_b = at("probs_band", [P, 2, 640], MISC + 4096)
        probsT_b = at("probs_band_T", [P, 2, 640], MISC + 12288)
        obH, obL = full("o_band_high", 0, F32R, 0, 4), full("o_band_low", 0, F32R, 16, 4)
        CH = A_HEADS * P
        za = at("z_hgrn", [P, 4, NT, A_HEADS, P], R(3))
        zq, zf, zi, zg = [za[:, w].rearrange("p c h t -> p (c h t)") for w in range(4)]
        hb = at("hgrn_log_decay", [P, NT * CH], R(1))
        attn = at("hgrn_attn", [P, NT * CH], R(1, 16))
        hd = at("hgrn_decays", [P, NT * CH], R(2))
        hqk = at("hgrn_decayed_qk", [P, NT * CH], R(2, 16))
        masks = at("level_masks", [P, 8, P], MISC)
        states = at("hgrn_state", [P, 2, CH], MISC + 4096)
        chunk_decay = at("hgrn_chunk_decay", [P, NT * A_HEADS], MISC + 8192)
        oaH, oaL = full("o_hgrn_high", 1, F32R, 0, 4), full("o_hgrn_low", 1, F32R, 16, 4)
        mgH, mgL = full("merged_high", 3, F32R), full("merged_low", 4, F32R)
        gate_in = at("gates_loaded", [P, 2, 2, S], MISC + 4096)
        x2 = full("x_mid", 2)
        h2H, h2L = full("h_ffn_high", 0, F32R), full("h_ffn_low", 1, F32R)
        actH, actL = full("act_high", 3, F32R), full("act_low", 4, F32R)
        proj = full("ple_proj", 3)
        p_in = full("p_in", 4, F32, 0, 2)
        pH, pL = full("p_high", 4, F32R, 8, 2), full("p_low", 4, F32R, 16, 2)
        h4H, h4L = full("h_rnn_high", 3, F32R), full("h_rnn_low", 4, F32R)
        xb = full("rnn_in", 0, F32, 0, RB)
        rgate = full("rnn_gate", 1, F32, 8, RB)
        yH, yL = full("rnn_y_high", 0, F32R, 0, RB), full("rnn_y_low", 1, F32R, 8, RB)
        conv = at("rnn_conv", [P, S], MISC + 4096)
        convH, convL = at("rnn_conv_high", [P, S], MISC + 8192, F32R), at("rnn_conv_low", [P, S], R(2, 16), F32R)
        r_buf = at("rnn_r", [P, S], MISC + 12288)
        i_buf = at("rnn_i", [P, S], MISC + 16384)
        w_ri = at("rnn_gate_weights", [P, RB, 2 * P], R(2, 20))
        w_riH, w_riL = [at(f"rnn_gate_weights_{n}", [P, 2 * P], R(2, k), F32R) for n, k in (("high", 30), ("low", 31))]
        x4 = full("x_late", 3)
        h5H, h5L = full("h_kv_high", 1, F32R), full("h_kv_low", 2, F32R)
        h6H, h6L = full("h_mla_high", 0, F32R), full("h_mla_low", 4, F32R)
        ckv = sq
        ckvH, ckvL = full("ckv_high", 2, F32R, 0, 2), full("ckv_low", 2, F32R, 8, 2)
        cq = full("cq", 2, F32, 16, 3)
        cqH, cqL = full("cq_high", 1, F32R, 0, 3), full("cq_low", 1, F32R, 12, 3)
        k_rope = at("k_rope", [P, S], R(1, 24))
        rotate = at("rope_rotate", [P, P], R(1, 28))
        causal = at("causal_mask", [P, P], R(1, 28) + 512)
        o_mla = at("o_mla_by_token", [P, 2, P], R(1, 28) + 1024)
        cos_sin = at("cos_sin", [P, 2, S], R(2, 24))
        cgate = full("mla_gate", 3)
        k_nope = full("k_nope", 0)
        v_mla = full("v_mla", 4)
        q_nope = full("q_nope", 2, F32, 0, 4)
        q_rope = full("q_rope", 2, F32, 16, 2)
        probs_c = at("probs_mla", [P, 2, S], MISC + 4096)
        probsT_c = at("probs_mla_T", [P, 2, S], MISC + 12288)
        y7H, y7L = full("y_mla_high", 0, F32R), full("y_mla_low", 4, F32R)
        x5 = full("x_last", 1)
        out_sb = full("x_out", 2)

        s_load = [sem(f"unit_loaded{j}") for j in range(2)]
        s_split = sem("unit_split")
        s_mm = sem("tile_done")
        s_free = [sem(f"bank{b}_read") for b in range(4)]
        s_const = sem("constants_loaded")
        s_x = [sem(f"x_loaded{k}") for k in range(4)]
        s_h = sem("chunk_high")
        s_l = sem("chunk_low")
        s_nsum = sem("norm_summed")
        s_ln, s_rstd = sem("logarithm"), sem("norm_rstd")
        s_ldone, s_vchain = sem("lambda_exp"), sem("vector_chain")
        s_wh = sem("unit_high")
        s_gz, s_gs = sem("gate_scaled"), sem("gate_sigmoid")
        s_gst = [sem(f"gate_stored{j}") for j in range(2)]
        s_bsq, s_bsum, s_brstd, s_bn = [sem(f"head_norm_{n}") for n in ("square", "sum", "rstd", "done")]
        s_vT, s_vt = sem("v_transposed"), sem("v_by_token")
        s_bconst, s_bias = sem("band_constants"), sem("bias_ready")
        s_ha, s_hp, s_hk, s_hscan = sem("hgrn_softplus"), sem("hgrn_logf"), sem("hgrn_k"), sem("hgrn_scan")
        s_lD, s_lE, s_lQ, s_lS, s_lP = [sem(f"level_{n}") for n in ("difference", "decay", "qk", "scores", "placed")]
        s_hm = sem("level_masks_loaded")
        s_eb, s_qe, s_kb, s_ke, s_kd = [sem(f"state_{n}") for n in ("exp_b", "q", "k_difference", "exp_k", "k")]
        s_hT, s_hTe = sem("hgrn_transposed"), sem("hgrn_transposed_read")
        s_hU, s_hst, s_hO, s_hOe = sem("state_update"), sem("state_new"), sem("hgrn_o"), sem("hgrn_o_read")
        s_h2, s_hn, s_hrstd, s_hw = sem("o_squared"), sem("o_summed"), sem("o_rstd"), sem("o_normed")
        s_hout, s_hoh, s_hol = sem("o_gated"), sem("o_high"), sem("o_low")
        s_gin = [sem(f"gates_in{j}") for j in range(2)]
        s_mg, s_mgh, s_mgl = sem("merged"), sem("merged_high"), sem("merged_low")
        s_x2 = sem("x_mid_loaded")
        s_silu, s_act, s_acth, s_actl = sem("silu"), sem("act"), sem("act_high"), sem("act_low")
        s_p, s_ph, s_pl, s_sig, s_pc, s_pz = [sem(f"ple_{n}") for n in ("loaded", "high", "low", "sigmoid", "product", "added")]
        s_xs3, s_xld4 = sem("x_spilled"), sem("x_reloaded")
        s_rg, s_cv, s_ch, s_cl = sem("rnn_gate_silu"), sem("conv_chain"), sem("conv_high"), sem("conv_low")
        s_wri, s_wrh, s_wrl = sem("gate_weights_loaded"), sem("gate_weights_high"), sem("gate_weights_low")
        s_ri, s_sg, s_ix, s_a, s_T, s_rs, s_rw = [sem(f"rnn_{n}") for n in ("products", "sigmoid", "ix", "a", "tanh", "sqrt", "chain")]
        s_yg, s_yh, s_yl = sem("rnn_y"), sem("rnn_y_high"), sem("rnn_y_low")
        s_xs5, s_xld5, s_cconst = sem("x_spilled_2"), sem("x_reloaded_2"), sem("mla_constants")
        s_c2, s_cs, s_crstd, s_cw, s_cwh, s_cwl = [sem(f"latent_{n}") for n in ("square", "sum", "rstd", "chain", "high", "low")]
        s_rot, s_kr, s_cg = sem("k_rotated"), sem("k_rope_chain"), sem("mla_gate_silu")
        s_rq, s_rotq, s_rqe, s_qready = [sem(f"q_rope_{n}") for n in ("raw", "rotated", "chain", "ready")]
        s_y7h, s_y7l = sem("mla_y_high"), sem("mla_y_low")
        s_out, s_fin = sem("out_stored"), sem("out_ready")

        block = ctx.enter_context(nc.Block())

        def base(stage):
            u0, t0, n, T, C = STAGE[stage]
            return u0, t0, n * T, MM_PER_UNIT // (2 * T)

        def mm_count(stage, item, h):
            u0, _, _, inc = base(stage)
            return item * (2 * inc) + (MM_PER_UNIT * u0 + inc * (h + 1))

        def bank_of(stage, j, h):
            return 2 * ((STAGE[stage][1] + j) % 2) + h

        def use_of(stage, i, j):
            return i + (STAGE[stage][1] + j) // 2

        @block.sync
        def _(sp):
            for k in range(4):
                sp.dma_start(x1[:, 2 * k:2 * k + 2], a["xT"][:, 2 * k:2 * k + 2]).then_inc(s_x[k], 16)

            def load(i, j):
                u = 2 * i + j
                await_at_least(sp, s_split, u - 1)
                sp.dma_start(w_staged[:, j], a["weights"][bass.ds(u, 1)].rearrange("u p n -> p (u n)")).then_inc(s_load[j], 16)

            items_of(sp, UNITS, load)
            for h in range(2):
                sp.wait_ge(s_fin, 4 * (h + 1))
                sp.dma_start(a["outT"][:, 4 * h:4 * h + 4], out_sb[:, 4 * h:4 * h + 4]).then_inc(s_out, 16)
            sp.wait_ge(s_out, 32)

        @block.gpsimd
        def _(pool):
            def split(i, j):
                u = 2 * i + j
                pool.wait_ge(s_load[j], (i + 1) * 16)
                if not (isinstance(i, int) and i == 0):
                    pool.wait_ge(s_mm, (u - 1) * MM_PER_UNIT)
                nc.gpsimd.tensor_tensor(derived[0:1, 72:73], w_staged[0:1, j, 0:1], w_staged[0:1, j, 0:1], ALU.add)
                nc.gpsimd.tensor_copy(w_high[:, j], w_staged[:, j]).then_inc(s_wh, 1)
                pool.wait_ge(s_wh, u + 1)
                nc.gpsimd.tensor_tensor(w_low[:, j], w_staged[:, j], f32(w_high[:, j]), ALU.subtract).then_inc(s_split, 1)

            items_of(pool, UNITS, split)

        class Attention:
            def __init__(self, name, items, width, scale, probs, probsT):
                self.items, self.width, self.scale, self.probs, self.probsT = items, width, scale, probs, probsT
                (self.scored, self.maxed, self.negated, self.probed, self.transposed, self.copied, self.summed,
                 self.inverted, self.out, self.outT, self.outH, self.outL) = [
                    sem(f"{name}_{n}") for n in ("scores", "max", "neg_max", "probs", "probs_T", "probs_T_copied",
                                                 "o", "inverse", "o_by_token", "o_T", "o_high", "o_low")]

            def scores_of(self, n):
                b = 2 * (n % 2)
                return ps[:, b:b + 2].rearrange("p b n -> p (b n)")[:, 0:self.items[n][2] * P]

        transposed_flat = ps[:, 4:6].rearrange("p b n -> p (b n)")

        def attention_tensor(pe, at_, scores, values, deferred, bank_free):
            N = len(at_.items)

            def emit_scores(n):
                await_at_least(pe, at_.probed, n - 1)
                scores(n, 2 * (n % 2)).then_inc(at_.scored, 1)

            emit_scores(0)
            emit_scores(1)
            for n, (h, j, nk) in enumerate(at_.items):
                pe.wait_ge(at_.probed, n + 1)
                await_at_least(pe, at_.copied, n)
                for k in range(nk):
                    last = nc.tensor.transpose(transposed_flat[:, k * P:(k + 1) * P],
                                               at_.probs[:, n % 2, k * P:(k + 1) * P], ident[:])
                last.then_inc(at_.transposed, 1)
                if n + 2 < N:
                    emit_scores(n + 2)
                pe.wait_ge(at_.copied, n + 1)
                await_at_least(pe, at_.out, n - 1)
                if n >= 2:
                    bank_free(n - 2)
                for k in range(nk):
                    last = nc.tensor.matmul(ps[:, 6 + n % 2, 0:at_.width],
                                            at_.probsT[:, n % 2, k * P:(k + 1) * P], values(n, k),
                                            start=(k == 0), stop=(k == nk - 1))
                last.then_inc(at_.summed, 1)
                if n >= 1:
                    deferred(n - 1)
            deferred(N - 1)

        def attention_scalar(act, at_, deferred):
            N = len(at_.items)
            for n, (h, j, nk) in enumerate(at_.items):
                q = n % 4
                act.wait_ge(at_.negated, n + 1)
                await_at_least(act, at_.transposed, n - 1)
                nc.scalar.activation(at_.probs[:, n % 2, 0:nk * P], at_.scores_of(n), ACT.Exp,
                                     bias=stat[:, 4 + q:5 + q], scale=at_.scale,
                                     accum_out=stat[:, 8 + q:9 + q]).then_inc(at_.probed, 1)
                if n >= 3:
                    deferred(n - 3)
            for n in range(N - 3, N):
                deferred(n)

        def attention_vector(dve, at_, destination, deferred):
            N = len(at_.items)
            for n in range(N + 2):
                if n < N:
                    q = n % 4
                    dve.wait_ge(at_.scored, n + 1)
                    nc.vector.reduce_max(stat[:, q:q + 1], at_.scores_of(n), AX.X).then_inc(at_.maxed, 1)
                    dve.wait_ge(at_.maxed, n + 1)
                    nc.vector.tensor_scalar(stat[:, 4 + q:5 + q], stat[:, q:q + 1], -at_.scale, None,
                                            ALU.mult).then_inc(at_.negated, 1)
                if 1 <= n <= N:
                    m = n - 1
                    nk = at_.items[m][2]
                    dve.wait_ge(at_.transposed, m + 1)
                    await_at_least(dve, at_.summed, m - 1)
                    nc.vector.tensor_copy(at_.probsT[:, m % 2, 0:nk * P], transposed_flat[:, 0:nk * P]).then_inc(at_.copied, 1)
                if n >= 2:
                    m = n - 2
                    q = m % 4
                    dve.wait_ge(at_.probed, m + 1)
                    nc.vector.reciprocal(stat[:, 12 + q:13 + q], stat[:, 8 + q:9 + q]).then_inc(at_.inverted, 1)
                    dve.wait_ge(at_.inverted, m + 1)
                    dve.wait_ge(at_.summed, m + 1)
                    destination(m, ps[:, 6 + m % 2, 0:at_.width], stat[:, 12 + q:13 + q]).then_inc(at_.out, 1)
                if n >= 3:
                    deferred(n - 3)
            deferred(N - 1)

        band = Attention("band", [(h, j, min(j + 1, 5)) for j in range(NT) for h in range(HEADS_B)], HD_B, 1.0, probs_b, probsT_b)
        mla = [Attention(f"mla{g}", [(4 * g + h, j, j + 1) for j in range(NT) for h in range(4)], P, SCALE_C, probs_c, probsT_c)
               for g in range(2)]

        @block.tensor
        def _(pe):
            def tile(stage, i, j, slot, width, column, chunks, rhs, first_wait=None):
                u0, t0, _, inc = base(stage)
                for h in range(2):
                    bank = bank_of(stage, j, h)
                    await_at_least(pe, s_free[bank], use_of(stage, i, j))
                    for n, (c, r) in enumerate(chunks):
                        if first_wait and h == 0:
                            pe.wait_ge(*first_wait(r))
                        wH = w_high[:, slot, c * width + column:c * width + column + P]
                        wL = w_low[:, slot, c * width + column:c * width + column + P]
                        tok = half_of(h)
                        nc.tensor.matmul(ps[:, bank], wH, rhs[0][:, r, tok], start=(n == 0), stop=False)
                        nc.tensor.matmul(ps[:, bank], wH, rhs[1][:, r, tok], start=False, stop=False)
                        last = nc.tensor.matmul(ps[:, bank], wL, rhs[0][:, r, tok], start=False, stop=(n == len(chunks) - 1))
                    last.then_inc(s_mm, inc)

            def gemm(stage, rhs, ready, hook=None, chunk0=0, after=None):
                u0, t0, n, T, C = STAGE[stage]

                def unit(i, j):
                    pe.wait_ge(s_split, 2 * i + (j + u0 + 1))
                    first = isinstance(i, int) and i == 0 and j == 0
                    tile(stage, i, j, (u0 + j) % 2, P, 0, [(c, chunk0 + c) for c in range(C)], rhs, ready if first else None)
                    if first and hook:
                        hook()
                    if after and j == 1:
                        after(i)

                items_of(pe, n, unit)

            def low(q):
                return lambda r: (s_l, 8 * q + r + 1)

            def norm(n, q):
                def hook():
                    pe.wait_ge(s_l, 8 * q + 8)
                    for h in range(2):
                        nc.tensor.matmul(ps[:, 4 + h], ones[:], acc[:, half_of(h)], start=True, stop=True).then_inc(s_nsum, 1)
                return hook

            pe.wait_ge(s_const, 48)
            gemm("gates", (h1H, h1L), low(0), norm(0, 0))
            gemm("zb", (h1H, h1L), None)

            pe.wait_ge(s_bconst, 32)
            for n in range(16):
                pe.wait_ge(s_bsq, n + 1)
                await_at_least(pe, s_brstd, n - 1)
                nc.tensor.matmul(ps[:, 4 + n % 2], head_ones[:], tmp[:, half_of(n % 2)], start=True, stop=True).then_inc(s_bsum, 1)
            for t in range(NT):
                await_at_least(pe, s_vt, t - 1)
                for c in range(4):
                    last = nc.tensor.transpose(ps[:, 6 + t % 2, c * P:(c + 1) * P], v_raw[:, c, t * P:(t + 1) * P], ident[:])
                last.then_inc(s_vT, 1)
            pe.wait_ge(s_vt, NT)
            pe.wait_ge(s_bn, 16)
            pe.wait_ge(s_bias, 2 * HEADS_B)

            def band_key_order(j, nk):
                near = [j - 1, j] if nk > 1 else [j]
                far = [t for t in (j - 3, j - 2) if t >= 0 and j - t < nk]
                return near + far + ([j - 4] if nk == 5 else [])

            def band_scores(n, bank):
                h, j, nk = band.items[n]
                rows = slice(64 * (h % 2), 64 * (h % 2) + 64)
                q = qk_b[rows, h // 2, j * P:(j + 1) * P]
                order = band_key_order(j, nk)
                near = min(nk, 2)
                out = ps[:, bank, 0:near * P]
                nc.tensor.matmul(out, q, qk_b[rows, 4 + h // 2, order[0] * P:(order[0] + near) * P], start=True, stop=False)
                last = nc.tensor.matmul(out, ident[:], bias[:, h, 256 - near * P:256], start=False, stop=True)
                far = min(nk, 4) - near
                if far > 0:
                    k0 = order[near] * P
                    last = nc.tensor.matmul(ps[:, bank, 256:256 + far * P], q, qk_b[rows, 4 + h // 2, k0:k0 + far * P], start=True, stop=True)
                if nk == 5:
                    k0 = (j - 4) * P
                    nc.tensor.matmul(ps[:, bank + 1, 0:P], q, qk_b[rows, 4 + h // 2, k0:k0 + P], start=True, stop=False)
                    last = nc.tensor.matmul(ps[:, bank + 1, 0:64], ident[:], far_mask[:], start=False, stop=True)
                return last

            def band_values(n, k):
                h, j, nk = band.items[n]
                return v_tok[:, band_key_order(j, nk)[k], h * HD_B:(h + 1) * HD_B]

            def band_out_T(m):
                h, j, _ = band.items[m]
                if h == HEADS_B - 1:
                    pe.wait_ge(band.out, m + 1)
                    for c in range(4):
                        last = nc.tensor.transpose(ps[:, 6 + m % 2, c * P:(c + 1) * P], o_tok[:, j % 2, c * P:(c + 1) * P], ident[:])
                    last.then_inc(band.outT, 1)

            def band_bank_free(m):
                h, j, _ = band.items[m]
                if h == HEADS_B - 1:
                    pe.wait_ge(band.outL, j + 1)

            attention_tensor(pe, band, band_scores, band_values, band_out_T, band_bank_free)
            pe.wait_ge(band.outL, NT)

            gemm("za", (h1H, h1L), None)

            for n in range(16):
                half = n % 2
                src = hqk
                if n < 14:
                    pe.wait_ge(s_lQ, n + 1)
                for c in range(4 * half, 4 * half + 4):
                    await_at_least(pe, s_lP, 8 * (n // 2) + c - 7)
                    for h in range(A_HEADS):
                        k0 = (c * A_HEADS + h) * P
                        if n < 14:
                            lhs, rhs = hqk[:, k0:k0 + P], hqk[:, k0:k0 + P]
                        else:
                            lhs, rhs = zf[:, k0:k0 + P], zq[:, k0:k0 + P]
                        last = nc.tensor.matmul(ps[:, c, h * P:(h + 1) * P], lhs, rhs, start=True, stop=True)
                    last.then_inc(s_lS, 1)
            pe.wait_ge(s_lP, 64)
            for n in range(16):
                c = n // 2
                if n % 2 == 0:
                    pe.wait_ge(s_kd, c // 4 + 1)
                await_at_least(pe, s_hTe, n - 3)
                for h in range(A_HEADS):
                    k0 = (c * A_HEADS + h) * P
                    src = hqk if n % 2 == 0 else zi
                    last = nc.tensor.transpose(ps[:, n % 4, h * P:(h + 1) * P], src[:, k0:k0 + P], ident[:])
                last.then_inc(s_hT, 1)
            pe.wait_ge(s_qe, 2)
            for c in range(NT):
                pe.wait_ge(s_hTe, 2 * c + 2)
                if c < NT - 1:
                    await_at_least(pe, s_hst, c - 1)
                    for h in range(A_HEADS):
                        k0 = (c * A_HEADS + h) * P
                        last = nc.tensor.matmul(ps[:, 6 + c % 2, h * P:(h + 1) * P], hb[:, k0:k0 + P], zf[:, k0:k0 + P], start=True, stop=True)
                    last.then_inc(s_hU, 1)
                await_at_least(pe, s_hOe, c - 1)
                await_at_least(pe, s_hst, c)
                for h in range(A_HEADS):
                    k0 = (c * A_HEADS + h) * P
                    out = ps[:, 4 + c % 2, h * P:(h + 1) * P]
                    last = nc.tensor.matmul(out, zf[:, k0:k0 + P], attn[:, k0:k0 + P], start=True, stop=(c == 0))
                    if c:
                        last = nc.tensor.matmul(out, states[:, (c - 1) % 2, h * P:(h + 1) * P], hd[:, k0:k0 + P], start=False, stop=True)
                last.then_inc(s_hO, 1)
            for c in range(NT):
                pe.wait_ge(s_h2, c + 1)
                await_at_least(pe, s_hrstd, c - 1)
                nc.tensor.matmul(ps[:, c % 2], ones[:], hqk[:, c * CH:(c + 1) * CH], start=True, stop=True).then_inc(s_hn, 1)
            pe.wait_ge(s_hrstd, NT)

            u0 = STAGE["merge"][0]
            pe.wait_ge(s_hol, NT)

            def merge(i, j):
                pe.wait_ge(s_split, 2 * i + (j + u0 + 1))
                for part, rhs in enumerate(((oaH, oaL), (obH, obL))):
                    tile("merge", 2 * i + j, part, (u0 + j) % 2, P, 0, [(4 * part + c, c) for c in range(4)], rhs)

            items_of(pe, DC, merge)
            gemm("wout", (mgH, mgL), lambda r: (s_mgl, r + 1))
            for g, n in enumerate(FF_GROUPS):
                pairs0 = sum(FF_GROUPS[:g])
                gemm(f"gu{g}", (h2H, h2L), low(1) if g == 0 else None, norm(1, 1) if g == 0 else None)
                gemm(f"dn{g}", (actH, actL), lambda r, p0=pairs0: (s_actl, p0 + r + 1))

            def wide(stage, rhs, ready, moving_weights=False):
                u0, t0, n, T, C = STAGE[stage]
                if ready:
                    pe.wait_ge(*ready)
                for u in range(n):
                    pe.wait_ge(s_split, u0 + u + 1)
                    for r in range(T):
                        t = u * T + r
                        tile(stage, t // 2, t % 2, (u0 + u) % 2, T * P, r * P, [(c, c) for c in range(C)], rhs)

            wide("proj", (pH, pL), (s_pl, 2))
            gemm("pleg", (h2H, h2L), low(2), norm(2, 2))

            def rnn_gates(n):
                pe.wait_ge(s_cl, n + 1)
                pe.wait_ge(s_wrl, n + 1)
                await_at_least(pe, s_sg, 2 * n)
                for g in range(2):
                    wH, wL = [w[:, g * P:(g + 1) * P] for w in (w_riH, w_riL)]
                    for h in range(2):
                        bank, tok = 4 + 2 * g + h, half_of(h)
                        nc.tensor.matmul(ps[:, bank], wH, convH[:, tok], start=True, stop=False)
                        nc.tensor.matmul(ps[:, bank], wH, convL[:, tok], start=False, stop=False)
                        nc.tensor.matmul(ps[:, bank], wL, convH[:, tok], start=False, stop=True).then_inc(s_ri, 1)

            gemm("xg", (h4H, h4L), low(3), norm(3, 3), after=rnn_gates)
            gemm("wo1", (yH, yL), lambda r: (s_yl, r + 1))
            gemm("wo2", (yH, yL), lambda r: (s_yl, r + 1), None, 5)
            gemm("dkv", (h5H, h5L), low(5), norm(4, 4))
            gemm("cq", (h6H, h6L), low(6))

            def latent():
                for k, chunks in enumerate((2, 3)):
                    for c in range(chunks):
                        n = 2 * k + c
                        pe.wait_ge(s_c2, n + 1)
                        await_at_least(pe, s_crstd, 2 * k)
                        for h in range(2):
                            nc.tensor.matmul(ps[:, 4 + h], ones[:], acc[:, half_of(h)], start=(c == 0), stop=(c == chunks - 1)).then_inc(s_cs, 1)

            gemm("cgate", (h6H, h6L), None, latent)
            pe.wait_ge(s_cconst, 48)
            for h in range(2):
                nc.tensor.matmul(ps[:, 6 + h], rotate[:], tmp[:, half_of(h)], start=True, stop=True).then_inc(s_rot, 1)
            wide("uk", (ckvH, ckvL), (s_cwl, 2))
            u0, t0, _, _, _ = STAGE["uv"]
            for v in range(2):
                pe.wait_ge(s_split, u0 + v + 1)
                for r in range(4):
                    for h in range(2):
                        t = 4 * v + r
                        bank = bank_of("uv", t % 2, h)
                        pe.wait_ge(s_free[bank], use_of("uv", t // 2, t % 2))
                        tok = slice((2 * r + h) * P, (2 * r + h + 1) * P)
                        for c in range(2):
                            wH = w_high[:, (u0 + v) % 2, c * HALF:(c + 1) * HALF]
                            wL = w_low[:, (u0 + v) % 2, c * HALF:(c + 1) * HALF]
                            nc.tensor.matmul(ps[:, bank], ckvH[:, c, tok], wH, start=(c == 0), stop=False)
                            nc.tensor.matmul(ps[:, bank], ckvL[:, c, tok], wH, start=False, stop=False)
                            last = nc.tensor.matmul(ps[:, bank], ckvH[:, c, tok], wL, start=False, stop=(c == 1))
                        last.then_inc(s_mm, 2)
            for g in range(2):
                at_ = mla[g]
                wide(f"uq{g}", (cqH, cqL), (s_cwl, 5) if g == 0 else None)
                for n in range(4):
                    pe.wait_ge(s_rq, g + 1)
                    if n >= 2:
                        pe.wait_ge(s_qready, 4 * g + n - 1)
                    nc.tensor.matmul(ps[:, 4 + n % 2], rotate[:], q_rope[:, n // 2, half_of(n % 2)], start=True, stop=True).then_inc(s_rotq, 1)
                pe.wait_ge(s_qready, 4 * (g + 1))

                def mla_scores(n, bank):
                    h, j, nk = at_.items[n]
                    hl = h % 4
                    rows = slice(64 * (hl % 2), 64 * (hl % 2) + 64)
                    for b in range((nk + 3) // 4):
                        k0, k1 = b * HALF, min((b + 1) * HALF, nk * P)
                        out = ps[:, bank + b, 0:k1 - k0]
                        diagonal = k1 == nk * P
                        nc.tensor.matmul(out, q_nope[:, hl, j * P:(j + 1) * P], k_nope[:, h, k0:k1], start=True, stop=False)
                        last = nc.tensor.matmul(out, q_rope[rows, hl // 2, j * P:(j + 1) * P], k_rope[rows, k0:k1], start=False, stop=not diagonal)
                        if diagonal:
                            last = nc.tensor.matmul(ps[:, bank + b, k1 - k0 - P:k1 - k0], ident[:], causal[:], start=False, stop=True)
                    return last

                def mla_values(n, k):
                    h = at_.items[n][0]
                    return v_mla[:, k, h * P:(h + 1) * P]

                def mla_out_T(m):
                    pe.wait_ge(at_.out, m + 1)
                    nc.tensor.transpose(ps[:, 6 + m % 2, 0:P], o_mla[:, m % 2], ident[:]).then_inc(at_.outT, 1)

                attention_tensor(pe, at_, mla_scores, mla_values, mla_out_T, lambda m: pe.wait_ge(at_.outL, m + 1))
                pe.wait_ge(at_.outL, len(at_.items))
            gemm("wob", (y7H, y7L), lambda r: (s_y7l, r + 1))
            norm(5, 7)()

        @block.scalar
        def _(act):
            def split_x(q, x, H, gain, ready=None, squares=True):
                def chunk(i, j):
                    m = 2 * i + j
                    if ready:
                        ready(i, j)
                    if squares:
                        await_at_least(act, s_l, m + (8 * q - 1))
                        last = nc.scalar.activation(sq[:, j], chunk_of(x, m), ACT.Square)
                    if H is not None:
                        last = nc.scalar.activation(chunk_of(H, m), chunk_of(x, m), ACT.Copy, scale=vec[:, bass.ds(m + gain, 1)])
                    last.then_inc(s_h, 1)
                items_of(act, DC, chunk)

            logarithms = [0]

            def inverse_root(items):
                for out, sums, scale, _ in items:
                    nc.scalar.activation(out, sums, ACT.Ln, bias=eps, scale=scale).then_inc(s_ln, 1)
                for k, (out, _, _, done) in enumerate(items):
                    act.wait_ge(s_ln, logarithms[0] + k + 1)
                    nc.scalar.activation(out, out, ACT.Exp, scale=-0.5).then_inc(done, 1)
                logarithms[0] += len(items)

            def norm_rstd(n):
                act.wait_ge(s_nsum, 2 * n + 2)
                inverse_root([(rstd[:, half_of(h)], ps[:, 4 + h], 1.0 / D, s_rstd) for h in range(2)])

            def updated(stage):
                return lambda i, j: act.wait_ge(s_free[bank_of(stage, j, 1)], use_of(stage, i, j) + 1)

            act.dma_start(vec[:], a["vectors"]).then_inc(s_const, 16)
            act.dma_start(ident[:], a["identity"]).then_inc(s_const, 16)
            act.dma_start(ones[:], a["ones"]).then_inc(s_const, 16)
            act.dma_start(head_ones[:], a["head_ones"]).then_inc(s_bconst, 16)
            act.dma_start(far_mask[:], a["far_mask"]).then_inc(s_bconst, 16)
            act.wait_ge(s_const, 48)
            nc.scalar.activation(derived[:, 21:31], V(V_LAM, RB), ACT.Abs).then_inc(s_ldone, 1)
            act.wait_ge(s_ldone, 1)
            nc.scalar.activation(derived[:, 31:41], derived[:, 21:31], ACT.Exp, scale=-1.0).then_inc(s_ldone, 1)

            def x_in(i, j):
                if j == 0:
                    act.wait_ge(s_x[i], 16)

            for i in range(4):
                for j in range(2):
                    m = 2 * i + j
                    x_in(i, j)
                    await_at_least(act, s_l, m - 1)
                    nc.scalar.activation(sq[:, j], x1[:, m], ACT.Square)
                    nc.scalar.activation(h1H[:, m], x1[:, m], ACT.Copy, scale=V(G_MIX + m)).then_inc(s_h, 1)
            norm_rstd(0)

            def gate(i, j):
                act.wait_ge(s_gz, 2 * i + j + 1)
                nc.scalar.activation(sq[:, j], sq[:, j], ACT.Sigmoid).then_inc(s_gs, 1)
                act.wait_ge(s_gs, 2 * i + j + 1)
                act.dma_start(a["gates"][bass.ds(2 * i + j, 1)].rearrange("u p n -> p (u n)"), sq[:, j]).then_inc(s_gst[j], 16)

            items_of(act, 16, gate)

            act.wait_ge(s_free[3], use_of("zb", 5, 1) + 1)
            for n in range(18):
                if n < 16:
                    c, h = n // 2, n % 2
                    await_at_least(act, s_bsum, n - 1)
                    nc.scalar.activation(tmp[:, half_of(h)], qk_b[:, c, half_of(h)], ACT.Square).then_inc(s_bsq, 1)
                if 1 <= n <= 16:
                    m = n - 1
                    act.wait_ge(s_bsum, m + 1)
                    await_at_least(act, s_bn, m - 1)
                    inverse_root([(acc[:, half_of(m % 2)], ps[:, 4 + m % 2], 1.0 / HD_B, s_brstd)])
            for t in range(NT):
                act.wait_ge(s_vT, t + 1)
                nc.scalar.activation(v_tok[:, t], ps[:, 6 + t % 2], ACT.Copy).then_inc(s_vt, 1)
            act.wait_ge(s_vT, NT)
            act.dma_start(bias[:], a["bias"]).then_inc(s_bconst, 16)

            def band_high(m):
                h, j, _ = band.items[m]
                if h == HEADS_B - 1:
                    act.wait_ge(band.outT, j + 1)
                    nc.scalar.activation(obH[:, :, j * P:(j + 1) * P], ps[:, 6 + m % 2].rearrange("p (c t) -> p c t", c=4), ACT.Copy).then_inc(band.outH, 1)

            attention_scalar(act, band, band_high)

            act.wait_ge(s_free[3], use_of("za", 7, 1) + 1)
            act.dma_start(masks[:], a["masks"]).then_inc(s_hm, 16)
            nchain = 0
            for k in range(4):
                part = slice(k * S, (k + 1) * S)
                for f, src, scale, bias_ in ((ACT.Abs, zf, 1.0, 0.0), (ACT.Exp, hd, -1.0, 0.0), (ACT.Ln, hd, 1.0, 1.0)):
                    nc.scalar.activation(hd[:, part], src[:, part], f, scale=scale, bias=bias_).then_inc(s_ha, 1)
                    nchain += 1
                    act.wait_ge(s_ha, nchain)
            for k in range(4):
                part = slice(k * S, (k + 1) * S)
                act.wait_ge(s_hp, 2 * k + 2)
                nc.scalar.activation(zf[:, part], hd[:, part], ACT.Exp).then_inc(s_hk, 1)
            for n in range(14):
                size = LEVELS[n // 2]
                d = hd[:, (n % 2) * 4 * CH:(n % 2 + 1) * 4 * CH].rearrange("p (n two s) -> p n two s", two=2, s=size)
                act.wait_ge(s_lD, n + 1)
                nc.scalar.activation(d[:, :, 1], d[:, :, 1], ACT.Exp)
                nc.scalar.activation(d[:, :, 0], d[:, :, 0], ACT.Exp, scale=-1.0).then_inc(s_lE, 1)
            act.wait_ge(s_lQ, 14)
            for k in range(2):
                part = slice(k * 4 * CH, (k + 1) * 4 * CH)
                nc.scalar.activation(hd[:, part], hb[:, part], ACT.Exp).then_inc(s_eb, 1)
            nc.scalar.activation(chunk_decay[:], hb[:].rearrange("p (n t) -> p n t", t=P)[:, :, P - 1], ACT.Exp).then_inc(s_eb, 1)
            for k in range(2):
                part = slice(k * 4 * CH, (k + 1) * 4 * CH)
                act.wait_ge(s_kb, k + 1)
                nc.scalar.activation(hqk[:, part], hqk[:, part], ACT.Exp, scale=-1.0).then_inc(s_ke, 1)
            act.wait_ge(s_kd, 2)
            for n in range(16):
                c = n // 2
                act.wait_ge(s_hT, n + 1)
                dst = hb if n % 2 == 0 else zf
                nc.scalar.activation(dst[:, c * CH:(c + 1) * CH], ps[:, n % 4], ACT.Copy).then_inc(s_hTe, 1)
            for k in range(2):
                nc.scalar.activation(zg[:, k * 4 * CH:(k + 1) * 4 * CH], zg[:, k * 4 * CH:(k + 1) * 4 * CH], ACT.Silu)
            for c in range(NT):
                part = slice(c * CH, (c + 1) * CH)
                act.wait_ge(s_hO, c + 1)
                nc.scalar.activation(zi[:, part], ps[:, 4 + c % 2], ACT.Copy, scale=float(P ** -0.5)).then_inc(s_hOe, 1)
                act.wait_ge(s_hOe, c + 1)
                nc.scalar.activation(hqk[:, part], zi[:, part], ACT.Square).then_inc(s_h2, 1)
            for c in range(NT):
                part = slice(c * CH, (c + 1) * CH)
                act.wait_ge(s_hn, c + 1)
                inverse_root([(hd[:, part], ps[:, c % 2], 1.0 / P, s_hrstd)])
            act.wait_ge(s_hO, NT)
            for c in range(NT):
                act.wait_ge(s_hout, c + 1)
                nc.scalar.activation(oaH[:, :, c * P:(c + 1) * P], zi[:, c * CH:(c + 1) * CH].rearrange("p (h t) -> p h t", h=4), ACT.Copy).then_inc(s_hoh, 1)
            act.dma_start(x2[:], a["xT"]).then_inc(s_x2, 16)

            def gates_in(m, j):
                act.dma_start(gate_in[:, j], a["gates"].rearrange("(g m) p n -> m p g n", g=2)[bass.ds(m, 1)].rearrange("m p g n -> p (m g) n")).then_inc(s_gin[j], 16)

            for j in range(2):
                act.wait_ge(s_gst[j], 8 * 16)
            for j in range(2):
                gates_in(j, j)

            def merged_high(i, j):
                m = 2 * i + j
                act.wait_ge(s_mg, m + 1)
                nc.scalar.activation(chunk_of(mgH, m), gate_in[:, j, 0], ACT.Copy).then_inc(s_mgh, 1)
                act.wait_ge(s_mgl, m + 1)

            for i in range(4):
                for j in range(2):
                    merged_high(i, j)
                    if i < 3:
                        gates_in(2 * i + j + 2, j)
            split_x(1, x2, h2H, G_FFN, updated("wout"))
            norm_rstd(1)
            for g, n in enumerate(FF_GROUPS):
                p0 = sum(FF_GROUPS[:g])
                u0 = f"gu{g}"

                def pair(i, j, p0=p0, u0=u0):
                    m = 2 * i + j
                    act.wait_ge(s_free[bank_of(u0, 0, 1)], m + (STAGE[u0][1] // 2 + 1))
                    nc.scalar.activation(sq[:, 0], sq[:, 0], ACT.Silu).then_inc(s_silu, 1)
                    act.wait_ge(s_act, m + (p0 + 1))
                    nc.scalar.activation(chunk_of(actH, m), tmp[:], ACT.Copy).then_inc(s_acth, 1)

                items_of(act, n, pair)
            split_x(2, x2, h2H, G_PLE, updated("dn2"))
            act.wait_ge(s_mm, mm_count("dn2", 7, 1))
            act.dma_start(p_in[:], a["pT"]).then_inc(s_p, 16)
            act.wait_ge(s_p, 16)
            for c in range(2):
                nc.scalar.activation(pH[:, c], p_in[:, c], ACT.Copy).then_inc(s_ph, 1)
            norm_rstd(2)

            def ple(i, j):
                m = 2 * i + j
                act.wait_ge(s_free[bank_of("pleg", j, 1)], use_of("pleg", i, j) + 1)
                nc.scalar.activation(tmp[:], tmp[:], ACT.Sigmoid).then_inc(s_sig, 1)
                act.wait_ge(s_pz, m + 1)
                await_at_least(act, s_l, m + (8 * 3 - 1))
                nc.scalar.activation(sq[:, j], chunk_of(x2, m), ACT.Square)
                nc.scalar.activation(chunk_of(h4H, m), chunk_of(x2, m), ACT.Copy, scale=vec[:, bass.ds(m + G_A, 1)]).then_inc(s_h, 1)

            items_of(act, DC, ple)
            act.wait_ge(s_l, 8 * 4)
            act.dma_start(a["x_spill_rnn"], x2[:]).then_inc(s_xs3, 16)
            norm_rstd(3)

            act.wait_ge(s_xs3, 16)
            act.dma_start(w_ri[:], a["rnn_gate_weights"]).then_inc(s_wri, 16)
            act.wait_ge(s_wri, 16)

            def y_high(n):
                act.wait_ge(s_yg, n + 1)
                nc.scalar.activation(chunk_of(yH, n), chunk_of(rgate, n), ACT.Copy).then_inc(s_yh, 1)

            def rnn_block(n):
                first = isinstance(n, int)
                of = lambda column: vec[:, bass.ds(n + column, 1)]
                derived_of = lambda column: derived[:, bass.ds(n + column, 1)]
                await_at_least(act, s_ri, 4 * n)
                nc.scalar.activation(w_riH[:], w_ri[:, n] if first else w_ri[:, bass.ds(n, 1)], ACT.Copy).then_inc(s_wrh, 1)
                act.wait_ge(s_cv, 4 * n + 4)
                nc.scalar.activation(convH[:], conv[:], ACT.Copy).then_inc(s_ch, 1)
                if not first:
                    y_high(n - 1)
                act.wait_ge(s_free[bank_of("xg", 1, 1)], use_of("xg", n, 1) + 1)
                nc.scalar.activation(chunk_of(rgate, n), chunk_of(rgate, n), ACT.Silu).then_inc(s_rg, 1)
                for g, (buf, b) in enumerate(((r_buf, V_BR), (i_buf, V_BI))):
                    act.wait_ge(s_ri, 4 * n + (2 * g + 2))
                    nc.scalar.activation(buf[:], ps[:, 4 + 2 * g:6 + 2 * g].rearrange("p b n -> p (b n)"), ACT.Sigmoid, bias=of(b)).then_inc(s_sg, 1)
                act.wait_ge(s_sg, 2 * n + 2)
                nc.scalar.activation(chunk_of(xb, n), r_buf[:], ACT.Exp, scale=derived_of(1)).then_inc(s_a, 1)
                act.wait_ge(s_a, n + 1)
                nc.scalar.activation(r_buf[:], r_buf[:], ACT.Tanh, scale=derived_of(11)).then_inc(s_T, 1)
                act.wait_ge(s_T, n + 1)
                nc.scalar.activation(r_buf[:], r_buf[:], ACT.Sqrt).then_inc(s_rs, 1)

            rnn_block(0)
            with act.Fori(1, RB) as n:
                rnn_block(n)
            act.wait_ge(s_mm, mm_count("xg", 2 * RB - 1, 1))
            act.dma_start(x4[:], a["x_spill_rnn"]).then_inc(s_xld4, 16)
            y_high(RB - 1)
            split_x(4, x4, None, 0, updated("wo2"))
            split_x(5, x4, h5H, G_KV, None, False)
            norm_rstd(4)
            split_x(6, x4, h6H, G_B, None, False)
            act.dma_start(a["x_spill_mla"], x4[:]).then_inc(s_xs5, 16)
            n = 0
            for k, (stage, chunks, width, src, H) in enumerate((("dkv", 2, 256, ckv, ckvH), ("cq", 3, 384, cq, cqH))):
                act.wait_ge(s_free[bank_of(stage, 2, 1)], use_of(stage, 0, 2) + 1)
                if k == 0:
                    act.dma_start(rotate[:], a["rotate"]).then_inc(s_cconst, 16)
                    act.dma_start(causal[:], a["causal"]).then_inc(s_cconst, 16)
                else:
                    act.wait_ge(s_cwl, 2)
                for c in range(chunks):
                    await_at_least(act, s_cs, 2 * n)
                    nc.scalar.activation(acc[:], src[:, c], ACT.Square).then_inc(s_c2, 1)
                    n += 1
                act.wait_ge(s_cs, 2 * n)
                inverse_root([(acc[:, half_of(h)], ps[:, 4 + h], 1.0 / width, s_crstd) for h in range(2)])
                for c in range(chunks):
                    act.wait_ge(s_cw, 2 * k + c + 1)
                    nc.scalar.activation(H[:, c], src[:, c], ACT.Copy).then_inc(s_cwh, 1)
            act.wait_ge(s_cwl, 5)
            act.dma_start(cos_sin[:], a["cos_sin"]).then_inc(s_cconst, 16)

            def mla_gate(i, j):
                act.wait_ge(s_free[bank_of("cgate", j, 1)], use_of("cgate", i, j) + 1)
                nc.scalar.activation(chunk_of(cgate, 2 * i + j), chunk_of(cgate, 2 * i + j), ACT.Silu).then_inc(s_cg, 1)

            items_of(act, DC, mla_gate)
            for g in range(2):
                attention_scalar(act, mla[g], lambda m: None)
            act.wait_ge(mla[1].outL, len(mla[1].items))
            act.dma_start(x5[:], a["x_spill_mla"]).then_inc(s_xld5, 16)
            for m in range(DC):
                nc.scalar.activation(y7H[:, m], cgate[:, m], ACT.Copy).then_inc(s_y7h, 1)
            split_x(7, x5, None, 0, updated("wob"))
            norm_rstd(5)

        @block.vector
        def _(dve):
            def low_of(L, source, H):
                return nc.vector.tensor_tensor(L, source, f32(H), ALU.subtract)

            def split_x(q, x, H, L, gain, before=None, after_h=True, squares=True):
                def chunk(i, j):
                    m = 2 * i + j
                    if before:
                        before(i, j)
                    dve.wait_ge(s_h, m + (8 * q + 1))
                    if squares:
                        if isinstance(i, int) and m == 0:
                            last = nc.vector.tensor_copy(acc[:], sq[:, j])
                        else:
                            dve.wait_ge(s_l, m + 8 * q)
                            last = nc.vector.tensor_tensor(acc[:], acc[:], sq[:, j], ALU.add)
                    if H is not None:
                        last = nc.vector.scalar_tensor_tensor(out=chunk_of(L, m), in0=chunk_of(x, m), scalar=vec[:, bass.ds(m + gain, 1)],
                                                              in1=f32(chunk_of(H, m)), op0=ALU.mult, op1=ALU.subtract)
                    last.then_inc(s_l, 1)
                items_of(dve, DC, chunk)

            def norm_rstd(n):
                dve.wait_ge(s_rstd, 2 * n + 2)

            def read(stage, i, j, h, operation):
                dve.wait_ge(s_mm, mm_count(stage, 2 * i + j, h))
                bank = bank_of(stage, j, h)
                operation(ps[:, bank]).then_inc(s_free[bank], 1)

            def scaled(stage, destination, start=0, signal=None):
                def one(i, j):
                    for h in range(2):
                        read(stage, i, j, h, lambda p: nc.vector.tensor_tensor(
                            chunk_of(destination, 2 * i + j)[..., half_of(h)], p, rstd[:, half_of(h)], ALU.mult))
                items_of(dve, STAGE[stage][2], one)

            def add_to(stage, x):
                def one(i, j):
                    for h in range(2):
                        xm = chunk_of(x, 2 * i + j)[..., half_of(h)]
                        read(stage, i, j, h, lambda p: nc.vector.tensor_tensor(xm, p, xm, ALU.add))
                return one

            chain = [0]

            def link(instruction):
                chain[0] += 1
                instruction.then_inc(s_vchain, 1)
                dve.wait_ge(s_vchain, chain[0])

            dve.wait_ge(s_const, 48)
            link(nc.vector.tensor_scalar(q_gain_scaled, V(V_QN), float(HD_B ** -0.5), None, ALU.mult))
            dve.wait_ge(s_ldone, 2)
            e, s_, s2, poly = derived[:, 31:41], derived[:, 41:51], derived[:, 51:61], derived[:, 61:71]
            link(nc.vector.tensor_scalar(s2, e, 2.0, None, ALU.add))
            link(nc.vector.reciprocal(s_, s2))
            link(nc.vector.tensor_tensor(s_, e, s_, ALU.mult))
            link(nc.vector.tensor_tensor(s2, s_, s_, ALU.mult))
            link(nc.vector.tensor_scalar(poly, s2, 1.0 / 15, 1.0 / 13, ALU.mult, ALU.add))
            for k in (11, 9, 7, 5, 3, 1):
                link(nc.vector.tensor_tensor(poly, poly, s2, ALU.mult))
                link(nc.vector.tensor_scalar(poly, poly, 1.0 / k, None, ALU.add))
            link(nc.vector.tensor_tensor(poly, poly, s_, ALU.mult))
            link(nc.vector.tensor_scalar(s2, V(V_LAM, RB), -1.0, 0.0, ALU.mult, ALU.max))
            link(nc.vector.scalar_tensor_tensor(out=s2, in0=poly, scalar=2.0, in1=s2, op0=ALU.mult, op1=ALU.add))
            link(nc.vector.tensor_scalar(derived[:, 1:11], s2, -8.0, None, ALU.mult))
            link(nc.vector.tensor_scalar(derived[:, 11:21], s2, 4.0, None, ALU.mult))

            split_x(0, x1, h1H, h1L, G_MIX)
            norm_rstd(0)

            def gate(i, j):
                if not (isinstance(i, int) and i == 0):
                    dve.wait_ge(s_gst[j], i * 16)
                for h in range(2):
                    dve.wait_ge(s_mm, mm_count("gates", 2 * i + j, h))
                    nc.vector.tensor_tensor(sq[:, j, half_of(h)], ps[:, 2 * j + h], rstd[:, half_of(h)], ALU.mult).then_inc(s_free[2 * j + h], 1)
                dve.wait_ge(s_free[2 * j + 1], i + 1)
                dve.nop().then_inc(s_gz, 1)

            items_of(dve, 16, gate)
            scaled("zb", zb)

            for n in range(16):
                c, h = n // 2, n % 2
                dve.wait_ge(s_brstd, n + 1)
                x = qk_b[:, c, half_of(h)]
                nc.vector.scalar_tensor_tensor(out=x, in0=x, scalar=q_gain_scaled if c < 4 else V(V_KN), in1=acc[:, half_of(h)],
                                               op0=ALU.mult, op1=ALU.mult).then_inc(s_bn, 1)
            dve.wait_ge(s_bconst, 48)
            for h in range(HEADS_B):
                nc.vector.tensor_scalar(bias[:, h], bias[:, h], V(V_CFAR + h), None, ALU.subtract).then_inc(s_bias, 1)
            dve.wait_ge(s_bias, HEADS_B)
            for h in range(HEADS_B):
                nc.vector.memset(bias[0:64, h, 192:256], NEG).then_inc(s_bias, 1)

            def band_destination(m, o, inverse):
                h, j, _ = band.items[m]
                if h == 0:
                    await_at_least(dve, band.outT, j - 1)
                return nc.vector.tensor_scalar(o_tok[:, j % 2, h * HD_B:(h + 1) * HD_B], o, inverse, None, ALU.mult)

            def band_low(m):
                h, j, _ = band.items[m]
                if h == HEADS_B - 1:
                    dve.wait_ge(band.outH, j + 1)
                    low_of(obL[:, :, j * P:(j + 1) * P], ps[:, 6 + m % 2].rearrange("p (c t) -> p c t", c=4),
                           obH[:, :, j * P:(j + 1) * P]).then_inc(band.outL, 1)

            attention_vector(dve, band, band_destination, band_low)

            for t in range(16):
                w, head = t // 4, t % 4
                for h in range(2):
                    read("za", t // 2, t % 2, h, lambda p: nc.vector.tensor_tensor(
                        za[:, w, 4 * h:4 * h + 4, head], p.rearrange("p (c t) -> p c t", c=4),
                        rstd[:, half_of(h)].rearrange("p (c t) -> p c t", c=4), ALU.mult))
            for k in range(4):
                part = slice(k * S, (k + 1) * S)
                dve.wait_ge(s_ha, 3 * k + 3)
                nc.vector.scalar_tensor_tensor(out=hqk[:, part], in0=zf[:, part], scalar=0.0, in1=hd[:, part],
                                               op0=ALU.min, op1=ALU.subtract).then_inc(s_hp, 1)
                dve.wait_ge(s_hp, 2 * k + 1)
                nc.vector.tensor_tensor(hd[:, part], hqk[:, part], zf[:, part], ALU.subtract).then_inc(s_hp, 1)
            for n in range(NT * A_HEADS):
                last = nc.vector.tensor_tensor_scan(out=hb[:, n * P:(n + 1) * P], data0=ones[:], data1=hqk[:, n * P:(n + 1) * P],
                                                    initial=0.0, op0=ALU.mult, op1=ALU.add)
            last.then_inc(s_hscan, 1)
            nc.vector.memset(attn[:], 0.0).then_inc(s_hscan, 1)
            dve.wait_ge(s_hscan, 2)
            dve.wait_ge(s_hk, 4)
            dve.wait_ge(s_hm, 16)
            for n in range(18):
                if n < 14:
                    await_at_least(dve, s_lQ, n - 1)
                    size = LEVELS[n // 2]
                    part = slice((n % 2) * 4 * CH, (n % 2 + 1) * 4 * CH)
                    b_ = hb[:, part].rearrange("p (n w) -> p n w", w=2 * size)
                    nc.vector.tensor_tensor(hd[:, part].rearrange("p (n w) -> p n w", w=2 * size), b_,
                                            b_[:, :, size - 1:size].broadcast_to([P, 4 * CH // (2 * size), 2 * size]),
                                            ALU.subtract).then_inc(s_lD, 1)
                if 1 <= n <= 14:
                    m = n - 1
                    size = LEVELS[m // 2]
                    part = slice((m % 2) * 4 * CH, (m % 2 + 1) * 4 * CH)
                    two = lambda t: t[:, part].rearrange("p (n two s) -> p n two s", two=2, s=size)
                    dve.wait_ge(s_lE, m + 1)
                    await_at_least(dve, s_lS, 4 * (m - 1))
                    nc.vector.tensor_tensor(two(hqk)[:, :, 1], two(hd)[:, :, 1], two(zq)[:, :, 1], ALU.mult)
                    nc.vector.tensor_tensor(two(hqk)[:, :, 0], two(hd)[:, :, 0], two(zf)[:, :, 0], ALU.mult).then_inc(s_lQ, 1)
                if n >= 2:
                    m = n - 2
                    for k in range(4):
                        c = 4 * (m % 2) + k
                        dve.wait_ge(s_lS, 4 * m + k + 1)
                        nc.vector.copy_predicated(attn[:, c * CH:(c + 1) * CH].rearrange("p (h t) -> p h t", h=A_HEADS),
                                                  masks[:, m // 2:m // 2 + 1, :].bitcast(mybir.dt.int32).broadcast_to([P, A_HEADS, P]),
                                                  ps[:, c].rearrange("p (h t) -> p h t", h=A_HEADS)).then_inc(s_lP, 1)
            b_ = hb[:].rearrange("p (n t) -> p n t", t=P)
            for k in range(2):
                part = slice(k * 4 * CH, (k + 1) * 4 * CH)
                bk = hb[:, part].rearrange("p (n t) -> p n t", t=P)
                nc.vector.tensor_tensor(hqk[:, part].rearrange("p (n t) -> p n t", t=P), bk,
                                        bk[:, :, P - 1:P].broadcast_to([P, 4 * A_HEADS, P]), ALU.subtract).then_inc(s_kb, 1)
            for k in range(2):
                part = slice(k * 4 * CH, (k + 1) * 4 * CH)
                dve.wait_ge(s_ke, k + 1)
                nc.vector.tensor_tensor(hqk[:, part], hqk[:, part], zf[:, part], ALU.mult).then_inc(s_kd, 1)
            for k in range(2):
                part = slice(k * 4 * CH, (k + 1) * 4 * CH)
                dve.wait_ge(s_eb, k + 1)
                nc.vector.tensor_tensor(hd[:, part], hd[:, part], zq[:, part], ALU.mult).then_inc(s_qe, 1)
            dve.wait_ge(s_eb, 3)
            for c in range(NT - 1):
                dve.wait_ge(s_hU, c + 1)
                if c == 0:
                    nc.vector.tensor_copy(states[:, 0], ps[:, 6]).then_inc(s_hst, 1)
                else:
                    dve.wait_ge(s_hst, c)
                    dve.wait_ge(s_hO, c)
                    for h in range(A_HEADS):
                        hs = slice(h * P, (h + 1) * P)
                        last = nc.vector.scalar_tensor_tensor(out=states[:, c % 2, hs], in0=states[:, (c - 1) % 2, hs],
                                                              scalar=chunk_decay[:, c * A_HEADS + h:c * A_HEADS + h + 1],
                                                              in1=ps[:, 6 + c % 2, hs], op0=ALU.mult, op1=ALU.add)
                    last.then_inc(s_hst, 1)
            for c in range(NT + 1):
                if c < NT:
                    part = slice(c * CH, (c + 1) * CH)
                    dve.wait_ge(s_hrstd, c + 1)
                    nc.vector.scalar_tensor_tensor(out=zi[:, part], in0=zi[:, part], scalar=V(V_ONORM), in1=hd[:, part],
                                                   op0=ALU.mult, op1=ALU.mult).then_inc(s_hw, 1)
                    dve.wait_ge(s_hw, c + 1)
                    nc.vector.tensor_tensor(zi[:, part], zi[:, part], zg[:, part], ALU.mult).then_inc(s_hout, 1)
                if c >= 1:
                    m = c - 1
                    dve.wait_ge(s_hoh, m + 1)
                    low_of(oaL[:, :, m * P:(m + 1) * P], zi[:, m * CH:(m + 1) * CH].rearrange("p (h t) -> p h t", h=A_HEADS),
                           oaH[:, :, m * P:(m + 1) * P]).then_inc(s_hol, 1)

            def merge(i, j):
                m = 2 * i + j
                dve.wait_ge(s_gin[j], i * 16 + 16)
                for part in range(2):
                    for h in range(2):
                        dve.wait_ge(s_mm, mm_count("merge", m * 2 + part, h))
                        g = gate_in[:, j, part, half_of(h)]
                        nc.vector.tensor_tensor(g, ps[:, 2 * part + h], g, ALU.mult).then_inc(s_free[2 * part + h], 1)
                dve.wait_ge(s_free[3], m + (STAGE["merge"][1] // 2 + 1))
                nc.vector.tensor_tensor(gate_in[:, j, 0], gate_in[:, j, 0], gate_in[:, j, 1], ALU.add).then_inc(s_mg, 1)
                dve.wait_ge(s_mgh, m + 1)
                low_of(chunk_of(mgL, m), gate_in[:, j, 0], chunk_of(mgH, m)).then_inc(s_mgl, 1)

            items_of(dve, DC, merge)
            dve.wait_ge(s_x2, 16)
            split_x(1, x2, h2H, h2L, G_FFN, add_to("wout", x2))
            norm_rstd(1)
            for g, n in enumerate(FF_GROUPS):
                p0 = sum(FF_GROUPS[:g])
                stage = f"gu{g}"

                def pair(i, j, p0=p0, stage=stage):
                    m = 2 * i + j
                    for part in range(2):
                        for h in range(2):
                            read(stage, m, part, h, lambda p: nc.vector.tensor_tensor(sq[:, part, half_of(h)], p, rstd[:, half_of(h)], ALU.mult))
                    dve.wait_ge(s_silu, m + (p0 + 1))
                    dve.wait_ge(s_free[bank_of(stage, 1, 1)], m + (STAGE[stage][1] // 2 + 1))
                    nc.vector.tensor_tensor(tmp[:], sq[:, 0], sq[:, 1], ALU.mult).then_inc(s_act, 1)
                    dve.wait_ge(s_acth, m + (p0 + 1))
                    low_of(chunk_of(actL, m), tmp[:], chunk_of(actH, m)).then_inc(s_actl, 1)

                items_of(dve, n, pair)
                if g < 2:
                    items_of(dve, DC, add_to(f"dn{g}", x2))
            split_x(2, x2, h2H, h2L, G_PLE, add_to("dn2", x2))
            for c in range(2):
                dve.wait_ge(s_ph, c + 1)
                low_of(pL[:, c], p_in[:, c], pH[:, c]).then_inc(s_pl, 1)
            for t in range(DC):
                for h in range(2):
                    read("proj", t // 2, t % 2, h, lambda p: nc.vector.tensor_copy(proj[:, t, half_of(h)], p))
            norm_rstd(2)

            def ple_add(i, j):
                m = 2 * i + j
                for h in range(2):
                    read("pleg", i, j, h, lambda p: nc.vector.tensor_tensor(tmp[:, half_of(h)], p, rstd[:, half_of(h)], ALU.mult))
                dve.wait_ge(s_sig, m + 1)
                nc.vector.tensor_tensor(tmp[:], tmp[:], chunk_of(proj, m), ALU.mult).then_inc(s_pc, 1)
                dve.wait_ge(s_pc, m + 1)
                nc.vector.tensor_tensor(chunk_of(x2, m), chunk_of(x2, m), tmp[:], ALU.add).then_inc(s_pz, 1)

            split_x(3, x2, h4H, h4L, G_A, ple_add)
            norm_rstd(3)
            dve.wait_ge(s_xs3, 16)

            def project(n, j, destination):
                for h in range(2):
                    read("xg", n, j, h, lambda p: nc.vector.tensor_tensor(
                        chunk_of(destination, n)[..., half_of(h)], p, rstd[:, half_of(h)], ALU.mult))

            def recurrence(n):
                dve.wait_ge(s_rs, n + 1)
                nc.vector.scalar_tensor_tensor(out=r_buf[:], in0=chunk_of(xb, n), scalar=1.0, in1=r_buf[:],
                                               op0=ALU.add, op1=ALU.mult).then_inc(s_rw, 1)
                dve.wait_ge(s_rw, 3 * n + 1)
                nc.vector.tensor_tensor(i_buf[:], i_buf[:], r_buf[:], ALU.mult).then_inc(s_rw, 1)
                dve.wait_ge(s_rw, 3 * n + 2)
                nc.vector.tensor_tensor_scan(out=r_buf[:], data0=xb[:].rearrange("p c t -> p (c t)")[:, bass.ds(n * S, S)], data1=i_buf[:], initial=0.0,
                                             op0=ALU.mult, op1=ALU.add).then_inc(s_rw, 1)
                dve.wait_ge(s_rw, 3 * n + 3)
                dve.wait_ge(s_rg, n + 1)
                nc.vector.tensor_tensor(chunk_of(rgate, n), r_buf[:], chunk_of(rgate, n), ALU.mult).then_inc(s_yg, 1)

            def y_low(n):
                dve.wait_ge(s_yh, n + 1)
                low_of(chunk_of(yL, n), chunk_of(rgate, n), chunk_of(yH, n)).then_inc(s_yl, 1)

            def rnn_block(n):
                first = isinstance(n, int)
                w = lambda k: vec[:, bass.ds(4 * n + (V_CW + k), 1)]
                project(n, 0, xb)
                dve.wait_ge(s_free[bank_of("xg", 0, 1)], use_of("xg", n, 0) + 1)
                await_at_least(dve, s_ix, n)
                x = chunk_of(xb, n)
                nc.vector.tensor_scalar(conv[:], x, w(3), vec[:, bass.ds(n + V_CB, 1)], ALU.mult, ALU.add).then_inc(s_cv, 1)
                for k in (1, 2, 3):
                    dve.wait_ge(s_cv, 4 * n + k)
                    nc.vector.scalar_tensor_tensor(out=conv[:, k:], in0=x[..., 0:S - k], scalar=w(3 - k), in1=conv[:, k:],
                                                   op0=ALU.mult, op1=ALU.add).then_inc(s_cv, 1)
                dve.wait_ge(s_wrh, n + 1)
                low_of(w_riL[:], w_ri[:, n] if first else w_ri[:, bass.ds(n, 1)], w_riH[:]).then_inc(s_wrl, 1)
                dve.wait_ge(s_ch, n + 1)
                low_of(convL[:], conv[:], convH[:]).then_inc(s_cl, 1)
                if not first:
                    recurrence(n - 1)
                project(n, 1, rgate)
                if not first:
                    y_low(n - 1)
                dve.wait_ge(s_sg, 2 * n + 2)
                nc.vector.tensor_tensor(i_buf[:], i_buf[:], conv[:], ALU.mult).then_inc(s_ix, 1)

            rnn_block(0)
            with dve.Fori(1, RB) as n:
                rnn_block(n)
            dve.wait_ge(s_ix, RB)
            recurrence(RB - 1)
            y_low(RB - 1)
            dve.wait_ge(s_xld4, 16)
            items_of(dve, DC, add_to("wo1", x4))
            split_x(4, x4, None, None, 0, add_to("wo2", x4))
            split_x(5, x4, h5H, h5L, G_KV, squares=False)
            norm_rstd(4)
            split_x(6, x4, h6H, h6L, G_B, squares=False)
            for t in range(3):
                for h in range(2):
                    dst = ckv[:, t, half_of(h)] if t < 2 else tmp[:, half_of(h)]
                    read("dkv", t // 2, t % 2, h, lambda p: nc.vector.tensor_tensor(dst, p, rstd[:, half_of(h)], ALU.mult))
            for t in range(3):
                for h in range(2):
                    dst = cq[:, t, half_of(h)]
                    dve.wait_ge(s_mm, mm_count("cq", t, h))
                    bank = bank_of("cq", t, h)
                    nc.vector.tensor_tensor(dst, ps[:, bank], rstd[:, half_of(h)], ALU.mult).then_inc(s_free[bank], 1)
            for k, (chunks, src, H, L, gain) in enumerate(((2, ckv, ckvH, ckvL, V_KVN), (3, cq, cqH, cqL, V_CQN))):
                dve.wait_ge(s_crstd, 2 * k + 2)
                for c in range(chunks):
                    nc.vector.scalar_tensor_tensor(out=src[:, c], in0=src[:, c], scalar=V(gain + c), in1=acc[:],
                                                   op0=ALU.mult, op1=ALU.mult).then_inc(s_cw, 1)
                for c in range(chunks):
                    dve.wait_ge(s_cwh, 2 * k + c + 1)
                    low_of(L[:, c], src[:, c], H[:, c]).then_inc(s_cwl, 1)
            dve.wait_ge(s_xs5, 16)
            scaled("cgate", cgate)
            for h in range(2):
                dve.wait_ge(s_rot, h + 1)
                nc.vector.tensor_tensor(sq[:, 0, half_of(h)], ps[:, 6 + h], cos_sin[:, 1, half_of(h)], ALU.mult).then_inc(s_kr, 1)
            nc.vector.tensor_tensor(k_rope[:], tmp[:], cos_sin[:, 0], ALU.mult).then_inc(s_kr, 1)
            dve.wait_ge(s_kr, 3)
            nc.vector.tensor_tensor(k_rope[:], k_rope[:], sq[:, 0], ALU.add).then_inc(s_kr, 1)
            for t in range(DC):
                for h in range(2):
                    read("uk", t // 2, t % 2, h, lambda p: nc.vector.tensor_copy(k_nope[:, t, half_of(h)], p))
            for t in range(DC):
                v, r = t // 4, t % 4
                for h in range(2):
                    read("uv", t // 2, t % 2, h, lambda p: nc.vector.tensor_copy(v_mla[:, 2 * r + h, v * HALF:(v + 1) * HALF], p))
            for g in range(2):
                at_ = mla[g]
                for t in range(6):
                    dst = q_nope[:, t] if t < 4 else q_rope[:, t - 4]
                    for h in range(2):
                        read(f"uq{g}", t // 2, t % 2, h, lambda p: nc.vector.tensor_copy(dst[:, half_of(h)], p))
                last_bank = bank_of(f"uq{g}", 1, 1)
                dve.wait_ge(s_free[last_bank], use_of(f"uq{g}", 2, 1) + 1)
                dve.nop().then_inc(s_rq, 1)
                for n in range(4):
                    t, h = n // 2, n % 2
                    x = q_rope[:, t, half_of(h)]
                    dve.wait_ge(s_rotq, 4 * g + n + 1)
                    nc.vector.tensor_tensor(sq[:, 0, half_of(h)], ps[:, 4 + n % 2], cos_sin[:, 1, half_of(h)], ALU.mult).then_inc(s_rqe, 1)
                    nc.vector.tensor_tensor(x, x, cos_sin[:, 0, half_of(h)], ALU.mult).then_inc(s_rqe, 1)
                    dve.wait_ge(s_rqe, 8 * g + 2 * n + 2)
                    nc.vector.tensor_tensor(x, x, sq[:, 0, half_of(h)], ALU.add).then_inc(s_qready, 1)
                if g == 0:
                    dve.wait_ge(s_cg, DC)

                def mla_destination(m, o, inverse):
                    await_at_least(dve, at_.outT, m - 1)
                    return nc.vector.tensor_scalar(o_mla[:, m % 2], o, inverse, None, ALU.mult)

                def mla_gated(m):
                    h, j, _ = at_.items[m]
                    dve.wait_ge(at_.outT, m + 1)
                    y = cgate[:, h, j * P:(j + 1) * P]
                    nc.vector.tensor_tensor(y, ps[:, 6 + m % 2, 0:P], y, ALU.mult).then_inc(at_.outL, 1)

                attention_vector(dve, at_, mla_destination, mla_gated)
            for m in range(DC):
                dve.wait_ge(s_y7h, m + 1)
                low_of(y7L[:, m], cgate[:, m], y7H[:, m]).then_inc(s_y7l, 1)
            dve.wait_ge(s_xld5, 16)
            split_x(7, x5, None, None, 0, add_to("wob", x5))
            norm_rstd(5)
            for m in range(DC):
                nc.vector.scalar_tensor_tensor(out=out_sb[:, m], in0=x5[:, m], scalar=V(G_FIN + m), in1=rstd[:],
                                               op0=ALU.mult, op1=ALU.mult).then_inc(s_fin, 1)


def _feature_major(x):
    return np.ascontiguousarray(x.T.reshape(-1, P, x.shape[0]).transpose(1, 0, 2))


def _unit(w):
    u = w.reshape(-1, P, w.shape[1]).transpose(1, 0, 2).reshape(P, -1)
    return np.concatenate([u, np.zeros((P, 1024 - u.shape[1]), np.float32)], axis=1)


def _stream(x):
    col = lambda w, t, n=P: w[:, t * n:(t + 1) * n]
    w_in, wa, wb = x["w_in"][0], x["w_branch_a"][0], x["w_branch_b"][0]
    units = [_unit(col(w_in, t)) for t in list(range(28, 44)) + list(range(16, 28)) + list(range(16))]
    units += [_unit(np.concatenate([col(wa, m), col(wb, m)])) for m in range(DC)]
    units += [_unit(col(x["w_out"][0], m)) for m in range(DC)]
    f0 = 0
    for n in FF_GROUPS:
        for f in range(f0, f0 + n):
            units += [_unit(col(x["w_ffn_gate"][0], f)), _unit(col(x["w_ffn_up"][0], f))]
        units += [_unit(col(x["w_ffn_down"][0], m)[f0 * P:(f0 + n) * P]) for m in range(DC)]
        f0 += n
    units += [_unit(col(x["w_ple_proj"][0], v, 512)) for v in range(2)]
    units += [_unit(col(x["w_ple_gate"][0], m)) for m in range(DC)]
    units += [_unit(col(x["w_in_a_2"][0], part * RB + n)) for n in range(RB) for part in range(2)]
    for k in range(2):
        units += [_unit(col(x["w_out_a_2"][0], m)[k * 640:(k + 1) * 640]) for m in range(DC)]
    dkv, wb_ = x["w_dkv_2"], x["w_in_b_2"][0]
    units += [_unit(dkv[:, 0:P]), _unit(dkv[:, P:2 * P]), _unit(np.concatenate([dkv[:, 256:320]] * 2, axis=1))]
    units += [_unit(col(wb_, m)) for m in range(11)]
    units += [_unit(col(x["w_uk_2"].reshape(256, 1024), v, 512)) for v in range(2)]
    units += [_unit(col(x["w_uv_2"].reshape(256, 1024), v, 512)) for v in range(2)]
    uq = x["w_uq_2"][0]
    for g in range(2):
        for h in (4 * g, 4 * g + 2):
            units.append(_unit(uq[:, h:h + 2, 0:P].reshape(384, 256)))
        units.append(_unit(uq[:, 4 * g:4 * g + 4, P:].reshape(384, 256)))
    units += [_unit(col(x["w_out_b_2"][0], m)) for m in range(DC)]
    assert len(units) == UNITS
    return np.stack(units)


def _vectors(x):
    cols = lambda v: v.reshape(-1, P).T
    twice = lambda v: np.concatenate([v, v])[:, None]
    parts = [cols(x[n].reshape(-1)) for n in ("norm_mix_g", "norm_ffn_g", "norm_ple_g", "norm_a_2", "norm_kv_2", "norm_b_2", "final_norm_2")]
    parts += [cols(x["hgrn_onorm_g"][0]), twice(x["attn_qnorm_g"][0]), twice(x["attn_knorm_g"][0])]
    parts += [cols(x[n][0]) for n in ("conv_b_2", "lru_lambda_2", "b_rg_2", "b_ig_2")]
    parts.append(x["conv_w_2"][0].reshape(4, RB, P).transpose(2, 1, 0).reshape(P, 4 * RB))
    parts += [cols(x["kv_norm_2"]), cols(x["q_norm_2"][0]), np.full((P, 1), EPS, np.float32)]
    parts.append(np.broadcast_to(x["attn_rel_bias"][0, :, 256], (P, HEADS_B)))
    parts.append(np.ones((P, 1), np.float32))
    return np.ascontiguousarray(np.concatenate(parts, axis=1))


def _constants():
    i = np.arange(P)
    s, t = i[:, None], i[None, :]
    levels = [(s // (2 * n) == t // (2 * n)) & (s % (2 * n) < n) & (t % (2 * n) >= n) for n in LEVELS] + [s == t]
    rotate = np.zeros((P, P), np.float32)
    for b in (0, 64):
        for k in range(32):
            rotate[b + 32 + k, b + k] = -1.0
            rotate[b + k, b + 32 + k] = 1.0
    inv = np.float32(10000.0) ** (-np.arange(0, 64, 2, dtype=np.float32) / np.float32(64))
    angle = np.arange(S, dtype=np.float32)[None, :] * inv[i % 32][:, None]
    return {
        "identity": np.eye(P, dtype=np.float32),
        "ones": np.ones((P, P), np.float32),
        "head_ones": (s // 64 == t // 64).astype(np.float32),
        "far_mask": np.ascontiguousarray(np.broadcast_to(np.where(s >= 64, np.float32(NEG), np.float32(0)), (P, 64))),
        "masks": np.ascontiguousarray(np.stack(levels, axis=1).astype(np.float32)),
        "rotate": rotate,
        "causal": np.where(t > s, np.float32(NEG), np.float32(0)),
        "cos_sin": np.ascontiguousarray(np.stack([np.cos(angle), np.sin(angle)], axis=1).astype(np.float32)),
    }


def _arrays(x):
    t, k = np.arange(P)[:, None], np.arange(256)[None, :]
    arrays = {
        "xT": _feature_major(x["x"][0]),
        "pT": _feature_major(x["p"][0, 0]),
        "weights": _stream(x),
        "vectors": _vectors(x),
        "rnn_gate_weights": np.ascontiguousarray(np.concatenate([x["w_rg_2"][0], x["w_ig_2"][0]], axis=2).transpose(1, 0, 2)),
        "bias": np.ascontiguousarray(x["attn_rel_bias"][0][:, np.clip(t + P - k, -128, 128) + 128].transpose(1, 0, 2)),
    }
    arrays.update(_constants())
    return arrays


def _build(nc, arrays):
    aps = {}
    for name, v in arrays.items():
        aps[name] = nc.dram_tensor(name + "_in", v.shape, mybir.dt.from_np(v.dtype), kind="ExternalInput").ap()
    for name, shape in (("gates", (16, P, S)), ("x_spill_rnn", (P, DC, S)), ("x_spill_mla", (P, DC, S))):
        aps[name] = nc.dram_tensor(name, shape, F32, kind="Internal").ap()
    aps["outT"] = nc.dram_tensor("outT", (P, DC, S), F32, kind="ExternalOutput").ap()
    fused_kernel(nc, aps)


def kernel(**inputs):
    import concourse.bacc as bacc
    from concourse.bass_utils import run_bass_kernel_spmd

    arrays = _arrays({name: np.asarray(v) for name, v in inputs.items()})
    nc = bacc.Bacc("TRN2", target_bir_lowering=False, num_devices=1)
    _build(nc, arrays)
    r = run_bass_kernel_spmd(nc, [{name + "_in": v for name, v in arrays.items()}], core_ids=[0])
    out = np.asarray(r.results[0]["outT"])
    return np.ascontiguousarray(out.transpose(1, 0, 2).reshape(D, S).T)[None]
```

```python
import numpy as np
from contextlib import ExitStack
import concourse.bass as bass
from concourse import mybir

F32 = mybir.dt.float32
F32R = mybir.dt.float32r
ACT = mybir.ActivationFunctionType
ALU = mybir.AluOpType
AX = mybir.AxisListType

P = 128
D = 1024
S = 1024
HALF = 512
EPS = 1e-6
DC = D // P
A_HEADS = 4
HEADS_B = 8
HD_B = 64
D_FF = 2816
FF_GROUPS = (8, 8, 6)
RNN = 1280
RB = RNN // P
HEADS_C = 8
SCALE_C = float((128 + 64) ** -0.5)
NEG = -1e30
LEVELS = (64, 32, 16, 8, 4, 2, 1)
NT = S // P

G_MIX, G_FFN, G_PLE, G_A, G_KV, G_B, G_FIN = 0, 8, 16, 24, 32, 40, 48
V_ONORM, V_QN, V_KN = 56, 57, 58
V_CB, V_LAM, V_BR, V_BI, V_CW = 59, 69, 79, 89, 99
V_KVN, V_CQN, V_EPS, V_CFAR, V_ONE = 139, 141, 144, 145, 153
NVEC = 154

STREAM = [
    ("zqk", 8, 1, 8), ("zv", 4, 1, 8), ("gates", 16, 1, 8), ("za", 16, 1, 8), ("merge", 8, 2, 4), ("wout", 8, 1, 8),
    ("gu0", 16, 1, 8), ("dn0", 8, 1, 8), ("gu1", 16, 1, 8), ("dn1", 8, 1, 8), ("gu2", 12, 1, 8), ("dn2", 8, 1, 6),
    ("proj", 2, 4, 2), ("pleg", 8, 1, 8), ("xg", 2 * RB, 1, 8),
    ("wo1", 8, 1, 5), ("wo2", 8, 1, 5), ("dkv", 3, 1, 8), ("cq", 3, 1, 8), ("cgate", 8, 1, 8),
    ("uk", 2, 4, 2), ("uv", 2, 4, 2), ("uq0", 3, 2, 3), ("uq1", 3, 2, 3), ("wob", 8, 1, 8),
]
STAGE = {}
_u = _t = 0
for _name, _n, _T, _C in STREAM:
    STAGE[_name] = (_u, _t, _n, _T, _C)
    _u += _n
    _t += _n * _T
UNITS = _u
MM_PER_UNIT = 16


def half_of(h):
    return slice(h * HALF, (h + 1) * HALF)


def items_of(eng, n, body, start=0):
    first = start // 2
    for j in range(min(2, n)):
        body(first, j)
    pairs = n // 2
    if pairs == first + 2:
        for j in range(2):
            body(first + 1, j)
    elif pairs > first + 2:
        with eng.Fori(first + 1, pairs) as i:
            for j in range(2):
                body(i, j)
    if n % 2 and n > 2:
        body(n // 2, 0)


def chunk_of(t, m):
    return t[:, m] if isinstance(m, int) else t[:, bass.ds(m, 1)]


def await_at_least(eng, semaphore, count):
    if not isinstance(count, int) or count > 0:
        eng.wait_ge(semaphore, count)


def fused_kernel(nc, a):
    ctx = ExitStack()
    with ctx:
        def sem(name):
            return ctx.enter_context(nc.semaphore(name))

        BASE = (nc.sbuf_base + 31) // 32 * 32
        REG = 32768

        def at(name, shape, off, dt=F32):
            return nc.alloc_sbuf_tensor_at(name, shape, dt, offset=BASE + off)

        def R(r, kib=0):
            return r * REG + kib * 1024

        RING = R(5)
        w_staged = at("w_staged", [P, 2, 1024], RING)
        w_high = at("w_high", [P, 2, 1024], RING + 8192, F32R)
        w_low = at("w_low", [P, 2, 1024], RING + 16384, F32R)
        MISC = RING + 24576
        rstd = at("rstd", [P, S], MISC)
        sq = at("squares", [P, 2, S], MISC + 4096)
        acc = at("square_sum", [P, S], MISC + 12288)
        tmp = at("tmp", [P, S], MISC + 16384)
        ident = at("identity", [P, P], MISC + 20480)
        ones = at("ones", [P, P], MISC + 20992)
        vec = at("vectors", [P, NVEC], MISC + 21504)
        derived = at("derived_vectors", [P, 80], MISC + 21504 + 640)
        stat = at("softmax_stats", [P, 16], MISC + 21504 + 960)

        def V(c, n=1):
            return vec[:, c:c + n]

        eps = V(V_EPS)
        qk_gains = derived[:, 41:49]

        def full(name, region, dt=F32, kib=0, chunks=8):
            return at(name, [P, chunks, S], R(region, kib), dt)

        def f32(t):
            return t.bitcast(F32)

        ps = ctx.enter_context(nc.psum_tensor("ps", [P, 8, HALF], F32))

        x1 = full("x_in", 0)
        h1H, h1L = full("h_mix_high", 3, F32R), full("h_mix_low", 2, F32R)
        qk_b, v_raw = full("z_band_qk", 1), full("z_band_v", 4, chunks=4)
        v_tok = at("v_band_by_token", [P, NT, HEADS_B * HD_B], R(4, 16))
        bias = at("band_bias", [P, HEADS_B, 256], R(4, 0))
        o_tok = at("o_band_by_token", [P, 2, HEADS_B * HD_B], R(4, 8))
        head_ones = at("head_ones", [P, P], MISC + 22528)
        far_mask = at("far_mask", [P, 64], MISC + 23040)
        probs_b = at("probs_band", [P, 2, 640], MISC + 4096)
        probsT_b = at("probs_band_T", [P, 2, 640], MISC + 12288)
        obH, obL = full("o_band_high", 0, F32R, 0, 4), full("o_band_low", 0, F32R, 16, 4)
        CH = A_HEADS * P
        z_qf, z_ig = [at(f"z_hgrn_{n}", [P, 2, NT, A_HEADS, P], R(r)) for n, r in (("qf", 1), ("ig", 4))]
        za = {"q": z_qf[:, 0], "f": z_qf[:, 1], "i": z_ig[:, 0], "g": z_ig[:, 1]}
        zq, zf, zi, zg = [za[w].rearrange("p c h t -> p (c h t)") for w in "qfig"]
        hb = at("hgrn_log_decay", [P, NT * CH], MISC + 4096)
        k_end = at("hgrn_k_to_end", [P, NT * CH], R(3))
        attn = at("hgrn_attn", [P, NT * CH], R(3, 16))
        hd = at("hgrn_decays", [P, NT * CH], R(2))
        hqk = at("hgrn_decayed_qk", [P, NT * CH], R(2, 16))
        masks = at("level_masks", [P, 8, P], MISC)
        states = at("hgrn_state", [P, 2, CH], MISC + 4096)
        o_sq = at("hgrn_o_squares", [P, 2, CH], MISC + 8192)
        o_rstd = at("hgrn_o_rstd", [P, 4, CH], MISC + 12288)
        chunk_decay = at("hgrn_chunk_decay", [P, NT * A_HEADS], MISC + 23296)
        o_h = at("hgrn_o", [P, NT * CH], R(2, 16))
        oaH, oaL = full("o_hgrn_high", 1, F32R, 0, 4), full("o_hgrn_low", 1, F32R, 16, 4)
        mgH, mgL = full("merged_high", 3, F32R), full("merged_low", 4, F32R)
        gate_in = at("gates_loaded", [P, 2, 2, S], MISC + 4096)
        x2 = full("x_mid", 2)
        h2H, h2L = full("h_ffn_high", 0, F32R), full("h_ffn_low", 1, F32R)
        actH, actL = full("act_high", 3, F32R), full("act_low", 4, F32R)
        proj = full("ple_proj", 3)
        p_in = full("p_in", 4, F32, 0, 2)
        pH, pL = full("p_high", 4, F32R, 8, 2), full("p_low", 4, F32R, 16, 2)
        h4H, h4L = full("h_rnn_high", 3, F32R), full("h_rnn_low", 4, F32R)
        xb = full("rnn_in", 0, F32, 0, RB)
        rgate = full("rnn_gate", 1, F32, 8, RB)
        yH, yL = full("rnn_y_high", 0, F32R, 0, RB), full("rnn_y_low", 1, F32R, 8, RB)
        conv = at("rnn_conv", [P, S], MISC + 4096)
        convH, convL = at("rnn_conv_high", [P, S], MISC + 8192, F32R), at("rnn_conv_low", [P, S], R(2, 16), F32R)
        r_buf = at("rnn_r", [P, S], MISC + 12288)
        i_buf = at("rnn_i", [P, S], MISC + 16384)
        w_ri = at("rnn_gate_weights", [P, RB, 2 * P], R(2, 20))
        w_riH, w_riL = [at(f"rnn_gate_weights_{n}", [P, 2 * P], R(2, k), F32R) for n, k in (("high", 30), ("low", 31))]
        x4 = full("x_late", 3)
        h5H, h5L = full("h_kv_high", 1, F32R), full("h_kv_low", 2, F32R)
        h6H, h6L = full("h_mla_high", 0, F32R), full("h_mla_low", 4, F32R)
        ckv = sq
        ckvH, ckvL = full("ckv_high", 2, F32R, 0, 2), full("ckv_low", 2, F32R, 8, 2)
        cq = full("cq", 2, F32, 16, 3)
        cqH, cqL = full("cq_high", 1, F32R, 0, 3), full("cq_low", 1, F32R, 12, 3)
        k_rope = at("k_rope", [P, S], R(1, 24))
        rotate = at("rope_rotate", [P, P], R(1, 28))
        causal = at("causal_mask", [P, P], R(1, 28) + 512)
        o_mla = at("o_mla_by_token", [P, 2, P], R(1, 28) + 1024)
        cos_sin = at("cos_sin", [P, 2, S], R(2, 24))
        cgate = full("mla_gate", 3)
        k_nope = full("k_nope", 0)
        v_mla = full("v_mla", 4)
        q_nope = full("q_nope", 2, F32, 0, 4)
        q_rope = full("q_rope", 2, F32, 16, 2)
        probs_c = at("probs_mla", [P, 2, S], MISC + 4096)
        probsT_c = at("probs_mla_T", [P, 2, S], MISC + 12288)
        y7H, y7L = full("y_mla_high", 0, F32R), full("y_mla_low", 4, F32R)
        x5 = full("x_last", 1)
        out_sb = full("x_out", 2)

        s_load = [sem(f"unit_loaded{j}") for j in range(2)]
        s_split = sem("unit_split")
        s_mm = sem("tile_done")
        s_free = [sem(f"bank{b}_read") for b in range(4)]
        s_const = sem("constants_loaded")
        s_x = [sem(f"x_loaded{k}") for k in range(4)]
        s_h = sem("chunk_high")
        s_l = sem("chunk_low")
        s_nsum = sem("norm_summed")
        s_ln, s_rstd = sem("logarithm"), sem("norm_rstd")
        s_ldone, s_vchain = sem("lambda_exp"), sem("vector_chain")
        s_wh = sem("unit_high")
        s_gz, s_gs = sem("gate_scaled"), sem("gate_sigmoid")
        s_gst = [sem(f"gate_stored{j}") for j in range(2)]
        s_bsq, s_bsum, s_bln, s_brstd, s_bn = [sem(f"head_norm_{n}") for n in ("square", "sum", "ln", "rstd", "done")]
        s_vT, s_vt = sem("v_transposed"), sem("v_by_token")
        s_bconst, s_bias = sem("band_constants"), sem("bias_ready")
        s_hg, s_ha, s_hp, s_hk, s_hscan = sem("hgrn_gate_silu"), sem("hgrn_softplus"), sem("hgrn_logf"), sem("hgrn_k"), sem("hgrn_scan")
        s_lD0, s_lD, s_lE, s_lQ, s_lS, s_lP = [sem(f"level_{n}") for n in ("first_difference", "difference", "decay", "qk", "scores", "placed")]
        s_hm = sem("level_masks_loaded")
        s_eb, s_qe, s_kb, s_ke, s_kd = [sem(f"state_{n}") for n in ("exp_b", "q", "k_difference", "exp_k", "k")]
        s_iT, s_iTe = sem("values_transposed"), sem("values_by_token")
        s_hT, s_hTe = sem("keys_transposed"), sem("keys_by_token")
        s_hU, s_hst, s_hO, s_hOe = sem("state_update"), sem("state_new"), sem("hgrn_o"), sem("hgrn_o_read")
        s_h2, s_hn, s_hrstd, s_hw = sem("o_squared"), sem("o_summed"), sem("o_rstd"), sem("o_normed")
        s_hout, s_hoh, s_hol = sem("o_gated"), sem("o_high"), sem("o_low")
        s_gin = [sem(f"gates_in{j}") for j in range(2)]
        s_mg, s_mgh, s_mgl = sem("merged"), sem("merged_high"), sem("merged_low")
        s_x2 = sem("x_mid_loaded")
        s_silu, s_act, s_acth, s_actl = sem("silu"), sem("act"), sem("act_high"), sem("act_low")
        s_p, s_ph, s_pl, s_sig, s_pc, s_pz = [sem(f"ple_{n}") for n in ("loaded", "high", "low", "sigmoid", "product", "added")]
        s_xs3, s_xld4 = sem("x_spilled"), sem("x_reloaded")
        s_rg, s_cv, s_ch, s_cl = sem("rnn_gate_silu"), sem("conv_chain"), sem("conv_high"), sem("conv_low")
        s_wri, s_wrh, s_wrl = sem("gate_weights_loaded"), sem("gate_weights_high"), sem("gate_weights_low")
        s_ri, s_sg, s_ix, s_a, s_T, s_rs, s_rw = [sem(f"rnn_{n}") for n in ("products", "sigmoid", "ix", "a", "tanh", "sqrt", "chain")]
        s_yg, s_yh, s_yl = sem("rnn_y"), sem("rnn_y_high"), sem("rnn_y_low")
        s_xs5, s_xld5, s_cconst = sem("x_spilled_2"), sem("x_reloaded_2"), sem("mla_constants")
        s_c2, s_cs, s_crstd, s_cw, s_cwh, s_cwl = [sem(f"latent_{n}") for n in ("square", "sum", "rstd", "chain", "high", "low")]
        s_rot, s_kr, s_cg = sem("k_rotated"), sem("k_rope_chain"), sem("mla_gate_silu")
        s_rq, s_rotq, s_rqe, s_qready = [sem(f"q_rope_{n}") for n in ("raw", "rotated", "chain", "ready")]
        s_y7h, s_y7l = sem("mla_y_high"), sem("mla_y_low")
        s_out, s_fin = sem("out_stored"), sem("out_ready")

        block = ctx.enter_context(nc.Block())

        def base(stage):
            u0, t0, n, T, C = STAGE[stage]
            return u0, t0, n * T, MM_PER_UNIT // (2 * T)

        def mm_count(stage, item, h):
            u0, _, _, inc = base(stage)
            return item * (2 * inc) + (MM_PER_UNIT * u0 + inc * (h + 1))

        def bank_of(stage, j, h):
            return 2 * ((STAGE[stage][1] + j) % 2) + h

        def use_of(stage, i, j):
            return i + (STAGE[stage][1] + j) // 2

        def level_difference(engine, n):
            size = LEVELS[n // 2]
            part = slice((n % 2) * 4 * CH, (n % 2 + 1) * 4 * CH)
            b_ = hb[:, part].rearrange("p (n w) -> p n w", w=2 * size)
            return engine.tensor_tensor(hd[:, part].rearrange("p (n w) -> p n w", w=2 * size), b_,
                                        b_[:, :, size - 1:size].broadcast_to([P, 4 * CH // (2 * size), 2 * size]), ALU.subtract)

        @block.sync
        def _(sp):
            for k in range(4):
                sp.dma_start(x1[:, 2 * k:2 * k + 2], a["xT"][:, 2 * k:2 * k + 2]).then_inc(s_x[k], 16)

            def load(i, j):
                u = 2 * i + j
                await_at_least(sp, s_split, u - 1)
                sp.dma_start(w_staged[:, j], a["weights"][bass.ds(u, 1)].rearrange("u p n -> p (u n)")).then_inc(s_load[j], 16)

            items_of(sp, UNITS, load)
            for h in range(2):
                sp.wait_ge(s_fin, 4 * (h + 1))
                sp.dma_start(a["outT"][:, 4 * h:4 * h + 4], out_sb[:, 4 * h:4 * h + 4]).then_inc(s_out, 16)
            sp.wait_ge(s_out, 32)

        @block.gpsimd
        def _(pool):
            def split(i, j):
                u = 2 * i + j
                pool.wait_ge(s_load[j], (i + 1) * 16)
                if not (isinstance(i, int) and i == 0):
                    pool.wait_ge(s_mm, (u - 1) * MM_PER_UNIT)
                nc.gpsimd.tensor_tensor(derived[0:1, 72:73], w_staged[0:1, j, 0:1], w_staged[0:1, j, 0:1], ALU.add)
                nc.gpsimd.tensor_copy(w_high[:, j], w_staged[:, j]).then_inc(s_wh, 1)
                pool.wait_ge(s_wh, u + 1)
                nc.gpsimd.tensor_tensor(w_low[:, j], w_staged[:, j], f32(w_high[:, j]), ALU.subtract).then_inc(s_split, 1)

            merge0 = STAGE["merge"][0]
            items_of(pool, merge0, split)

            def to_end(k):
                part = slice(k * 4 * CH, (k + 1) * 4 * CH)
                bk = hb[:, part].rearrange("p (n t) -> p n t", t=P)
                nc.gpsimd.tensor_tensor(k_end[:, part].rearrange("p (n t) -> p n t", t=P), bk,
                                        bk[:, :, P - 1:P].broadcast_to([P, 4 * A_HEADS, P]), ALU.subtract).then_inc(s_kb, 1)

            pool.wait_ge(s_hscan, 1)
            pool.wait_ge(s_mm, mm_count("za", 15, 1))
            to_end(0)
            for n in range(2, 14):
                pool.wait_ge(s_lQ, n - 1)
                level_difference(nc.gpsimd, n).then_inc(s_lD, 1)
            to_end(1)
            items_of(pool, UNITS, split, merge0)

        class Attention:
            def __init__(self, name, items, width, scale, probs, probsT):
                self.items, self.width, self.scale, self.probs, self.probsT = items, width, scale, probs, probsT
                (self.scored, self.maxed, self.negated, self.probed, self.transposed, self.copied, self.summed,
                 self.inverted, self.out, self.outT, self.outH, self.outL) = [
                    sem(f"{name}_{n}") for n in ("scores", "max", "neg_max", "probs", "probs_T", "probs_T_copied",
                                                 "o", "inverse", "o_by_token", "o_T", "o_high", "o_low")]

            def scores_of(self, n):
                b = 2 * (n % 2)
                return ps[:, b:b + 2].rearrange("p b n -> p (b n)")[:, 0:self.items[n][2] * P]

        transposed_flat = ps[:, 4:6].rearrange("p b n -> p (b n)")

        def attention_tensor(pe, at_, scores, values, deferred, bank_free):
            N = len(at_.items)

            def emit_scores(n):
                await_at_least(pe, at_.probed, n - 1)
                scores(n, 2 * (n % 2)).then_inc(at_.scored, 1)

            emit_scores(0)
            emit_scores(1)
            for n, (h, j, nk) in enumerate(at_.items):
                pe.wait_ge(at_.probed, n + 1)
                await_at_least(pe, at_.copied, n)
                for k in range(nk):
                    last = nc.tensor.transpose(transposed_flat[:, k * P:(k + 1) * P],
                                               at_.probs[:, n % 2, k * P:(k + 1) * P], ident[:])
                last.then_inc(at_.transposed, 1)
                if n + 2 < N:
                    emit_scores(n + 2)
                pe.wait_ge(at_.copied, n + 1)
                await_at_least(pe, at_.out, n - 1)
                if n >= 2:
                    bank_free(n - 2)
                for k in range(nk):
                    last = nc.tensor.matmul(ps[:, 6 + n % 2, 0:at_.width],
                                            at_.probsT[:, n % 2, k * P:(k + 1) * P], values(n, k),
                                            start=(k == 0), stop=(k == nk - 1))
                last.then_inc(at_.summed, 1)
                if n >= 1:
                    deferred(n - 1)
            deferred(N - 1)

        def attention_scalar(act, at_, deferred):
            N = len(at_.items)
            for n, (h, j, nk) in enumerate(at_.items):
                q = n % 4
                act.wait_ge(at_.negated, n + 1)
                await_at_least(act, at_.transposed, n - 1)
                nc.scalar.activation(at_.probs[:, n % 2, 0:nk * P], at_.scores_of(n), ACT.Exp,
                                     bias=stat[:, 4 + q:5 + q], scale=at_.scale,
                                     accum_out=stat[:, 8 + q:9 + q]).then_inc(at_.probed, 1)
                if n >= 3:
                    deferred(n - 3)
            for n in range(N - 3, N):
                deferred(n)

        def attention_vector(dve, at_, destination, deferred):
            N = len(at_.items)
            for n in range(N + 2):
                if n < N:
                    q = n % 4
                    dve.wait_ge(at_.scored, n + 1)
                    nc.vector.reduce_max(stat[:, q:q + 1], at_.scores_of(n), AX.X).then_inc(at_.maxed, 1)
                    dve.wait_ge(at_.maxed, n + 1)
                    nc.vector.tensor_scalar(stat[:, 4 + q:5 + q], stat[:, q:q + 1], -at_.scale, None,
                                            ALU.mult).then_inc(at_.negated, 1)
                if 1 <= n <= N:
                    m = n - 1
                    nk = at_.items[m][2]
                    dve.wait_ge(at_.transposed, m + 1)
                    await_at_least(dve, at_.summed, m - 1)
                    nc.vector.tensor_copy(at_.probsT[:, m % 2, 0:nk * P], transposed_flat[:, 0:nk * P]).then_inc(at_.copied, 1)
                if n >= 2:
                    m = n - 2
                    q = m % 4
                    dve.wait_ge(at_.probed, m + 1)
                    nc.vector.reciprocal(stat[:, 12 + q:13 + q], stat[:, 8 + q:9 + q]).then_inc(at_.inverted, 1)
                    dve.wait_ge(at_.inverted, m + 1)
                    dve.wait_ge(at_.summed, m + 1)
                    destination(m, ps[:, 6 + m % 2, 0:at_.width], stat[:, 12 + q:13 + q]).then_inc(at_.out, 1)
                if n >= 3:
                    deferred(n - 3)
            deferred(N - 1)

        band = Attention("band", [(h, j, min(j + 1, 5)) for j in range(NT) for h in range(HEADS_B)], HD_B, 1.0, probs_b, probsT_b)
        mla = [Attention(f"mla{g}", [(4 * g + h, j, j + 1) for j in range(NT) for h in range(4)], P, SCALE_C, probs_c, probsT_c)
               for g in range(2)]

        @block.tensor
        def _(pe):
            def tile(stage, i, j, slot, width, column, chunks, rhs, first_wait=None):
                u0, t0, _, inc = base(stage)
                for h in range(2):
                    bank = bank_of(stage, j, h)
                    await_at_least(pe, s_free[bank], use_of(stage, i, j))
                    for n, (c, r) in enumerate(chunks):
                        if first_wait and h == 0:
                            pe.wait_ge(*first_wait(r))
                        wH = w_high[:, slot, c * width + column:c * width + column + P]
                        wL = w_low[:, slot, c * width + column:c * width + column + P]
                        tok = half_of(h)
                        nc.tensor.matmul(ps[:, bank], wH, rhs[0][:, r, tok], start=(n == 0), stop=False)
                        nc.tensor.matmul(ps[:, bank], wH, rhs[1][:, r, tok], start=False, stop=False)
                        last = nc.tensor.matmul(ps[:, bank], wL, rhs[0][:, r, tok], start=False, stop=(n == len(chunks) - 1))
                    last.then_inc(s_mm, inc)

            def gemm(stage, rhs, ready, hook=None, chunk0=0, after=None):
                u0, t0, n, T, C = STAGE[stage]

                def unit(i, j):
                    pe.wait_ge(s_split, 2 * i + (j + u0 + 1))
                    first = isinstance(i, int) and i == 0 and j == 0
                    tile(stage, i, j, (u0 + j) % 2, P, 0, [(c, chunk0 + c) for c in range(C)], rhs, ready if first else None)
                    if first and hook:
                        hook()
                    if after and j == 1:
                        after(i)

                items_of(pe, n, unit)

            def low(q):
                return lambda r: (s_l, 8 * q + r + 1)

            def norm(n, q):
                def hook():
                    pe.wait_ge(s_l, 8 * q + 8)
                    for h in range(2):
                        nc.tensor.matmul(ps[:, 4 + h], ones[:], acc[:, half_of(h)], start=True, stop=True).then_inc(s_nsum, 1)
                return hook

            pe.wait_ge(s_const, 48)
            gemm("zqk", (h1H, h1L), low(0), norm(0, 0))
            gemm("zv", (h1H, h1L), None)

            def band_sums(i):
                first = isinstance(i, int)
                if first:
                    pe.wait_ge(s_bconst, 32)
                pe.wait_ge(s_bsq, i + 1)
                await_at_least(pe, s_brstd, 2 * i)
                for h in range(2):
                    nc.tensor.matmul(ps[:, 4 + h], head_ones[:], tmp[:, half_of(h)], start=True, stop=True).then_inc(s_bsum, 1)
                if first:
                    for t in range(NT):
                        await_at_least(pe, s_vt, t - 1)
                        for c in range(4):
                            last = nc.tensor.transpose(ps[:, 6 + t % 2, c * P:(c + 1) * P], v_raw[:, c, t * P:(t + 1) * P], ident[:])
                        last.then_inc(s_vT, 1)

            gemm("gates", (h1H, h1L), None, after=band_sums)
            pe.wait_ge(s_vt, NT)
            pe.wait_ge(s_bn, DC)
            pe.wait_ge(s_bias, 2 * HEADS_B)

            def band_key_order(j, nk):
                near = [j - 1, j] if nk > 1 else [j]
                far = [t for t in (j - 3, j - 2) if t >= 0 and j - t < nk]
                return near + far + ([j - 4] if nk == 5 else [])

            def band_scores(n, bank):
                h, j, nk = band.items[n]
                rows = slice(64 * (h % 2), 64 * (h % 2) + 64)
                q = qk_b[rows, h // 2, j * P:(j + 1) * P]
                order = band_key_order(j, nk)
                near = min(nk, 2)
                out = ps[:, bank, 0:near * P]
                nc.tensor.matmul(out, q, qk_b[rows, 4 + h // 2, order[0] * P:(order[0] + near) * P], start=True, stop=False)
                last = nc.tensor.matmul(out, ident[:], bias[:, h, 256 - near * P:256], start=False, stop=True)
                far = min(nk, 4) - near
                if far > 0:
                    k0 = order[near] * P
                    last = nc.tensor.matmul(ps[:, bank, 256:256 + far * P], q, qk_b[rows, 4 + h // 2, k0:k0 + far * P], start=True, stop=True)
                if nk == 5:
                    k0 = (j - 4) * P
                    nc.tensor.matmul(ps[:, bank + 1, 0:P], q, qk_b[rows, 4 + h // 2, k0:k0 + P], start=True, stop=False)
                    last = nc.tensor.matmul(ps[:, bank + 1, 0:64], ident[:], far_mask[:], start=False, stop=True)
                return last

            def band_values(n, k):
                h, j, nk = band.items[n]
                return v_tok[:, band_key_order(j, nk)[k], h * HD_B:(h + 1) * HD_B]

            def band_out_T(m):
                h, j, _ = band.items[m]
                if h == HEADS_B - 1:
                    pe.wait_ge(band.out, m + 1)
                    for c in range(4):
                        last = nc.tensor.transpose(ps[:, 6 + m % 2, c * P:(c + 1) * P], o_tok[:, j % 2, c * P:(c + 1) * P], ident[:])
                    last.then_inc(band.outT, 1)

            def band_bank_free(m):
                h, j, _ = band.items[m]
                if h == HEADS_B - 1:
                    pe.wait_ge(band.outL, j + 1)

            attention_tensor(pe, band, band_scores, band_values, band_out_T, band_bank_free)
            pe.wait_ge(band.outL, NT)

            gemm("za", (h1H, h1L), None)

            pe.wait_ge(s_free[bank_of("za", 1, 1)], use_of("za", 7, 1) + 1)
            for m in range(16):
                half = m % 2
                if m == 1:
                    for c in range(NT):
                        await_at_least(pe, s_iTe, c - 3)
                        for h in range(A_HEADS):
                            k0 = (c * A_HEADS + h) * P
                            last = nc.tensor.transpose(ps[:, 4 + c % 4, h * P:(h + 1) * P], zi[:, k0:k0 + P], ident[:])
                        last.then_inc(s_iT, 1)
                    pe.wait_ge(s_iTe, NT)
                if m >= 2:
                    pe.wait_ge(s_lQ, m - 1)
                for k in range(4):
                    c = 4 * half + k
                    await_at_least(pe, s_lP, 4 * (m - 2) + k + 1)
                    for h in range(A_HEADS):
                        k0 = (c * A_HEADS + h) * P
                        lhs, rhs = (zf, zq) if m < 2 else (hqk, hqk)
                        last = nc.tensor.matmul(ps[:, c, h * P:(h + 1) * P], lhs[:, k0:k0 + P], rhs[:, k0:k0 + P], start=True, stop=True)
                    last.then_inc(s_lS, 1)

            def keys_by_token(c):
                pe.wait_ge(s_kd, c // 4 + 1)
                await_at_least(pe, s_hTe, c - 1)
                for h in range(A_HEADS):
                    k0 = (c * A_HEADS + h) * P
                    last = nc.tensor.transpose(ps[:, c % 2, h * P:(h + 1) * P], k_end[:, k0:k0 + P], ident[:])
                last.then_inc(s_hT, 1)

            def o_norm(c):
                pe.wait_ge(s_h2, c + 1)
                await_at_least(pe, s_hrstd, c - 1)
                nc.tensor.matmul(ps[:, 2 + c % 2], ones[:], o_sq[:, c % 2], start=True, stop=True).then_inc(s_hn, 1)

            pe.wait_ge(s_lP, 60)
            keys_by_token(0)
            pe.wait_ge(s_lP, 64)
            for c in range(NT):
                if c + 1 < NT:
                    keys_by_token(c + 1)
                    pe.wait_ge(s_hTe, c + 1)
                    await_at_least(pe, s_hst, c - 1)
                    for h in range(A_HEADS):
                        k0 = (c * A_HEADS + h) * P
                        last = nc.tensor.matmul(ps[:, 6 + c % 2, h * P:(h + 1) * P], k_end[:, k0:k0 + P], zi[:, k0:k0 + P], start=True, stop=True)
                    last.then_inc(s_hU, 1)
                await_at_least(pe, s_hOe, c - 1)
                await_at_least(pe, s_hst, c)
                if c:
                    pe.wait_ge(s_qe, c // 4 + 1)
                for h in range(A_HEADS):
                    k0 = (c * A_HEADS + h) * P
                    out = ps[:, 4 + c % 2, h * P:(h + 1) * P]
                    last = nc.tensor.matmul(out, zi[:, k0:k0 + P], attn[:, k0:k0 + P], start=True, stop=(c == 0))
                    if c:
                        last = nc.tensor.matmul(out, states[:, (c - 1) % 2, h * P:(h + 1) * P], hd[:, k0:k0 + P], start=False, stop=True)
                last.then_inc(s_hO, 1)
                if c:
                    o_norm(c - 1)
            o_norm(NT - 1)
            pe.wait_ge(s_hrstd, NT)

            u0 = STAGE["merge"][0]
            pe.wait_ge(s_hol, NT)

            def merge(i, j):
                pe.wait_ge(s_split, 2 * i + (j + u0 + 1))
                for part, rhs in enumerate(((oaH, oaL), (obH, obL))):
                    tile("merge", 2 * i + j, part, (u0 + j) % 2, P, 0, [(4 * part + c, c) for c in range(4)], rhs)

            items_of(pe, DC, merge)
            gemm("wout", (mgH, mgL), lambda r: (s_mgl, r + 1))
            for g, n in enumerate(FF_GROUPS):
                pairs0 = sum(FF_GROUPS[:g])
                gemm(f"gu{g}", (h2H, h2L), low(1) if g == 0 else None, norm(1, 1) if g == 0 else None)
                gemm(f"dn{g}", (actH, actL), lambda r, p0=pairs0: (s_actl, p0 + r + 1))

            def wide(stage, rhs, ready, moving_weights=False):
                u0, t0, n, T, C = STAGE[stage]
                if ready:
                    pe.wait_ge(*ready)
                for u in range(n):
                    pe.wait_ge(s_split, u0 + u + 1)
                    for r in range(T):
                        t = u * T + r
                        tile(stage, t // 2, t % 2, (u0 + u) % 2, T * P, r * P, [(c, c) for c in range(C)], rhs)

            wide("proj", (pH, pL), (s_pl, 2))
            gemm("pleg", (h2H, h2L), low(2), norm(2, 2))

            def rnn_gates(n):
                pe.wait_ge(s_cl, n + 1)
                pe.wait_ge(s_wrl, n + 1)
                await_at_least(pe, s_sg, 2 * n)
                for g in range(2):
                    wH, wL = [w[:, g * P:(g + 1) * P] for w in (w_riH, w_riL)]
                    for h in range(2):
                        bank, tok = 4 + 2 * g + h, half_of(h)
                        nc.tensor.matmul(ps[:, bank], wH, convH[:, tok], start=True, stop=False)
                        nc.tensor.matmul(ps[:, bank], wH, convL[:, tok], start=False, stop=False)
                        nc.tensor.matmul(ps[:, bank], wL, convH[:, tok], start=False, stop=True).then_inc(s_ri, 1)

            gemm("xg", (h4H, h4L), low(3), norm(3, 3), after=rnn_gates)
            gemm("wo1", (yH, yL), lambda r: (s_yl, r + 1))
            gemm("wo2", (yH, yL), lambda r: (s_yl, r + 1), None, 5)
            gemm("dkv", (h5H, h5L), low(5), norm(4, 4))
            gemm("cq", (h6H, h6L), low(6))

            def latent():
                for k, chunks in enumerate((2, 3)):
                    for c in range(chunks):
                        n = 2 * k + c
                        pe.wait_ge(s_c2, n + 1)
                        await_at_least(pe, s_crstd, 2 * k)
                        for h in range(2):
                            nc.tensor.matmul(ps[:, 4 + h], ones[:], acc[:, half_of(h)], start=(c == 0), stop=(c == chunks - 1)).then_inc(s_cs, 1)

            gemm("cgate", (h6H, h6L), None, latent)
            pe.wait_ge(s_cconst, 48)
            for h in range(2):
                nc.tensor.matmul(ps[:, 6 + h], rotate[:], tmp[:, half_of(h)], start=True, stop=True).then_inc(s_rot, 1)
            wide("uk", (ckvH, ckvL), (s_cwl, 2))
            u0, t0, _, _, _ = STAGE["uv"]
            for v in range(2):
                pe.wait_ge(s_split, u0 + v + 1)
                for r in range(4):
                    for h in range(2):
                        t = 4 * v + r
                        bank = bank_of("uv", t % 2, h)
                        pe.wait_ge(s_free[bank], use_of("uv", t // 2, t % 2))
                        tok = slice((2 * r + h) * P, (2 * r + h + 1) * P)
                        for c in range(2):
                            wH = w_high[:, (u0 + v) % 2, c * HALF:(c + 1) * HALF]
                            wL = w_low[:, (u0 + v) % 2, c * HALF:(c + 1) * HALF]
                            nc.tensor.matmul(ps[:, bank], ckvH[:, c, tok], wH, start=(c == 0), stop=False)
                            nc.tensor.matmul(ps[:, bank], ckvL[:, c, tok], wH, start=False, stop=False)
                            last = nc.tensor.matmul(ps[:, bank], ckvH[:, c, tok], wL, start=False, stop=(c == 1))
                        last.then_inc(s_mm, 2)
            for g in range(2):
                at_ = mla[g]
                wide(f"uq{g}", (cqH, cqL), (s_cwl, 5) if g == 0 else None)
                for n in range(4):
                    pe.wait_ge(s_rq, g + 1)
                    if n >= 2:
                        pe.wait_ge(s_qready, 4 * g + n - 1)
                    nc.tensor.matmul(ps[:, 4 + n % 2], rotate[:], q_rope[:, n // 2, half_of(n % 2)], start=True, stop=True).then_inc(s_rotq, 1)
                pe.wait_ge(s_qready, 4 * (g + 1))

                def mla_scores(n, bank):
                    h, j, nk = at_.items[n]
                    hl = h % 4
                    rows = slice(64 * (hl % 2), 64 * (hl % 2) + 64)
                    for b in range((nk + 3) // 4):
                        k0, k1 = b * HALF, min((b + 1) * HALF, nk * P)
                        out = ps[:, bank + b, 0:k1 - k0]
                        diagonal = k1 == nk * P
                        nc.tensor.matmul(out, q_nope[:, hl, j * P:(j + 1) * P], k_nope[:, h, k0:k1], start=True, stop=False)
                        last = nc.tensor.matmul(out, q_rope[rows, hl // 2, j * P:(j + 1) * P], k_rope[rows, k0:k1], start=False, stop=not diagonal)
                        if diagonal:
                            last = nc.tensor.matmul(ps[:, bank + b, k1 - k0 - P:k1 - k0], ident[:], causal[:], start=False, stop=True)
                    return last

                def mla_values(n, k):
                    h = at_.items[n][0]
                    return v_mla[:, k, h * P:(h + 1) * P]

                def mla_out_T(m):
                    pe.wait_ge(at_.out, m + 1)
                    nc.tensor.transpose(ps[:, 6 + m % 2, 0:P], o_mla[:, m % 2], ident[:]).then_inc(at_.outT, 1)

                attention_tensor(pe, at_, mla_scores, mla_values, mla_out_T, lambda m: pe.wait_ge(at_.outL, m + 1))
                pe.wait_ge(at_.outL, len(at_.items))
            gemm("wob", (y7H, y7L), lambda r: (s_y7l, r + 1))
            norm(5, 7)()

        @block.scalar
        def _(act):
            def split_x(q, x, H, gain, ready=None, squares=True):
                def chunk(i, j):
                    m = 2 * i + j
                    if ready:
                        ready(i, j)
                    if squares:
                        await_at_least(act, s_l, m + (8 * q - 1))
                        last = nc.scalar.activation(sq[:, j], chunk_of(x, m), ACT.Square)
                    if H is not None:
                        last = nc.scalar.activation(chunk_of(H, m), chunk_of(x, m), ACT.Copy, scale=vec[:, bass.ds(m + gain, 1)])
                    last.then_inc(s_h, 1)
                items_of(act, DC, chunk)

            logarithms = [0]

            def inverse_root(items):
                for out, sums, scale, _ in items:
                    nc.scalar.activation(out, sums, ACT.Ln, bias=eps, scale=scale).then_inc(s_ln, 1)
                for k, (out, _, _, done) in enumerate(items):
                    act.wait_ge(s_ln, logarithms[0] + k + 1)
                    nc.scalar.activation(out, out, ACT.Exp, scale=-0.5).then_inc(done, 1)
                logarithms[0] += len(items)

            def norm_rstd(n):
                act.wait_ge(s_nsum, 2 * n + 2)
                inverse_root([(rstd[:, half_of(h)], ps[:, 4 + h], 1.0 / D, s_rstd) for h in range(2)])

            def updated(stage):
                return lambda i, j: act.wait_ge(s_free[bank_of(stage, j, 1)], use_of(stage, i, j) + 1)

            act.dma_start(vec[:], a["vectors"]).then_inc(s_const, 16)
            act.dma_start(ident[:], a["identity"]).then_inc(s_const, 16)
            act.dma_start(ones[:], a["ones"]).then_inc(s_const, 16)
            act.dma_start(head_ones[:], a["head_ones"]).then_inc(s_bconst, 16)
            act.dma_start(far_mask[:], a["far_mask"]).then_inc(s_bconst, 16)
            act.wait_ge(s_const, 48)
            nc.scalar.activation(derived[:, 21:31], V(V_LAM, RB), ACT.Abs).then_inc(s_ldone, 1)
            act.wait_ge(s_ldone, 1)
            nc.scalar.activation(derived[:, 31:41], derived[:, 21:31], ACT.Exp, scale=-1.0).then_inc(s_ldone, 1)

            def x_in(i, j):
                if j == 0:
                    act.wait_ge(s_x[i], 16)

            for i in range(4):
                for j in range(2):
                    m = 2 * i + j
                    x_in(i, j)
                    await_at_least(act, s_l, m - 1)
                    nc.scalar.activation(sq[:, j], x1[:, m], ACT.Square)
                    nc.scalar.activation(h1H[:, m], x1[:, m], ACT.Copy, scale=V(G_MIX + m)).then_inc(s_h, 1)
            norm_rstd(0)

            act.wait_ge(s_free[bank_of("zv", 1, 1)], use_of("zv", 1, 1) + 1)

            def gate(i, j):
                if j == 0:
                    await_at_least(act, s_bsum, 2 * i)
                    nc.scalar.activation(tmp[:], chunk_of(qk_b, i), ACT.Square).then_inc(s_bsq, 1)
                act.wait_ge(s_gz, 2 * i + j + 1)
                nc.scalar.activation(sq[:, j], sq[:, j], ACT.Sigmoid).then_inc(s_gs, 1)
                act.wait_ge(s_gs, 2 * i + j + 1)
                act.dma_start(a["gates"][bass.ds(2 * i + j, 1)].rearrange("u p n -> p (u n)"), sq[:, j]).then_inc(s_gst[j], 16)
                if j == 1:
                    act.wait_ge(s_bsum, 2 * i + 2)
                    await_at_least(act, s_bn, i)
                    for h in range(2):
                        nc.scalar.activation(acc[:, half_of(h)], ps[:, 4 + h], ACT.Ln, bias=eps, scale=1.0 / HD_B).then_inc(s_bln, 1)
                    for h in range(2):
                        act.wait_ge(s_bln, 2 * i + h + 1)
                        nc.scalar.activation(acc[:, half_of(h)], acc[:, half_of(h)], ACT.Exp, scale=-0.5).then_inc(s_brstd, 1)
                    if isinstance(i, int):
                        for t in range(NT):
                            act.wait_ge(s_vT, t + 1)
                            nc.scalar.activation(v_tok[:, t], ps[:, 6 + t % 2], ACT.Copy).then_inc(s_vt, 1)
                        act.dma_start(bias[:], a["bias"]).then_inc(s_bconst, 16)

            items_of(act, 16, gate)
            for j in range(2):
                act.wait_ge(s_gst[j], 8 * 16)

            def band_high(m):
                h, j, _ = band.items[m]
                if h == HEADS_B - 1:
                    act.wait_ge(band.outT, j + 1)
                    nc.scalar.activation(obH[:, :, j * P:(j + 1) * P], ps[:, 6 + m % 2].rearrange("p (c t) -> p c t", c=4), ACT.Copy).then_inc(band.outH, 1)

            attention_scalar(act, band, band_high)

            parts = [slice(k * S, (k + 1) * S) for k in range(4)]
            act.wait_ge(s_free[bank_of("za", 1, 1)], use_of("za", 1, 1) + 1)
            for step, (f, src, scale, bias_) in enumerate(((ACT.Abs, zf, 1.0, 0.0), (ACT.Exp, zq, -1.0, 0.0), (ACT.Ln, zq, 1.0, 1.0))):
                for k, part in enumerate(parts):
                    await_at_least(act, s_ha, 4 * (step - 1) + k + 1)
                    nc.scalar.activation(zq[:, part], src[:, part], f, scale=scale, bias=bias_).then_inc(s_ha, 1)
            for k, part in enumerate(parts):
                act.wait_ge(s_hp, 2 * k + 2)
                nc.scalar.activation(zf[:, part], zq[:, part], ACT.Exp).then_inc(s_hk, 1)
            act.wait_ge(s_free[bank_of("za", 1, 1)], use_of("za", 3, 1) + 1)
            for part in parts:
                nc.scalar.activation(zg[:, part], zg[:, part], ACT.Silu).then_inc(s_hg, 1)
            act.wait_ge(s_free[bank_of("za", 1, 1)], use_of("za", 7, 1) + 1)
            act.dma_start(masks[:], a["masks"]).then_inc(s_hm, 16)

            def decays(n):
                size = LEVELS[n // 2]
                d = hd[:, (n % 2) * 4 * CH:(n % 2 + 1) * 4 * CH].rearrange("p (n two s) -> p n two s", two=2, s=size)
                if n < 2:
                    act.wait_ge(s_lD0, n + 1)
                else:
                    act.wait_ge(s_lD, n - 1)
                nc.scalar.activation(d[:, :, 1], d[:, :, 1], ACT.Exp)
                nc.scalar.activation(d[:, :, 0], d[:, :, 0], ACT.Exp, scale=-1.0).then_inc(s_lE, 1)

            def k_end_decays(k):
                part = slice(k * 4 * CH, (k + 1) * 4 * CH)
                act.wait_ge(s_kb, k + 1)
                nc.scalar.activation(k_end[:, part], k_end[:, part], ACT.Exp, scale=-1.0).then_inc(s_ke, 1)

            for k in range(2):
                decays(k)
                for c in range(4 * k, 4 * k + 4):
                    act.wait_ge(s_iT, c + 1)
                    nc.scalar.activation(zi[:, c * CH:(c + 1) * CH], ps[:, 4 + c % 4], ACT.Copy).then_inc(s_iTe, 1)
            k_end_decays(0)
            for n in range(2, 14):
                decays(n)
            for k in range(2):
                part = slice(k * 4 * CH, (k + 1) * 4 * CH)
                act.wait_ge(s_lQ, 13 + k)
                nc.scalar.activation(hd[:, part], hb[:, part], ACT.Exp).then_inc(s_eb, 1)
            nc.scalar.activation(chunk_decay[:], hb[:].rearrange("p (n t) -> p n t", t=P)[:, :, P - 1], ACT.Exp).then_inc(s_eb, 1)
            k_end_decays(1)

            def keys_copied(c):
                act.wait_ge(s_hT, c + 1)
                nc.scalar.activation(k_end[:, c * CH:(c + 1) * CH], ps[:, c % 2], ACT.Copy).then_inc(s_hTe, 1)

            def o_rstds(m):
                act.wait_ge(s_hn, m + 2)
                await_at_least(act, s_hw, m - 2)
                inverse_root([(o_rstd[:, c % 4], ps[:, 2 + c % 2], 1.0 / P, s_hrstd) for c in (m, m + 1)])

            def oa_high(c):
                act.wait_ge(s_hout, c + 1)
                nc.scalar.activation(oaH[:, :, c * P:(c + 1) * P], o_h[:, c * CH:(c + 1) * CH].rearrange("p (h t) -> p h t", h=4), ACT.Copy).then_inc(s_hoh, 1)

            keys_copied(0)
            for c in range(NT):
                part = slice(c * CH, (c + 1) * CH)
                if c + 1 < NT:
                    keys_copied(c + 1)
                act.wait_ge(s_hO, c + 1)
                nc.scalar.activation(o_h[:, part], ps[:, 4 + c % 2], ACT.Copy, scale=float(P ** -0.5)).then_inc(s_hOe, 1)
                act.wait_ge(s_hOe, c + 1)
                await_at_least(act, s_hn, c - 1)
                nc.scalar.activation(o_sq[:, c % 2], o_h[:, part], ACT.Square).then_inc(s_h2, 1)
                if c in (2, 4, 6):
                    o_rstds(c - 2)
                if c in (4, 6):
                    oa_high(c - 4)
                    oa_high(c - 3)
            o_rstds(6)
            for c in range(4, NT):
                oa_high(c)
            act.wait_ge(s_hol, NT)
            act.dma_start(x2[:], a["xT"]).then_inc(s_x2, 16)

            def gates_in(m, j):
                act.dma_start(gate_in[:, j], a["gates"].rearrange("(g m) p n -> m p g n", g=2)[bass.ds(m, 1)].rearrange("m p g n -> p (m g) n")).then_inc(s_gin[j], 16)

            for j in range(2):
                gates_in(j, j)

            def merged_high(i, j):
                m = 2 * i + j
                act.wait_ge(s_mg, m + 1)
                nc.scalar.activation(chunk_of(mgH, m), gate_in[:, j, 0], ACT.Copy).then_inc(s_mgh, 1)
                act.wait_ge(s_mgl, m + 1)

            for i in range(4):
                for j in range(2):
                    merged_high(i, j)
                    if i < 3:
                        gates_in(2 * i + j + 2, j)
            split_x(1, x2, h2H, G_FFN, updated("wout"))
            norm_rstd(1)
            for g, n in enumerate(FF_GROUPS):
                p0 = sum(FF_GROUPS[:g])
                u0 = f"gu{g}"

                def pair(i, j, p0=p0, u0=u0):
                    m = 2 * i + j
                    act.wait_ge(s_free[bank_of(u0, 0, 1)], m + (STAGE[u0][1] // 2 + 1))
                    nc.scalar.activation(sq[:, 0], sq[:, 0], ACT.Silu).then_inc(s_silu, 1)
                    act.wait_ge(s_act, m + (p0 + 1))
                    nc.scalar.activation(chunk_of(actH, m), tmp[:], ACT.Copy).then_inc(s_acth, 1)

                items_of(act, n, pair)
            split_x(2, x2, h2H, G_PLE, updated("dn2"))
            act.wait_ge(s_mm, mm_count("dn2", 7, 1))
            act.dma_start(p_in[:], a["pT"]).then_inc(s_p, 16)
            act.wait_ge(s_p, 16)
            for c in range(2):
                nc.scalar.activation(pH[:, c], p_in[:, c], ACT.Copy).then_inc(s_ph, 1)
            norm_rstd(2)

            def ple(i, j):
                m = 2 * i + j
                act.wait_ge(s_free[bank_of("pleg", j, 1)], use_of("pleg", i, j) + 1)
                nc.scalar.activation(tmp[:], tmp[:], ACT.Sigmoid).then_inc(s_sig, 1)
                act.wait_ge(s_pz, m + 1)
                await_at_least(act, s_l, m + (8 * 3 - 1))
                nc.scalar.activation(sq[:, j], chunk_of(x2, m), ACT.Square)
                nc.scalar.activation(chunk_of(h4H, m), chunk_of(x2, m), ACT.Copy, scale=vec[:, bass.ds(m + G_A, 1)]).then_inc(s_h, 1)

            items_of(act, DC, ple)
            act.wait_ge(s_l, 8 * 4)
            act.dma_start(a["x_spill_rnn"], x2[:]).then_inc(s_xs3, 16)
            norm_rstd(3)

            act.wait_ge(s_xs3, 16)
            act.dma_start(w_ri[:], a["rnn_gate_weights"]).then_inc(s_wri, 16)
            act.wait_ge(s_wri, 16)

            def y_high(n):
                act.wait_ge(s_yg, n + 1)
                nc.scalar.activation(chunk_of(yH, n), chunk_of(rgate, n), ACT.Copy).then_inc(s_yh, 1)

            def rnn_block(n):
                first = isinstance(n, int)
                of = lambda column: vec[:, bass.ds(n + column, 1)]
                derived_of = lambda column: derived[:, bass.ds(n + column, 1)]
                await_at_least(act, s_ri, 4 * n)
                nc.scalar.activation(w_riH[:], w_ri[:, n] if first else w_ri[:, bass.ds(n, 1)], ACT.Copy).then_inc(s_wrh, 1)
                act.wait_ge(s_cv, 4 * n + 4)
                nc.scalar.activation(convH[:], conv[:], ACT.Copy).then_inc(s_ch, 1)
                if not first:
                    y_high(n - 1)
                act.wait_ge(s_free[bank_of("xg", 1, 1)], use_of("xg", n, 1) + 1)
                nc.scalar.activation(chunk_of(rgate, n), chunk_of(rgate, n), ACT.Silu).then_inc(s_rg, 1)
                for g, (buf, b) in enumerate(((r_buf, V_BR), (i_buf, V_BI))):
                    act.wait_ge(s_ri, 4 * n + (2 * g + 2))
                    nc.scalar.activation(buf[:], ps[:, 4 + 2 * g:6 + 2 * g].rearrange("p b n -> p (b n)"), ACT.Sigmoid, bias=of(b)).then_inc(s_sg, 1)
                act.wait_ge(s_sg, 2 * n + 2)
                nc.scalar.activation(chunk_of(xb, n), r_buf[:], ACT.Exp, scale=derived_of(1)).then_inc(s_a, 1)
                act.wait_ge(s_a, n + 1)
                nc.scalar.activation(r_buf[:], r_buf[:], ACT.Tanh, scale=derived_of(11)).then_inc(s_T, 1)
                act.wait_ge(s_T, n + 1)
                nc.scalar.activation(r_buf[:], r_buf[:], ACT.Sqrt).then_inc(s_rs, 1)

            rnn_block(0)
            with act.Fori(1, RB) as n:
                rnn_block(n)
            act.wait_ge(s_mm, mm_count("xg", 2 * RB - 1, 1))
            act.dma_start(x4[:], a["x_spill_rnn"]).then_inc(s_xld4, 16)
            y_high(RB - 1)
            split_x(4, x4, None, 0, updated("wo2"))
            split_x(5, x4, h5H, G_KV, None, False)
            norm_rstd(4)
            split_x(6, x4, h6H, G_B, None, False)
            act.dma_start(a["x_spill_mla"], x4[:]).then_inc(s_xs5, 16)
            n = 0
            for k, (stage, chunks, width, src, H) in enumerate((("dkv", 2, 256, ckv, ckvH), ("cq", 3, 384, cq, cqH))):
                act.wait_ge(s_free[bank_of(stage, 2, 1)], use_of(stage, 0, 2) + 1)
                if k == 0:
                    act.dma_start(rotate[:], a["rotate"]).then_inc(s_cconst, 16)
                    act.dma_start(causal[:], a["causal"]).then_inc(s_cconst, 16)
                else:
                    act.wait_ge(s_cwl, 2)
                for c in range(chunks):
                    await_at_least(act, s_cs, 2 * n)
                    nc.scalar.activation(acc[:], src[:, c], ACT.Square).then_inc(s_c2, 1)
                    n += 1
                act.wait_ge(s_cs, 2 * n)
                inverse_root([(acc[:, half_of(h)], ps[:, 4 + h], 1.0 / width, s_crstd) for h in range(2)])
                for c in range(chunks):
                    act.wait_ge(s_cw, 2 * k + c + 1)
                    nc.scalar.activation(H[:, c], src[:, c], ACT.Copy).then_inc(s_cwh, 1)
            act.wait_ge(s_cwl, 5)
            act.dma_start(cos_sin[:], a["cos_sin"]).then_inc(s_cconst, 16)

            def mla_gate(i, j):
                act.wait_ge(s_free[bank_of("cgate", j, 1)], use_of("cgate", i, j) + 1)
                nc.scalar.activation(chunk_of(cgate, 2 * i + j), chunk_of(cgate, 2 * i + j), ACT.Silu).then_inc(s_cg, 1)

            items_of(act, DC, mla_gate)
            for g in range(2):
                attention_scalar(act, mla[g], lambda m: None)
            act.wait_ge(mla[1].outL, len(mla[1].items))
            act.dma_start(x5[:], a["x_spill_mla"]).then_inc(s_xld5, 16)
            for m in range(DC):
                nc.scalar.activation(y7H[:, m], cgate[:, m], ACT.Copy).then_inc(s_y7h, 1)
            split_x(7, x5, None, 0, updated("wob"))
            norm_rstd(5)

        @block.vector
        def _(dve):
            def low_of(L, source, H):
                return nc.vector.tensor_tensor(L, source, f32(H), ALU.subtract)

            def split_x(q, x, H, L, gain, before=None, after_h=True, squares=True):
                def chunk(i, j):
                    m = 2 * i + j
                    if before:
                        before(i, j)
                    dve.wait_ge(s_h, m + (8 * q + 1))
                    if squares:
                        if isinstance(i, int) and m == 0:
                            last = nc.vector.tensor_copy(acc[:], sq[:, j])
                        else:
                            dve.wait_ge(s_l, m + 8 * q)
                            last = nc.vector.tensor_tensor(acc[:], acc[:], sq[:, j], ALU.add)
                    if H is not None:
                        last = nc.vector.scalar_tensor_tensor(out=chunk_of(L, m), in0=chunk_of(x, m), scalar=vec[:, bass.ds(m + gain, 1)],
                                                              in1=f32(chunk_of(H, m)), op0=ALU.mult, op1=ALU.subtract)
                    last.then_inc(s_l, 1)
                items_of(dve, DC, chunk)

            def norm_rstd(n):
                dve.wait_ge(s_rstd, 2 * n + 2)

            def read(stage, i, j, h, operation):
                dve.wait_ge(s_mm, mm_count(stage, 2 * i + j, h))
                bank = bank_of(stage, j, h)
                operation(ps[:, bank]).then_inc(s_free[bank], 1)

            def scaled(stage, destination, start=0, signal=None):
                def one(i, j):
                    for h in range(2):
                        read(stage, i, j, h, lambda p: nc.vector.tensor_tensor(
                            chunk_of(destination, 2 * i + j)[..., half_of(h)], p, rstd[:, half_of(h)], ALU.mult))
                items_of(dve, STAGE[stage][2], one)

            def add_to(stage, x):
                def one(i, j):
                    for h in range(2):
                        xm = chunk_of(x, 2 * i + j)[..., half_of(h)]
                        read(stage, i, j, h, lambda p: nc.vector.tensor_tensor(xm, p, xm, ALU.add))
                return one

            chain = [0]

            def link(instruction):
                chain[0] += 1
                instruction.then_inc(s_vchain, 1)
                dve.wait_ge(s_vchain, chain[0])

            dve.wait_ge(s_const, 48)
            
            dve.wait_ge(s_ldone, 2)
            e, s_, s2, poly = derived[:, 31:41], derived[:, 41:51], derived[:, 51:61], derived[:, 61:71]
            link(nc.vector.tensor_scalar(s2, e, 2.0, None, ALU.add))
            link(nc.vector.reciprocal(s_, s2))
            link(nc.vector.tensor_tensor(s_, e, s_, ALU.mult))
            link(nc.vector.tensor_tensor(s2, s_, s_, ALU.mult))
            link(nc.vector.tensor_scalar(poly, s2, 1.0 / 15, 1.0 / 13, ALU.mult, ALU.add))
            for k in (11, 9, 7, 5, 3, 1):
                link(nc.vector.tensor_tensor(poly, poly, s2, ALU.mult))
                link(nc.vector.tensor_scalar(poly, poly, 1.0 / k, None, ALU.add))
            link(nc.vector.tensor_tensor(poly, poly, s_, ALU.mult))
            link(nc.vector.tensor_scalar(s2, V(V_LAM, RB), -1.0, 0.0, ALU.mult, ALU.max))
            link(nc.vector.scalar_tensor_tensor(out=s2, in0=poly, scalar=2.0, in1=s2, op0=ALU.mult, op1=ALU.add))
            link(nc.vector.tensor_scalar(derived[:, 1:11], s2, -8.0, None, ALU.mult))
            link(nc.vector.tensor_scalar(derived[:, 11:21], s2, 4.0, None, ALU.mult))
            for c in range(DC):
                link(nc.vector.tensor_scalar(qk_gains[:, c:c + 1], V(V_QN if c < 4 else V_KN), float(HD_B ** -0.5) if c < 4 else 1.0,
                                             None, ALU.mult))

            split_x(0, x1, h1H, h1L, G_MIX)
            norm_rstd(0)

            scaled("zqk", qk_b)
            scaled("zv", v_raw)

            def gate(i, j):
                if not (isinstance(i, int) and i == 0):
                    dve.wait_ge(s_gst[j], i * 16)
                for h in range(2):
                    read("gates", i, j, h, lambda p: nc.vector.tensor_tensor(sq[:, j, half_of(h)], p, rstd[:, half_of(h)], ALU.mult))
                dve.wait_ge(s_free[bank_of("gates", j, 1)], use_of("gates", i, j) + 1)
                dve.nop().then_inc(s_gz, 1)
                if j == 1:
                    dve.wait_ge(s_brstd, 2 * i + 2)
                    nc.vector.scalar_tensor_tensor(out=chunk_of(qk_b, i), in0=chunk_of(qk_b, i), scalar=derived[:, bass.ds(i + 41, 1)],
                                                   in1=acc[:], op0=ALU.mult, op1=ALU.mult).then_inc(s_bn, 1)

            items_of(dve, 16, gate)
            dve.wait_ge(s_bconst, 48)
            for h in range(HEADS_B):
                nc.vector.tensor_scalar(bias[:, h], bias[:, h], V(V_CFAR + h), None, ALU.subtract).then_inc(s_bias, 1)
            dve.wait_ge(s_bias, HEADS_B)
            for h in range(HEADS_B):
                nc.vector.memset(bias[0:64, h, 192:256], NEG).then_inc(s_bias, 1)

            def band_destination(m, o, inverse):
                h, j, _ = band.items[m]
                if h == 0:
                    await_at_least(dve, band.outT, j - 1)
                return nc.vector.tensor_scalar(o_tok[:, j % 2, h * HD_B:(h + 1) * HD_B], o, inverse, None, ALU.mult)

            def band_low(m):
                h, j, _ = band.items[m]
                if h == HEADS_B - 1:
                    dve.wait_ge(band.outH, j + 1)
                    low_of(obL[:, :, j * P:(j + 1) * P], ps[:, 6 + m % 2].rearrange("p (c t) -> p c t", c=4),
                           obH[:, :, j * P:(j + 1) * P]).then_inc(band.outL, 1)

            attention_vector(dve, band, band_destination, band_low)

            for t in range(16):
                w, head = "fgiq"[t // 4], t % 4
                if w == "i" and head == 0:
                    dve.wait_ge(s_hscan, 1)
                if w == "q" and head == 0:
                    dve.wait_ge(s_hk, 4)
                for h in range(2):
                    read("za", t // 2, t % 2, h, lambda p: nc.vector.tensor_tensor(
                        za[w][:, 4 * h:4 * h + 4, head], p.rearrange("p (c t) -> p c t", c=4),
                        rstd[:, half_of(h)].rearrange("p (c t) -> p c t", c=4), ALU.mult))
                if w == "g":
                    part = slice(head * S, (head + 1) * S)
                    dve.wait_ge(s_ha, 9 + head)
                    nc.vector.scalar_tensor_tensor(out=zi[:, part], in0=zf[:, part], scalar=0.0, in1=zq[:, part],
                                                   op0=ALU.min, op1=ALU.subtract).then_inc(s_hp, 1)
                    dve.wait_ge(s_hp, 2 * head + 1)
                    nc.vector.tensor_tensor(zq[:, part], zi[:, part], zf[:, part], ALU.subtract).then_inc(s_hp, 1)
                if t == 7:
                    for n in range(NT * A_HEADS):
                        last = nc.vector.tensor_tensor_scan(out=hb[:, n * P:(n + 1) * P], data0=ones[:], data1=zi[:, n * P:(n + 1) * P],
                                                            initial=0.0, op0=ALU.mult, op1=ALU.add)
                    last.then_inc(s_hscan, 1)
            dve.wait_ge(s_free[bank_of("za", 1, 1)], use_of("za", 7, 1) + 1)
            for n in range(2):
                level_difference(nc.vector, n).then_inc(s_lD0, 1)
            nc.vector.memset(attn[:], 0.0).then_inc(s_hscan, 1)
            dve.wait_ge(s_hscan, 2)
            dve.wait_ge(s_hm, 16)

            def place(m):
                level = 7 if m < 2 else m // 2 - 1
                for k in range(4):
                    c = 4 * (m % 2) + k
                    dve.wait_ge(s_lS, 4 * m + k + 1)
                    nc.vector.copy_predicated(attn[:, c * CH:(c + 1) * CH].rearrange("p (h t) -> p h t", h=A_HEADS),
                                              masks[:, level:level + 1, :].bitcast(mybir.dt.int32).broadcast_to([P, A_HEADS, P]),
                                              ps[:, c].rearrange("p (h t) -> p h t", h=A_HEADS)).then_inc(s_lP, 1)

            def k_to_end(k):
                part = slice(k * 4 * CH, (k + 1) * 4 * CH)
                dve.wait_ge(s_ke, k + 1)
                nc.vector.tensor_tensor(k_end[:, part], k_end[:, part], zf[:, part], ALU.mult).then_inc(s_kd, 1)

            for n in range(14):
                place(n)
                size = LEVELS[n // 2]
                part = slice((n % 2) * 4 * CH, (n % 2 + 1) * 4 * CH)
                two = lambda t: t[:, part].rearrange("p (n two s) -> p n two s", two=2, s=size)
                dve.wait_ge(s_lE, n + 1)
                if n >= 2:
                    dve.wait_ge(s_lS, 4 * n + 4)
                nc.vector.tensor_tensor(two(hqk)[:, :, 1], two(hd)[:, :, 1], two(zq)[:, :, 1], ALU.mult)
                nc.vector.tensor_tensor(two(hqk)[:, :, 0], two(hd)[:, :, 0], two(zf)[:, :, 0], ALU.mult).then_inc(s_lQ, 1)
                if n == 4:
                    k_to_end(0)
            place(14)
            for k in range(2):
                part = slice(k * 4 * CH, (k + 1) * 4 * CH)
                dve.wait_ge(s_eb, k + 1)
                nc.vector.tensor_tensor(hd[:, part], hd[:, part], zq[:, part], ALU.mult).then_inc(s_qe, 1)
                if k == 0:
                    place(15)
            k_to_end(1)
            dve.wait_ge(s_eb, 3)

            def oa_gated(c):
                part = slice(c * CH, (c + 1) * CH)
                dve.wait_ge(s_hrstd, c + 1)
                nc.vector.scalar_tensor_tensor(out=o_h[:, part], in0=o_h[:, part], scalar=V(V_ONORM), in1=o_rstd[:, c % 4],
                                               op0=ALU.mult, op1=ALU.mult).then_inc(s_hw, 1)
                dve.wait_ge(s_hw, c + 1)
                dve.wait_ge(s_hg, 4)
                nc.vector.tensor_tensor(o_h[:, part], o_h[:, part], zg[:, part], ALU.mult).then_inc(s_hout, 1)

            def oa_low(m):
                dve.wait_ge(s_hoh, m + 1)
                low_of(oaL[:, :, m * P:(m + 1) * P], o_h[:, m * CH:(m + 1) * CH].rearrange("p (h t) -> p h t", h=A_HEADS),
                       oaH[:, :, m * P:(m + 1) * P]).then_inc(s_hol, 1)

            for c in range(NT - 1):
                dve.wait_ge(s_hU, c + 1)
                if c == 0:
                    nc.vector.tensor_copy(states[:, 0], ps[:, 6]).then_inc(s_hst, 1)
                else:
                    dve.wait_ge(s_hst, c)
                    dve.wait_ge(s_hO, c)
                    for h in range(A_HEADS):
                        hs = slice(h * P, (h + 1) * P)
                        last = nc.vector.scalar_tensor_tensor(out=states[:, c % 2, hs], in0=states[:, (c - 1) % 2, hs],
                                                              scalar=chunk_decay[:, c * A_HEADS + h:c * A_HEADS + h + 1],
                                                              in1=ps[:, 6 + c % 2, hs], op0=ALU.mult, op1=ALU.add)
                    last.then_inc(s_hst, 1)
                if c in (3, 5):
                    oa_gated(c - 3)
                    oa_gated(c - 2)
                if c == 5:
                    oa_low(0)
                    oa_low(1)
            for c in range(4, NT):
                oa_gated(c)
                oa_low(c - 2)
            for c in range(NT - 2, NT):
                oa_low(c)

            def merge(i, j):
                m = 2 * i + j
                dve.wait_ge(s_gin[j], i * 16 + 16)
                for part in range(2):
                    for h in range(2):
                        dve.wait_ge(s_mm, mm_count("merge", m * 2 + part, h))
                        g = gate_in[:, j, part, half_of(h)]
                        nc.vector.tensor_tensor(g, ps[:, 2 * part + h], g, ALU.mult).then_inc(s_free[2 * part + h], 1)
                dve.wait_ge(s_free[3], m + (STAGE["merge"][1] // 2 + 1))
                nc.vector.tensor_tensor(gate_in[:, j, 0], gate_in[:, j, 0], gate_in[:, j, 1], ALU.add).then_inc(s_mg, 1)
                dve.wait_ge(s_mgh, m + 1)
                low_of(chunk_of(mgL, m), gate_in[:, j, 0], chunk_of(mgH, m)).then_inc(s_mgl, 1)

            items_of(dve, DC, merge)
            dve.wait_ge(s_x2, 16)
            split_x(1, x2, h2H, h2L, G_FFN, add_to("wout", x2))
            norm_rstd(1)
            for g, n in enumerate(FF_GROUPS):
                p0 = sum(FF_GROUPS[:g])
                stage = f"gu{g}"

                def pair(i, j, p0=p0, stage=stage):
                    m = 2 * i + j
                    for part in range(2):
                        for h in range(2):
                            read(stage, m, part, h, lambda p: nc.vector.tensor_tensor(sq[:, part, half_of(h)], p, rstd[:, half_of(h)], ALU.mult))
                    dve.wait_ge(s_silu, m + (p0 + 1))
                    dve.wait_ge(s_free[bank_of(stage, 1, 1)], m + (STAGE[stage][1] // 2 + 1))
                    nc.vector.tensor_tensor(tmp[:], sq[:, 0], sq[:, 1], ALU.mult).then_inc(s_act, 1)
                    dve.wait_ge(s_acth, m + (p0 + 1))
                    low_of(chunk_of(actL, m), tmp[:], chunk_of(actH, m)).then_inc(s_actl, 1)

                items_of(dve, n, pair)
                if g < 2:
                    items_of(dve, DC, add_to(f"dn{g}", x2))
            split_x(2, x2, h2H, h2L, G_PLE, add_to("dn2", x2))
            for c in range(2):
                dve.wait_ge(s_ph, c + 1)
                low_of(pL[:, c], p_in[:, c], pH[:, c]).then_inc(s_pl, 1)
            for t in range(DC):
                for h in range(2):
                    read("proj", t // 2, t % 2, h, lambda p: nc.vector.tensor_copy(proj[:, t, half_of(h)], p))
            norm_rstd(2)

            def ple_add(i, j):
                m = 2 * i + j
                for h in range(2):
                    read("pleg", i, j, h, lambda p: nc.vector.tensor_tensor(tmp[:, half_of(h)], p, rstd[:, half_of(h)], ALU.mult))
                dve.wait_ge(s_sig, m + 1)
                nc.vector.tensor_tensor(tmp[:], tmp[:], chunk_of(proj, m), ALU.mult).then_inc(s_pc, 1)
                dve.wait_ge(s_pc, m + 1)
                nc.vector.tensor_tensor(chunk_of(x2, m), chunk_of(x2, m), tmp[:], ALU.add).then_inc(s_pz, 1)

            split_x(3, x2, h4H, h4L, G_A, ple_add)
            norm_rstd(3)
            dve.wait_ge(s_xs3, 16)

            def project(n, j, destination):
                for h in range(2):
                    read("xg", n, j, h, lambda p: nc.vector.tensor_tensor(
                        chunk_of(destination, n)[..., half_of(h)], p, rstd[:, half_of(h)], ALU.mult))

            def recurrence(n):
                dve.wait_ge(s_rs, n + 1)
                nc.vector.scalar_tensor_tensor(out=r_buf[:], in0=chunk_of(xb, n), scalar=1.0, in1=r_buf[:],
                                               op0=ALU.add, op1=ALU.mult).then_inc(s_rw, 1)
                dve.wait_ge(s_rw, 3 * n + 1)
                nc.vector.tensor_tensor(i_buf[:], i_buf[:], r_buf[:], ALU.mult).then_inc(s_rw, 1)
                dve.wait_ge(s_rw, 3 * n + 2)
                nc.vector.tensor_tensor_scan(out=r_buf[:], data0=xb[:].rearrange("p c t -> p (c t)")[:, bass.ds(n * S, S)], data1=i_buf[:], initial=0.0,
                                             op0=ALU.mult, op1=ALU.add).then_inc(s_rw, 1)
                dve.wait_ge(s_rw, 3 * n + 3)
                dve.wait_ge(s_rg, n + 1)
                nc.vector.tensor_tensor(chunk_of(rgate, n), r_buf[:], chunk_of(rgate, n), ALU.mult).then_inc(s_yg, 1)

            def y_low(n):
                dve.wait_ge(s_yh, n + 1)
                low_of(chunk_of(yL, n), chunk_of(rgate, n), chunk_of(yH, n)).then_inc(s_yl, 1)

            def rnn_block(n):
                first = isinstance(n, int)
                w = lambda k: vec[:, bass.ds(4 * n + (V_CW + k), 1)]
                project(n, 0, xb)
                dve.wait_ge(s_free[bank_of("xg", 0, 1)], use_of("xg", n, 0) + 1)
                await_at_least(dve, s_ix, n)
                x = chunk_of(xb, n)
                nc.vector.tensor_scalar(conv[:], x, w(3), vec[:, bass.ds(n + V_CB, 1)], ALU.mult, ALU.add).then_inc(s_cv, 1)
                for k in (1, 2, 3):
                    dve.wait_ge(s_cv, 4 * n + k)
                    nc.vector.scalar_tensor_tensor(out=conv[:, k:], in0=x[..., 0:S - k], scalar=w(3 - k), in1=conv[:, k:],
                                                   op0=ALU.mult, op1=ALU.add).then_inc(s_cv, 1)
                dve.wait_ge(s_wrh, n + 1)
                low_of(w_riL[:], w_ri[:, n] if first else w_ri[:, bass.ds(n, 1)], w_riH[:]).then_inc(s_wrl, 1)
                dve.wait_ge(s_ch, n + 1)
                low_of(convL[:], conv[:], convH[:]).then_inc(s_cl, 1)
                if not first:
                    recurrence(n - 1)
                project(n, 1, rgate)
                if not first:
                    y_low(n - 1)
                dve.wait_ge(s_sg, 2 * n + 2)
                nc.vector.tensor_tensor(i_buf[:], i_buf[:], conv[:], ALU.mult).then_inc(s_ix, 1)

            rnn_block(0)
            with dve.Fori(1, RB) as n:
                rnn_block(n)
            dve.wait_ge(s_ix, RB)
            recurrence(RB - 1)
            y_low(RB - 1)
            dve.wait_ge(s_xld4, 16)
            items_of(dve, DC, add_to("wo1", x4))
            split_x(4, x4, None, None, 0, add_to("wo2", x4))
            split_x(5, x4, h5H, h5L, G_KV, squares=False)
            norm_rstd(4)
            split_x(6, x4, h6H, h6L, G_B, squares=False)
            for t in range(3):
                for h in range(2):
                    dst = ckv[:, t, half_of(h)] if t < 2 else tmp[:, half_of(h)]
                    read("dkv", t // 2, t % 2, h, lambda p: nc.vector.tensor_tensor(dst, p, rstd[:, half_of(h)], ALU.mult))
            for t in range(3):
                for h in range(2):
                    dst = cq[:, t, half_of(h)]
                    dve.wait_ge(s_mm, mm_count("cq", t, h))
                    bank = bank_of("cq", t, h)
                    nc.vector.tensor_tensor(dst, ps[:, bank], rstd[:, half_of(h)], ALU.mult).then_inc(s_free[bank], 1)
            for k, (chunks, src, H, L, gain) in enumerate(((2, ckv, ckvH, ckvL, V_KVN), (3, cq, cqH, cqL, V_CQN))):
                dve.wait_ge(s_crstd, 2 * k + 2)
                for c in range(chunks):
                    nc.vector.scalar_tensor_tensor(out=src[:, c], in0=src[:, c], scalar=V(gain + c), in1=acc[:],
                                                   op0=ALU.mult, op1=ALU.mult).then_inc(s_cw, 1)
                for c in range(chunks):
                    dve.wait_ge(s_cwh, 2 * k + c + 1)
                    low_of(L[:, c], src[:, c], H[:, c]).then_inc(s_cwl, 1)
            dve.wait_ge(s_xs5, 16)
            scaled("cgate", cgate)
            for h in range(2):
                dve.wait_ge(s_rot, h + 1)
                nc.vector.tensor_tensor(sq[:, 0, half_of(h)], ps[:, 6 + h], cos_sin[:, 1, half_of(h)], ALU.mult).then_inc(s_kr, 1)
            nc.vector.tensor_tensor(k_rope[:], tmp[:], cos_sin[:, 0], ALU.mult).then_inc(s_kr, 1)
            dve.wait_ge(s_kr, 3)
            nc.vector.tensor_tensor(k_rope[:], k_rope[:], sq[:, 0], ALU.add).then_inc(s_kr, 1)
            for t in range(DC):
                for h in range(2):
                    read("uk", t // 2, t % 2, h, lambda p: nc.vector.tensor_copy(k_nope[:, t, half_of(h)], p))
            for t in range(DC):
                v, r = t // 4, t % 4
                for h in range(2):
                    read("uv", t // 2, t % 2, h, lambda p: nc.vector.tensor_copy(v_mla[:, 2 * r + h, v * HALF:(v + 1) * HALF], p))
            for g in range(2):
                at_ = mla[g]
                for t in range(6):
                    dst = q_nope[:, t] if t < 4 else q_rope[:, t - 4]
                    for h in range(2):
                        read(f"uq{g}", t // 2, t % 2, h, lambda p: nc.vector.tensor_copy(dst[:, half_of(h)], p))
                last_bank = bank_of(f"uq{g}", 1, 1)
                dve.wait_ge(s_free[last_bank], use_of(f"uq{g}", 2, 1) + 1)
                dve.nop().then_inc(s_rq, 1)
                for n in range(4):
                    t, h = n // 2, n % 2
                    x = q_rope[:, t, half_of(h)]
                    dve.wait_ge(s_rotq, 4 * g + n + 1)
                    nc.vector.tensor_tensor(sq[:, 0, half_of(h)], ps[:, 4 + n % 2], cos_sin[:, 1, half_of(h)], ALU.mult).then_inc(s_rqe, 1)
                    nc.vector.tensor_tensor(x, x, cos_sin[:, 0, half_of(h)], ALU.mult).then_inc(s_rqe, 1)
                    dve.wait_ge(s_rqe, 8 * g + 2 * n + 2)
                    nc.vector.tensor_tensor(x, x, sq[:, 0, half_of(h)], ALU.add).then_inc(s_qready, 1)
                if g == 0:
                    dve.wait_ge(s_cg, DC)

                def mla_destination(m, o, inverse):
                    await_at_least(dve, at_.outT, m - 1)
                    return nc.vector.tensor_scalar(o_mla[:, m % 2], o, inverse, None, ALU.mult)

                def mla_gated(m):
                    h, j, _ = at_.items[m]
                    dve.wait_ge(at_.outT, m + 1)
                    y = cgate[:, h, j * P:(j + 1) * P]
                    nc.vector.tensor_tensor(y, ps[:, 6 + m % 2, 0:P], y, ALU.mult).then_inc(at_.outL, 1)

                attention_vector(dve, at_, mla_destination, mla_gated)
            for m in range(DC):
                dve.wait_ge(s_y7h, m + 1)
                low_of(y7L[:, m], cgate[:, m], y7H[:, m]).then_inc(s_y7l, 1)
            dve.wait_ge(s_xld5, 16)
            split_x(7, x5, None, None, 0, add_to("wob", x5))
            norm_rstd(5)
            for m in range(DC):
                nc.vector.scalar_tensor_tensor(out=out_sb[:, m], in0=x5[:, m], scalar=V(G_FIN + m), in1=rstd[:],
                                               op0=ALU.mult, op1=ALU.mult).then_inc(s_fin, 1)


def _feature_major(x):
    return np.ascontiguousarray(x.T.reshape(-1, P, x.shape[0]).transpose(1, 0, 2))


def _unit(w):
    u = w.reshape(-1, P, w.shape[1]).transpose(1, 0, 2).reshape(P, -1)
    return np.concatenate([u, np.zeros((P, 1024 - u.shape[1]), np.float32)], axis=1)


def _stream(x):
    col = lambda w, t, n=P: w[:, t * n:(t + 1) * n]
    w_in, wa, wb = x["w_in"][0], x["w_branch_a"][0], x["w_branch_b"][0]
    units = [_unit(col(w_in, t)) for t in list(range(16, 44)) + list(range(4, 8)) + list(range(12, 16)) + list(range(8, 12)) + list(range(4))]
    units += [_unit(np.concatenate([col(wa, m), col(wb, m)])) for m in range(DC)]
    units += [_unit(col(x["w_out"][0], m)) for m in range(DC)]
    f0 = 0
    for n in FF_GROUPS:
        for f in range(f0, f0 + n):
            units += [_unit(col(x["w_ffn_gate"][0], f)), _unit(col(x["w_ffn_up"][0], f))]
        units += [_unit(col(x["w_ffn_down"][0], m)[f0 * P:(f0 + n) * P]) for m in range(DC)]
        f0 += n
    units += [_unit(col(x["w_ple_proj"][0], v, 512)) for v in range(2)]
    units += [_unit(col(x["w_ple_gate"][0], m)) for m in range(DC)]
    units += [_unit(col(x["w_in_a_2"][0], part * RB + n)) for n in range(RB) for part in range(2)]
    for k in range(2):
        units += [_unit(col(x["w_out_a_2"][0], m)[k * 640:(k + 1) * 640]) for m in range(DC)]
    dkv, wb_ = x["w_dkv_2"], x["w_in_b_2"][0]
    units += [_unit(dkv[:, 0:P]), _unit(dkv[:, P:2 * P]), _unit(np.concatenate([dkv[:, 256:320]] * 2, axis=1))]
    units += [_unit(col(wb_, m)) for m in range(11)]
    units += [_unit(col(x["w_uk_2"].reshape(256, 1024), v, 512)) for v in range(2)]
    units += [_unit(col(x["w_uv_2"].reshape(256, 1024), v, 512)) for v in range(2)]
    uq = x["w_uq_2"][0]
    for g in range(2):
        for h in (4 * g, 4 * g + 2):
            units.append(_unit(uq[:, h:h + 2, 0:P].reshape(384, 256)))
        units.append(_unit(uq[:, 4 * g:4 * g + 4, P:].reshape(384, 256)))
    units += [_unit(col(x["w_out_b_2"][0], m)) for m in range(DC)]
    assert len(units) == UNITS
    return np.stack(units)


def _vectors(x):
    cols = lambda v: v.reshape(-1, P).T
    twice = lambda v: np.concatenate([v, v])[:, None]
    parts = [cols(x[n].reshape(-1)) for n in ("norm_mix_g", "norm_ffn_g", "norm_ple_g", "norm_a_2", "norm_kv_2", "norm_b_2", "final_norm_2")]
    parts += [cols(x["hgrn_onorm_g"][0]), twice(x["attn_qnorm_g"][0]), twice(x["attn_knorm_g"][0])]
    parts += [cols(x[n][0]) for n in ("conv_b_2", "lru_lambda_2", "b_rg_2", "b_ig_2")]
    parts.append(x["conv_w_2"][0].reshape(4, RB, P).transpose(2, 1, 0).reshape(P, 4 * RB))
    parts += [cols(x["kv_norm_2"]), cols(x["q_norm_2"][0]), np.full((P, 1), EPS, np.float32)]
    parts.append(np.broadcast_to(x["attn_rel_bias"][0, :, 256], (P, HEADS_B)))
    parts.append(np.ones((P, 1), np.float32))
    return np.ascontiguousarray(np.concatenate(parts, axis=1))


def _constants():
    i = np.arange(P)
    s, t = i[:, None], i[None, :]
    levels = [(s // (2 * n) == t // (2 * n)) & (s % (2 * n) < n) & (t % (2 * n) >= n) for n in LEVELS] + [s == t]
    rotate = np.zeros((P, P), np.float32)
    for b in (0, 64):
        for k in range(32):
            rotate[b + 32 + k, b + k] = -1.0
            rotate[b + k, b + 32 + k] = 1.0
    inv = np.float32(10000.0) ** (-np.arange(0, 64, 2, dtype=np.float32) / np.float32(64))
    angle = np.arange(S, dtype=np.float32)[None, :] * inv[i % 32][:, None]
    return {
        "identity": np.eye(P, dtype=np.float32),
        "ones": np.ones((P, P), np.float32),
        "head_ones": (s // 64 == t // 64).astype(np.float32),
        "far_mask": np.ascontiguousarray(np.broadcast_to(np.where(s >= 64, np.float32(NEG), np.float32(0)), (P, 64))),
        "masks": np.ascontiguousarray(np.stack(levels, axis=1).astype(np.float32)),
        "rotate": rotate,
        "causal": np.where(t > s, np.float32(NEG), np.float32(0)),
        "cos_sin": np.ascontiguousarray(np.stack([np.cos(angle), np.sin(angle)], axis=1).astype(np.float32)),
    }


def _arrays(x):
    t, k = np.arange(P)[:, None], np.arange(256)[None, :]
    arrays = {
        "xT": _feature_major(x["x"][0]),
        "pT": _feature_major(x["p"][0, 0]),
        "weights": _stream(x),
        "vectors": _vectors(x),
        "rnn_gate_weights": np.ascontiguousarray(np.concatenate([x["w_rg_2"][0], x["w_ig_2"][0]], axis=2).transpose(1, 0, 2)),
        "bias": np.ascontiguousarray(x["attn_rel_bias"][0][:, np.clip(t + P - k, -128, 128) + 128].transpose(1, 0, 2)),
    }
    arrays.update(_constants())
    return arrays


def _build(nc, arrays):
    aps = {}
    for name, v in arrays.items():
        aps[name] = nc.dram_tensor(name + "_in", v.shape, mybir.dt.from_np(v.dtype), kind="ExternalInput").ap()
    for name, shape in (("gates", (16, P, S)), ("x_spill_rnn", (P, DC, S)), ("x_spill_mla", (P, DC, S))):
        aps[name] = nc.dram_tensor(name, shape, F32, kind="Internal").ap()
    aps["outT"] = nc.dram_tensor("outT", (P, DC, S), F32, kind="ExternalOutput").ap()
    fused_kernel(nc, aps)


def kernel(**inputs):
    import concourse.bacc as bacc
    from concourse.bass_utils import run_bass_kernel_spmd

    arrays = _arrays({name: np.asarray(v) for name, v in inputs.items()})
    nc = bacc.Bacc("TRN2", target_bir_lowering=False, num_devices=1)
    _build(nc, arrays)
    r = run_bass_kernel_spmd(nc, [{name + "_in": v for name, v in arrays.items()}], core_ids=[0])
    out = np.asarray(r.results[0]["outT"])
    return np.ascontiguousarray(out.transpose(1, 0, 2).reshape(D, S).T)[None]
```

```python
import numpy as np
from contextlib import ExitStack
import concourse.bass as bass
from concourse import mybir

F32 = mybir.dt.float32
F32R = mybir.dt.float32r
ACT = mybir.ActivationFunctionType
ALU = mybir.AluOpType
AX = mybir.AxisListType

P = 128
D = 1024
S = 1024
HALF = 512
EPS = 1e-6
DC = D // P
A_HEADS = 4
HEADS_B = 8
HD_B = 64
D_FF = 2816
FF_GROUPS = (8, 8, 6)
RNN = 1280
RB = RNN // P
HEADS_C = 8
SCALE_C = float((128 + 64) ** -0.5)
NEG = -1e30
LEVELS = (64, 32, 16, 8, 4, 2, 1)
NT = S // P

G_MIX, G_FFN, G_PLE, G_A, G_KV, G_B, G_FIN = 0, 8, 16, 24, 32, 40, 48
V_ONORM, V_QN, V_KN = 56, 57, 58
V_CB, V_LAM, V_BR, V_BI, V_CW = 59, 69, 79, 89, 99
V_KVN, V_CQN, V_EPS, V_CFAR, V_ONE = 139, 141, 144, 145, 153
NVEC = 154

STREAM = [
    ("zqk", 8, 1, 8), ("zv", 4, 1, 8), ("gates", 16, 1, 8), ("za", 16, 1, 8), ("merge", 8, 2, 4), ("wout", 8, 1, 8),
    ("gu0", 16, 1, 8), ("dn0", 8, 1, 8), ("gu1", 16, 1, 8), ("dn1", 8, 1, 8), ("gu2", 12, 1, 8), ("dn2", 8, 1, 6),
    ("proj", 2, 4, 2), ("pleg", 8, 1, 8), ("xg", 2 * RB, 1, 8),
    ("wo1", 8, 1, 5), ("wo2", 8, 1, 5), ("dkv", 3, 1, 8), ("cq", 3, 1, 8), ("cgate", 8, 1, 8),
    ("uk", 2, 4, 2), ("uv", 2, 4, 2), ("uq0", 3, 2, 3), ("uq1", 3, 2, 3), ("wob", 8, 1, 8),
]
STAGE = {}
_u = _t = 0
for _name, _n, _T, _C in STREAM:
    STAGE[_name] = (_u, _t, _n, _T, _C)
    _u += _n
    _t += _n * _T
UNITS = _u
MM_PER_UNIT = 16


def half_of(h):
    return slice(h * HALF, (h + 1) * HALF)


def items_of(eng, n, body, start=0):
    first = start // 2
    for j in range(min(2, n)):
        body(first, j)
    pairs = n // 2
    if pairs == first + 2:
        for j in range(2):
            body(first + 1, j)
    elif pairs > first + 2:
        with eng.Fori(first + 1, pairs) as i:
            for j in range(2):
                body(i, j)
    if n % 2 and n > 2:
        body(n // 2, 0)


def chunk_of(t, m):
    return t[:, m] if isinstance(m, int) else t[:, bass.ds(m, 1)]


def await_at_least(eng, semaphore, count):
    if not isinstance(count, int) or count > 0:
        eng.wait_ge(semaphore, count)


def fused_kernel(nc, a):
    ctx = ExitStack()
    with ctx:
        def sem(name):
            return ctx.enter_context(nc.semaphore(name))

        BASE = (nc.sbuf_base + 31) // 32 * 32
        REG = 32768

        def at(name, shape, off, dt=F32):
            return nc.alloc_sbuf_tensor_at(name, shape, dt, offset=BASE + off)

        def R(r, kib=0):
            return r * REG + kib * 1024

        RING = R(5)
        w_staged = at("w_staged", [P, 2, 1024], RING)
        w_high = at("w_high", [P, 2, 1024], RING + 8192, F32R)
        w_low = at("w_low", [P, 2, 1024], RING + 16384, F32R)
        MISC = RING + 24576
        rstd = at("rstd", [P, S], MISC)
        sq = at("squares", [P, 2, S], MISC + 4096)
        acc = at("square_sum", [P, S], MISC + 12288)
        tmp = at("tmp", [P, S], MISC + 16384)
        ident = at("identity", [P, P], MISC + 20480)
        ones = at("ones", [P, P], MISC + 20992)
        vec = at("vectors", [P, NVEC], MISC + 21504)
        derived = at("derived_vectors", [P, 80], MISC + 21504 + 640)
        stat = at("softmax_stats", [P, 16], MISC + 21504 + 960)

        def V(c, n=1):
            return vec[:, c:c + n]

        eps = V(V_EPS)
        qk_gains = derived[:, 41:49]

        def full(name, region, dt=F32, kib=0, chunks=8):
            return at(name, [P, chunks, S], R(region, kib), dt)

        def f32(t):
            return t.bitcast(F32)

        ps = ctx.enter_context(nc.psum_tensor("ps", [P, 8, HALF], F32))

        x1 = full("x_in", 0)
        h1H, h1L = full("h_mix_high", 3, F32R), full("h_mix_low", 2, F32R)
        qk_b, v_raw = full("z_band_qk", 1), full("z_band_v", 4, chunks=4)
        v_tok = at("v_band_by_token", [P, NT, HEADS_B * HD_B], R(4, 16))
        bias = at("band_bias", [P, HEADS_B, 256], R(4, 0))
        biasL, biasH = [at(f"band_bias_{n}", [P, HEADS_B, 256], R(4, k), F32R) for n, k in (("low", 0), ("high", 8))]
        o_tok = [at(f"o_band_by_token{k}", [P, HEADS_B * HD_B], MISC + off) for k, off in enumerate((9216, 17408))]
        head_ones = at("head_ones", [P, P], MISC + 22528)
        far_mask = at("far_mask", [P, 64], MISC + 23040)
        ident_r = at("identity_r", [P, P], MISC + 23424, F32R)
        far_mask_r = at("far_mask_r", [P, 64], MISC + 23936, F32R)
        probs_b = at("probs_band", [P, 2, 640], MISC + 12288)
        probsT_b = at("probs_band_T", [P, 2, 640], MISC + 4096)
        obH, obL = full("o_band_high", 0, F32R, 0, 4), full("o_band_low", 0, F32R, 16, 4)
        CH = A_HEADS * P
        z_qf, z_ig = [at(f"z_hgrn_{n}", [P, 2, NT, A_HEADS, P], R(r)) for n, r in (("qf", 1), ("ig", 4))]
        za = {"q": z_qf[:, 0], "f": z_qf[:, 1], "i": z_ig[:, 0], "g": z_ig[:, 1]}
        zq, zf, zi, zg = [za[w].rearrange("p c h t -> p (c h t)") for w in "qfig"]
        hb = at("hgrn_log_decay", [P, NT * CH], MISC + 4096)
        k_end = at("hgrn_k_to_end", [P, NT * CH], R(3))
        attn = at("hgrn_attn", [P, NT * CH], R(3, 16))
        hd = at("hgrn_decays", [P, NT * CH], R(2))
        hqk = at("hgrn_decayed_qk", [P, NT * CH], R(2, 16))
        masks = at("level_masks", [P, 8, P], MISC)
        states = at("hgrn_state", [P, 2, CH], MISC + 4096)
        o_sq = at("hgrn_o_squares", [P, 2, CH], MISC + 8192)
        o_rstd = at("hgrn_o_rstd", [P, 4, CH], MISC + 12288)
        chunk_decay = at("hgrn_chunk_decay", [P, NT * A_HEADS], MISC + 23296)
        o_h = at("hgrn_o", [P, NT * CH], R(2, 16))
        oaH, oaL = full("o_hgrn_high", 1, F32R, 0, 4), full("o_hgrn_low", 1, F32R, 16, 4)
        mgH, mgL = full("merged_high", 3, F32R), full("merged_low", 4, F32R)
        gate_in = at("gates_loaded", [P, 2, 2, S], MISC + 4096)
        x2 = full("x_mid", 2)
        h2H, h2L = full("h_ffn_high", 0, F32R), full("h_ffn_low", 1, F32R)
        actH, actL = full("act_high", 3, F32R), full("act_low", 4, F32R)
        proj = full("ple_proj", 3)
        p_in = full("p_in", 4, F32, 24, 2)
        pH, pL = full("p_high", 3, F32R, 24, 2), full("p_low", 4, F32R, 24, 2)
        h4H, h4L = full("h_rnn_high", 3, F32R), full("h_rnn_low", 4, F32R)
        xb = full("rnn_in", 0, F32, 0, RB)
        rgate = full("rnn_gate", 1, F32, 8, RB)
        yH, yL = full("rnn_y_high", 0, F32R, 0, RB), full("rnn_y_low", 1, F32R, 8, RB)
        conv = at("rnn_conv", [P, S], MISC + 4096)
        convH, convL = at("rnn_conv_high", [P, S], MISC + 8192, F32R), at("rnn_conv_low", [P, S], R(2, 16), F32R)
        r_buf = at("rnn_r", [P, S], MISC + 12288)
        i_buf = at("rnn_i", [P, S], MISC + 16384)
        w_ri = at("rnn_gate_weights", [P, RB, 2 * P], R(2, 20))
        w_riH, w_riL = [at(f"rnn_gate_weights_{n}", [P, 2 * P], R(2, k), F32R) for n, k in (("high", 30), ("low", 31))]
        x4 = full("x_late", 3)
        h5H, h5L = full("h_kv_high", 1, F32R), full("h_kv_low", 2, F32R)
        h6H, h6L = full("h_mla_high", 0, F32R), full("h_mla_low", 4, F32R)
        ckv = sq
        ckvH, ckvL = full("ckv_high", 2, F32R, 0, 2), full("ckv_low", 2, F32R, 8, 2)
        cq = full("cq", 2, F32, 16, 3)
        cqH, cqL = full("cq_high", 1, F32R, 0, 3), full("cq_low", 1, F32R, 12, 3)
        k_rope = at("k_rope", [P, S], R(1, 24))
        rotate = at("rope_rotate", [P, P], R(1, 28))
        causal = at("causal_mask", [P, P], R(1, 28) + 512)
        causal_r = at("causal_mask_r", [P, P], R(1, 30), F32R)
        o_mla = at("o_mla_by_token", [P, 2, P], R(1, 28) + 1024)
        cos_sin = at("cos_sin", [P, 2, S], R(2, 24))
        cgate = full("mla_gate", 3)
        k_nope = full("k_nope", 0)
        v_mla = full("v_mla", 4)
        q_nope = full("q_nope", 2, F32, 0, 4)
        q_rope = full("q_rope", 2, F32, 16, 2)
        probs_c = at("probs_mla", [P, 2, S], MISC + 4096)
        probsT_c = at("probs_mla_T", [P, 2, S], MISC + 12288)
        y7H, y7L = full("y_mla_high", 0, F32R), full("y_mla_low", 4, F32R)
        x5 = full("x_last", 1)
        out_sb = full("x_out", 2)

        s_load = [sem(f"unit_loaded{j}") for j in range(2)]
        s_split = sem("unit_split")
        s_mm = sem("tile_done")
        s_free = [sem(f"bank{b}_read") for b in range(4)]
        s_const = sem("constants_loaded")
        s_x = [sem(f"x_loaded{k}") for k in range(4)]
        s_h = sem("chunk_high")
        s_l = sem("chunk_low")
        s_nsum = sem("norm_summed")
        s_ln, s_rstd = sem("logarithm"), sem("norm_rstd")
        s_sq0, s_sum0 = sem("first_squares"), sem("first_squares_summed")
        s_ldone, s_vchain = sem("derived_constants"), sem("vector_chain")
        s_wh = sem("unit_high")
        s_gz, s_gs = sem("gate_scaled"), sem("gate_sigmoid")
        s_gst = [sem(f"gate_stored{j}") for j in range(2)]
        s_bsq, s_bsum, s_bln, s_brstd, s_bn = [sem(f"head_norm_{n}") for n in ("square", "sum", "ln", "rstd", "done")]
        s_vT, s_vt = sem("v_transposed"), sem("v_by_token")
        s_bconst, s_bias, s_biasH, s_biasL = sem("band_constants"), sem("bias_masked"), sem("bias_high"), sem("bias_low")
        s_bandH = sem("band_o_high")
        s_hg, s_ha, s_hp, s_hk, s_hscan = sem("hgrn_gate_silu"), sem("hgrn_softplus"), sem("hgrn_logf"), sem("hgrn_k"), sem("hgrn_scan")
        s_lD0, s_lD, s_lE, s_lQ, s_lS, s_lP = [sem(f"level_{n}") for n in ("first_difference", "difference", "decay", "qk", "scores", "placed")]
        s_hm = sem("level_masks_loaded")
        s_eb, s_qe, s_kb, s_ke, s_kd = [sem(f"state_{n}") for n in ("exp_b", "q", "k_difference", "exp_k", "k")]
        s_iT, s_iTe = sem("values_transposed"), sem("values_by_token")
        s_hT, s_hTe = sem("keys_transposed"), sem("keys_by_token")
        s_hU, s_hst, s_hO, s_hOe = sem("state_update"), sem("state_new"), sem("hgrn_o"), sem("hgrn_o_read")
        s_h2, s_hn, s_hrstd, s_hw = sem("o_squared"), sem("o_summed"), sem("o_rstd"), sem("o_normed")
        s_hout, s_hoh, s_hol = sem("o_gated"), sem("o_high"), sem("o_low")
        s_gin = [sem(f"gates_in{j}") for j in range(2)]
        s_mg, s_mgh, s_mgl = sem("merged"), sem("merged_high"), sem("merged_low")
        s_x2 = sem("x_mid_loaded_then_p")
        s_silu, s_act, s_acth, s_actl = sem("silu"), sem("act"), sem("act_high"), sem("act_low")
        s_ph, s_pl, s_sig, s_pc, s_pz = [sem(f"ple_{n}") for n in ("high", "low", "sigmoid", "product", "added")]
        s_xs3 = sem("x_spilled")
        s_rg, s_cv, s_ch, s_cl = sem("rnn_gate_silu"), sem("conv_chain"), sem("conv_high"), sem("conv_low")
        s_wri, s_wrh, s_wrl = sem("gate_weights_loaded"), sem("gate_weights_high"), sem("gate_weights_low")
        s_ri, s_sg, s_ix, s_a, s_T, s_rs, s_rw = [sem(f"rnn_{n}") for n in ("products", "sigmoid", "ix", "a", "tanh", "sqrt", "chain")]
        s_yg, s_yh, s_yl = sem("rnn_y"), sem("rnn_y_high"), sem("rnn_y_low")
        s_xs5, s_xld5, s_cconst = sem("x_spilled_2"), sem("x_reloaded_2"), sem("mla_constants")
        s_c2, s_cs, s_crstd, s_cw, s_cwh, s_cwl = [sem(f"latent_{n}") for n in ("square", "sum", "rstd", "chain", "high", "low")]
        s_rot, s_kr, s_cg = sem("k_rotated"), sem("k_rope_chain"), sem("mla_gate_silu")
        s_rq, s_rotq, s_rqe, s_qready = [sem(f"q_rope_{n}") for n in ("raw", "rotated", "chain", "ready")]
        s_y7h, s_y7l = sem("mla_y_high"), sem("mla_y_low")
        s_out, s_fin = sem("out_stored"), sem("out_ready")

        block = ctx.enter_context(nc.Block())

        def base(stage):
            u0, t0, n, T, C = STAGE[stage]
            return u0, t0, n * T, MM_PER_UNIT // (2 * T)

        def mm_count(stage, item, h):
            u0, _, _, inc = base(stage)
            return item * (2 * inc) + (MM_PER_UNIT * u0 + inc * (h + 1))

        def bank_of(stage, j, h):
            return 2 * ((STAGE[stage][1] + j) % 2) + h

        def use_of(stage, i, j):
            return i + (STAGE[stage][1] + j) // 2

        def level_difference(engine, n):
            size = LEVELS[n // 2]
            part = slice((n % 2) * 4 * CH, (n % 2 + 1) * 4 * CH)
            b_ = hb[:, part].rearrange("p (n w) -> p n w", w=2 * size)
            return engine.tensor_tensor(hd[:, part].rearrange("p (n w) -> p n w", w=2 * size), b_,
                                        b_[:, :, size - 1:size].broadcast_to([P, 4 * CH // (2 * size), 2 * size]), ALU.subtract)

        @block.sync
        def _(sp):
            def load(i, j):
                u = 2 * i + j
                await_at_least(sp, s_split, u - 1)
                sp.dma_start(w_staged[:, j], a["weights"][bass.ds(u, 1)].rearrange("u p n -> p (u n)")).then_inc(s_load[j], 16)

            load(0, 0)
            for k in range(4):
                sp.dma_start(x1[:, 2 * k:2 * k + 2], a["xT"][:, 2 * k:2 * k + 2]).then_inc(s_x[k], 16)
            load(0, 1)
            items_of(sp, UNITS, load, 2)
            for h in range(4):
                sp.wait_ge(s_fin, 2 * (h + 1))
                sp.dma_start(a["outT"][:, 2 * h:2 * h + 2], out_sb[:, 2 * h:2 * h + 2]).then_inc(s_out, 16)
            sp.wait_ge(s_out, 4 * 16)

        @block.gpsimd
        def _(pool):
            def split(i, j):
                u = 2 * i + j
                pool.wait_ge(s_load[j], (i + 1) * 16)
                if not (isinstance(i, int) and i == 0):
                    pool.wait_ge(s_mm, (u - 1) * MM_PER_UNIT)
                nc.gpsimd.tensor_tensor(derived[0:1, 72:73], w_staged[0:1, j, 0:1], w_staged[0:1, j, 0:1], ALU.add)
                nc.gpsimd.tensor_copy(w_high[:, j], w_staged[:, j]).then_inc(s_wh, 1)
                pool.wait_ge(s_wh, u + 1)
                nc.gpsimd.tensor_tensor(w_low[:, j], w_staged[:, j], f32(w_high[:, j]), ALU.subtract).then_inc(s_split, 1)

            merge0 = STAGE["merge"][0]
            items_of(pool, merge0, split)

            def to_end(k):
                part = slice(k * 4 * CH, (k + 1) * 4 * CH)
                bk = hb[:, part].rearrange("p (n t) -> p n t", t=P)
                nc.gpsimd.tensor_tensor(k_end[:, part].rearrange("p (n t) -> p n t", t=P), bk,
                                        bk[:, :, P - 1:P].broadcast_to([P, 4 * A_HEADS, P]), ALU.subtract).then_inc(s_kb, 1)

            pool.wait_ge(s_hscan, 1)
            pool.wait_ge(s_mm, mm_count("za", 15, 1))
            to_end(0)
            for n in range(2, 14):
                pool.wait_ge(s_lQ, n - 1)
                level_difference(nc.gpsimd, n).then_inc(s_lD, 1)
            to_end(1)
            items_of(pool, UNITS, split, merge0)

        class Attention:
            def __init__(self, name, items, width, scale, probs, probsT):
                self.items, self.width, self.scale, self.probs, self.probsT = items, width, scale, probs, probsT
                (self.scored, self.maxed, self.negated, self.probed, self.transposed, self.copied, self.summed,
                 self.inverted, self.out, self.outT, self.outL) = [
                    sem(f"{name}_{n}") for n in ("scores", "max", "neg_max", "probs", "probs_T", "probs_T_copied",
                                                 "o", "inverse", "o_by_token", "o_T", "o_stored")]

            def scores_of(self, n):
                b = 2 * (n % 2)
                return ps[:, b:b + 2].rearrange("p b n -> p (b n)")[:, 0:self.items[n][2] * P]

        transposed_flat = ps[:, 4:6].rearrange("p b n -> p (b n)")

        def attention_tensor(pe, at_, scores, values, deferred, bank_free, between=None):
            N = len(at_.items)

            def emit_scores(n):
                await_at_least(pe, at_.probed, n - 1)
                scores(n, 2 * (n % 2)).then_inc(at_.scored, 1)

            emit_scores(0)
            if between:
                between()
            emit_scores(1)
            for n, (h, j, nk) in enumerate(at_.items):
                pe.wait_ge(at_.probed, n + 1)
                await_at_least(pe, at_.copied, n)
                for k in range(nk):
                    last = nc.tensor.transpose(transposed_flat[:, k * P:(k + 1) * P],
                                               at_.probs[:, n % 2, k * P:(k + 1) * P], ident[:])
                last.then_inc(at_.transposed, 1)
                if n + 2 < N:
                    emit_scores(n + 2)
                pe.wait_ge(at_.copied, n + 1)
                await_at_least(pe, at_.out, n - 1)
                if n >= 2:
                    bank_free(n - 2)
                for k in range(nk):
                    last = nc.tensor.matmul(ps[:, 6 + n % 2, 0:at_.width],
                                            at_.probsT[:, n % 2, k * P:(k + 1) * P], values(n, k),
                                            start=(k == 0), stop=(k == nk - 1))
                last.then_inc(at_.summed, 1)
                if n >= 1:
                    deferred(n - 1)
            deferred(N - 1)

        def attention_scalar(act, at_, deferred, between=None):
            N = len(at_.items)
            for n, (h, j, nk) in enumerate(at_.items):
                q = n % 4
                act.wait_ge(at_.negated, n + 1)
                await_at_least(act, at_.transposed, n - 1)
                nc.scalar.activation(at_.probs[:, n % 2, 0:nk * P], at_.scores_of(n), ACT.Exp,
                                     bias=stat[:, 4 + q:5 + q], scale=at_.scale,
                                     accum_out=stat[:, 8 + q:9 + q]).then_inc(at_.probed, 1)
                if n == 0 and between:
                    between()
                if n >= 3:
                    deferred(n - 3)
            for n in range(N - 3, N):
                deferred(n)

        def attention_vector(dve, at_, destination, deferred, between=None, buffer_free=None):
            N = len(at_.items)
            for n in range(N + 2):
                if n < N:
                    q = n % 4
                    dve.wait_ge(at_.scored, n + 1)
                    nc.vector.reduce_max(stat[:, q:q + 1], at_.scores_of(n), AX.X).then_inc(at_.maxed, 1)
                    dve.wait_ge(at_.maxed, n + 1)
                    nc.vector.tensor_scalar(stat[:, 4 + q:5 + q], stat[:, q:q + 1], -at_.scale, None,
                                            ALU.mult).then_inc(at_.negated, 1)
                if n == 0 and between:
                    between()
                if 1 <= n <= N:
                    m = n - 1
                    nk = at_.items[m][2]
                    if m < 2 and buffer_free:
                        buffer_free(m)
                    dve.wait_ge(at_.transposed, m + 1)
                    await_at_least(dve, at_.summed, m - 1)
                    nc.vector.tensor_copy(at_.probsT[:, m % 2, 0:nk * P], transposed_flat[:, 0:nk * P]).then_inc(at_.copied, 1)
                if n >= 2:
                    m = n - 2
                    q = m % 4
                    dve.wait_ge(at_.probed, m + 1)
                    nc.vector.reciprocal(stat[:, 12 + q:13 + q], stat[:, 8 + q:9 + q]).then_inc(at_.inverted, 1)
                    dve.wait_ge(at_.inverted, m + 1)
                    dve.wait_ge(at_.summed, m + 1)
                    destination(m, ps[:, 6 + m % 2, 0:at_.width], stat[:, 12 + q:13 + q]).then_inc(at_.out, 1)
                if n >= 3:
                    deferred(n - 3)
            deferred(N - 1)

        band = Attention("band", [(h, j, min(j + 1, 5)) for j in reversed(range(NT)) for h in range(HEADS_B)], HD_B, 1.0, probs_b, probsT_b)
        mla = [Attention(f"mla{g}", [(4 * g + h, j, j + 1) for j in reversed(range(NT)) for h in range(4)], P, SCALE_C, probs_c, probsT_c)
               for g in range(2)]

        @block.tensor
        def _(pe):
            def tile(stage, i, j, slot, width, column, chunks, rhs, first_wait=None):
                u0, t0, _, inc = base(stage)

                def bank_read(h):
                    await_at_least(pe, s_free[bank_of(stage, j, h)], use_of(stage, i, j))

                def chunk(h, n, c, r):
                    bank, tok = bank_of(stage, j, h), half_of(h)
                    wH = w_high[:, slot, c * width + column:c * width + column + P]
                    wL = w_low[:, slot, c * width + column:c * width + column + P]
                    last_chunk = n == len(chunks) - 1
                    nc.tensor.matmul(ps[:, bank], wH, rhs[0][:, r, tok], start=(n == 0), stop=False)
                    nc.tensor.matmul(ps[:, bank], wH, rhs[1][:, r, tok], start=False, stop=False)
                    last = nc.tensor.matmul(ps[:, bank], wL, rhs[0][:, r, tok], start=False, stop=last_chunk)
                    if last_chunk:
                        last.then_inc(s_mm, inc)

                if first_wait:
                    for h in range(2):
                        bank_read(h)
                    for n, (c, r) in enumerate(chunks):
                        pe.wait_ge(*first_wait(r))
                        for h in range(2):
                            chunk(h, n, c, r)
                else:
                    for h in range(2):
                        bank_read(h)
                        for n, (c, r) in enumerate(chunks):
                            chunk(h, n, c, r)

            def gemm(stage, rhs, ready, hook=None, chunk0=0, after=None, after_limit=None):
                u0, t0, n, T, C = STAGE[stage]

                def unit(i, j, after=None):
                    pe.wait_ge(s_split, 2 * i + (j + u0 + 1))
                    first = isinstance(i, int) and i == 0 and j == 0
                    tile(stage, i, j, (u0 + j) % 2, P, 0, [(c, chunk0 + c) for c in range(C)], rhs, ready if first else None)
                    if first and hook:
                        hook()
                    if after and j == 1:
                        after(i)

                if after_limit is None:
                    items_of(pe, n, lambda i, j: unit(i, j, after))
                else:
                    items_of(pe, after_limit, lambda i, j: unit(i, j, after))
                    items_of(pe, n - 2, unit, after_limit)
                    unit(n // 2 - 1, 0)
                    return lambda: unit(n // 2 - 1, 1)

            def low(q):
                return lambda r: (s_l, 8 * q + r + 1)

            def norm(n, q):
                def hook():
                    pe.wait_ge(*((s_sum0, 8) if n == 0 else (s_l, 8 * q + 8)))
                    for h in range(2):
                        nc.tensor.matmul(ps[:, 4 + h], ones[:], acc[:, half_of(h)], start=True, stop=True).then_inc(s_nsum, 1)
                return hook

            pe.wait_ge(s_const, 48)
            gemm("zqk", (h1H, h1L), low(0), norm(0, 0))

            def band_sums(c):
                if isinstance(c, int) and c == 0:
                    pe.wait_ge(s_bconst, 32)
                pe.wait_ge(s_bsq, c + 1)
                await_at_least(pe, s_brstd, 2 * c)
                for h in range(2):
                    nc.tensor.matmul(ps[:, 4 + h], head_ones[:], tmp[:, half_of(h)], start=True, stop=True).then_inc(s_bsum, 1)

            def beside_gates(i):
                band_sums(i + 2)
                if isinstance(i, int):
                    for t in range(NT):
                        await_at_least(pe, s_vt, t - 1)
                        for c in range(4):
                            last = nc.tensor.transpose(ps[:, 6 + t % 2, c * P:(c + 1) * P], v_raw[:, c, t * P:(t + 1) * P], ident[:])
                        last.then_inc(s_vT, 1)

            gemm("zv", (h1H, h1L), None, after=band_sums)
            last_gate = gemm("gates", (h1H, h1L), None, after=beside_gates, after_limit=12)
            pe.wait_ge(s_vt, NT)
            pe.wait_ge(s_ldone, 4)
            pe.wait_ge(s_bn, DC)
            pe.wait_ge(s_biasL, 1)

            def band_key_order(j, nk):
                near = [j - 1, j] if nk > 1 else [j]
                far = [t for t in (j - 3, j - 2) if t >= 0 and j - t < nk]
                return near + far + ([j - 4] if nk == 5 else [])

            def band_scores(n, bank):
                h, j, nk = band.items[n]
                if n < 2:
                    pe.wait_ge(s_free[bank_of("gates", n, 1)], use_of("gates", 7, n) + 1)
                rows = slice(64 * (h % 2), 64 * (h % 2) + 64)
                q = qk_b[rows, h // 2, j * P:(j + 1) * P]
                order = band_key_order(j, nk)
                near = min(nk, 2)
                out = ps[:, bank, 0:near * P]
                nc.tensor.matmul(out, q, qk_b[rows, 4 + h // 2, order[0] * P:(order[0] + near) * P], start=True, stop=False)
                nc.tensor.matmul(out, ident_r[:], biasH[:, h, 256 - near * P:256], start=False, stop=False)
                last = nc.tensor.matmul(out, ident_r[:], biasL[:, h, 256 - near * P:256], start=False, stop=True)
                far = min(nk, 4) - near
                if far > 0:
                    k0 = order[near] * P
                    last = nc.tensor.matmul(ps[:, bank, 256:256 + far * P], q, qk_b[rows, 4 + h // 2, k0:k0 + far * P], start=True, stop=True)
                if nk == 5:
                    k0 = (j - 4) * P
                    nc.tensor.matmul(ps[:, bank + 1, 0:P], q, qk_b[rows, 4 + h // 2, k0:k0 + P], start=True, stop=False)
                    last = nc.tensor.matmul(ps[:, bank + 1, 0:64], ident_r[:], far_mask_r[:], start=False, stop=True)
                return last

            def band_values(n, k):
                h, j, nk = band.items[n]
                return v_tok[:, band_key_order(j, nk)[k], h * HD_B:(h + 1) * HD_B]

            def band_out_T(m):
                h, j, _ = band.items[m]
                if h == HEADS_B - 1:
                    pe.wait_ge(band.out, m + 1)
                    for c in range(4):
                        last = nc.tensor.transpose(ps[:, 6 + m % 2, c * P:(c + 1) * P], o_tok[m // HEADS_B % 2][:, c * P:(c + 1) * P], ident[:])
                    last.then_inc(band.outT, 1)

            def band_bank_free(m):
                h, j, _ = band.items[m]
                if h == HEADS_B - 1:
                    pe.wait_ge(band.outL, m // HEADS_B + 1)

            attention_tensor(pe, band, band_scores, band_values, band_out_T, band_bank_free, between=last_gate)
            pe.wait_ge(band.outL, NT)

            gemm("za", (h1H, h1L), None)

            pe.wait_ge(s_free[bank_of("za", 1, 1)], use_of("za", 7, 1) + 1)
            for m in range(16):
                half = m % 2
                if m == 1:
                    for c in range(NT):
                        await_at_least(pe, s_iTe, c - 3)
                        for h in range(A_HEADS):
                            k0 = (c * A_HEADS + h) * P
                            last = nc.tensor.transpose(ps[:, 4 + c % 4, h * P:(h + 1) * P], zi[:, k0:k0 + P], ident[:])
                        last.then_inc(s_iT, 1)
                    pe.wait_ge(s_iTe, NT)
                if m >= 2:
                    pe.wait_ge(s_lQ, m - 1)
                for k in range(4):
                    c = 4 * half + k
                    await_at_least(pe, s_lP, 4 * (m - 2) + k + 1)
                    for h in range(A_HEADS):
                        k0 = (c * A_HEADS + h) * P
                        lhs, rhs = (zf, zq) if m < 2 else (hqk, hqk)
                        last = nc.tensor.matmul(ps[:, c, h * P:(h + 1) * P], lhs[:, k0:k0 + P], rhs[:, k0:k0 + P], start=True, stop=True)
                    last.then_inc(s_lS, 1)

            def keys_by_token(c):
                pe.wait_ge(s_kd, c // 4 + 1)
                await_at_least(pe, s_hTe, c - 1)
                for h in range(A_HEADS):
                    k0 = (c * A_HEADS + h) * P
                    last = nc.tensor.transpose(ps[:, c % 2, h * P:(h + 1) * P], k_end[:, k0:k0 + P], ident[:])
                last.then_inc(s_hT, 1)

            def o_norm(c):
                pe.wait_ge(s_h2, c + 1)
                await_at_least(pe, s_hrstd, c - 1)
                nc.tensor.matmul(ps[:, 2 + c % 2], ones[:], o_sq[:, c % 2], start=True, stop=True).then_inc(s_hn, 1)

            pe.wait_ge(s_lP, 60)
            keys_by_token(0)
            pe.wait_ge(s_lP, 64)
            for c in range(NT):
                if c + 1 < NT:
                    keys_by_token(c + 1)
                    pe.wait_ge(s_hTe, c + 1)
                    await_at_least(pe, s_hst, c - 1)
                    for h in range(A_HEADS):
                        k0 = (c * A_HEADS + h) * P
                        last = nc.tensor.matmul(ps[:, 6 + c % 2, h * P:(h + 1) * P], k_end[:, k0:k0 + P], zi[:, k0:k0 + P], start=True, stop=True)
                    last.then_inc(s_hU, 1)
                await_at_least(pe, s_hOe, c - 1)
                await_at_least(pe, s_hst, c)
                if c:
                    pe.wait_ge(s_qe, c // 4 + 1)
                for h in range(A_HEADS):
                    k0 = (c * A_HEADS + h) * P
                    out = ps[:, 4 + c % 2, h * P:(h + 1) * P]
                    last = nc.tensor.matmul(out, zi[:, k0:k0 + P], attn[:, k0:k0 + P], start=True, stop=(c == 0))
                    if c:
                        last = nc.tensor.matmul(out, states[:, (c - 1) % 2, h * P:(h + 1) * P], hd[:, k0:k0 + P], start=False, stop=True)
                last.then_inc(s_hO, 1)
                if c:
                    o_norm(c - 1)
            o_norm(NT - 1)
            pe.wait_ge(s_hrstd, NT)

            u0 = STAGE["merge"][0]
            pe.wait_ge(s_hol, NT)

            def merge(i, j):
                pe.wait_ge(s_split, 2 * i + (j + u0 + 1))
                for part, rhs in enumerate(((oaH, oaL), (obH, obL))):
                    tile("merge", 2 * i + j, part, (u0 + j) % 2, P, 0, [(4 * part + c, c) for c in range(4)], rhs)

            items_of(pe, DC, merge)
            gemm("wout", (mgH, mgL), lambda r: (s_mgl, r + 1))
            for g, n in enumerate(FF_GROUPS):
                pairs0 = sum(FF_GROUPS[:g])
                gemm(f"gu{g}", (h2H, h2L), low(1) if g == 0 else None, norm(1, 1) if g == 0 else None)
                gemm(f"dn{g}", (actH, actL), lambda r, p0=pairs0: (s_actl, p0 + r + 1))

            def wide(stage, rhs, ready, after_second=None):
                u0, t0, n, T, C = STAGE[stage]
                if ready:
                    pe.wait_ge(*ready)
                for u in range(n):
                    pe.wait_ge(s_split, u0 + u + 1)
                    for r in range(T):
                        t = u * T + r
                        tile(stage, t // 2, t % 2, (u0 + u) % 2, T * P, r * P, [(c, c) for c in range(C)], rhs)
                    if u == 1 and after_second:
                        after_second()

            wide("proj", (pH, pL), (s_pl, 2))
            gemm("pleg", (h2H, h2L), low(2), norm(2, 2))

            def rnn_gates(n):
                pe.wait_ge(s_cl, n + 1)
                pe.wait_ge(s_wrl, n + 1)
                await_at_least(pe, s_sg, 2 * n)
                for g in range(2):
                    wH, wL = [w[:, g * P:(g + 1) * P] for w in (w_riH, w_riL)]
                    for h in range(2):
                        bank, tok = 4 + 2 * g + h, half_of(h)
                        nc.tensor.matmul(ps[:, bank], wH, convH[:, tok], start=True, stop=False)
                        nc.tensor.matmul(ps[:, bank], wH, convL[:, tok], start=False, stop=False)
                        nc.tensor.matmul(ps[:, bank], wL, convH[:, tok], start=False, stop=True).then_inc(s_ri, 1)

            gemm("xg", (h4H, h4L), low(3), norm(3, 3), after=rnn_gates)
            gemm("wo1", (yH, yL), lambda r: (s_yl, r + 1))
            gemm("wo2", (yH, yL), lambda r: (s_yl, r + 1), None, 5)
            gemm("dkv", (h5H, h5L), low(5), norm(4, 4))

            def latent(k):
                def hook():
                    chunks = 2 + k
                    for c in range(chunks):
                        pe.wait_ge(s_c2, 2 * k + c + 1)
                        await_at_least(pe, s_crstd, 2 * k)
                        for h in range(2):
                            nc.tensor.matmul(ps[:, 4 + h], ones[:], acc[:, half_of(h)], start=(c == 0), stop=(c == chunks - 1)).then_inc(s_cs, 1)
                return hook

            gemm("cq", (h6H, h6L), low(6), latent(0))
            gemm("cgate", (h6H, h6L), None, latent(1))
            pe.wait_ge(s_cconst, 48)
            pe.wait_ge(s_ldone, 5)
            for h in range(2):
                nc.tensor.matmul(ps[:, 6 + h], rotate[:], tmp[:, half_of(h)], start=True, stop=True).then_inc(s_rot, 1)
            wide("uk", (ckvH, ckvL), (s_cwl, 2))
            u0, t0, _, _, _ = STAGE["uv"]
            for v in range(2):
                pe.wait_ge(s_split, u0 + v + 1)
                for r in range(4):
                    for h in range(2):
                        t = 4 * v + r
                        bank = bank_of("uv", t % 2, h)
                        pe.wait_ge(s_free[bank], use_of("uv", t // 2, t % 2))
                        tok = slice((2 * r + h) * P, (2 * r + h + 1) * P)
                        for c in range(2):
                            wH = w_high[:, (u0 + v) % 2, c * HALF:(c + 1) * HALF]
                            wL = w_low[:, (u0 + v) % 2, c * HALF:(c + 1) * HALF]
                            nc.tensor.matmul(ps[:, bank], ckvH[:, c, tok], wH, start=(c == 0), stop=False)
                            nc.tensor.matmul(ps[:, bank], ckvL[:, c, tok], wH, start=False, stop=False)
                            last = nc.tensor.matmul(ps[:, bank], ckvH[:, c, tok], wL, start=False, stop=(c == 1))
                        last.then_inc(s_mm, 2)
            for g in range(2):
                at_ = mla[g]

                def rotate_queries():
                    pe.wait_ge(s_rq, g + 1)
                    for n in range(4):
                        nc.tensor.matmul(ps[:, 4 + n], rotate[:], q_rope[:, n // 2, half_of(n % 2)], start=True, stop=True).then_inc(s_rotq, 1)

                wide(f"uq{g}", (cqH, cqL), (s_cwl, 5) if g == 0 else None, rotate_queries)
                pe.wait_ge(s_qready, 4 * (g + 1))
                pe.wait_ge(s_free[bank_of(f"uq{g}", 1, 1)], use_of(f"uq{g}", 2, 1) + 1)

                def mla_scores(n, bank):
                    h, j, nk = at_.items[n]
                    hl = h % 4
                    rows = slice(64 * (hl % 2), 64 * (hl % 2) + 64)
                    for b in range((nk + 3) // 4):
                        k0, k1 = b * HALF, min((b + 1) * HALF, nk * P)
                        out = ps[:, bank + b, 0:k1 - k0]
                        diagonal = k1 == nk * P
                        nc.tensor.matmul(out, q_nope[:, hl, j * P:(j + 1) * P], k_nope[:, h, k0:k1], start=True, stop=False)
                        last = nc.tensor.matmul(out, q_rope[rows, hl // 2, j * P:(j + 1) * P], k_rope[rows, k0:k1], start=False, stop=not diagonal)
                        if diagonal:
                            last = nc.tensor.matmul(ps[:, bank + b, k1 - k0 - P:k1 - k0], ident_r[:], causal_r[:], start=False, stop=True)
                    return last

                def mla_values(n, k):
                    h = at_.items[n][0]
                    return v_mla[:, k, h * P:(h + 1) * P]

                def mla_out_T(m):
                    pe.wait_ge(at_.out, m + 1)
                    nc.tensor.transpose(ps[:, 6 + m % 2, 0:P], o_mla[:, m % 2], ident[:]).then_inc(at_.outT, 1)

                attention_tensor(pe, at_, mla_scores, mla_values, mla_out_T, lambda m: pe.wait_ge(at_.outL, m + 1))
                pe.wait_ge(at_.outL, len(at_.items))
            gemm("wob", (y7H, y7L), lambda r: (s_y7l, r + 1))
            norm(5, 7)()

        @block.scalar
        def _(act):
            def split_x(q, x, H, gain, ready=None, squares=True):
                def chunk(i, j):
                    m = 2 * i + j
                    if ready:
                        ready(i, j)
                    if squares:
                        await_at_least(act, s_l, m + (8 * q - 1))
                        last = nc.scalar.activation(sq[:, j], chunk_of(x, m), ACT.Square)
                    if H is not None:
                        last = nc.scalar.activation(chunk_of(H, m), chunk_of(x, m), ACT.Copy, scale=vec[:, bass.ds(m + gain, 1)])
                    last.then_inc(s_h, 1)
                items_of(act, DC, chunk)

            logarithms = [0]

            def inverse_root(items):
                for out, sums, scale, _ in items:
                    nc.scalar.activation(out, sums, ACT.Ln, bias=eps, scale=scale).then_inc(s_ln, 1)
                for k, (out, _, _, done) in enumerate(items):
                    act.wait_ge(s_ln, logarithms[0] + k + 1)
                    nc.scalar.activation(out, out, ACT.Exp, scale=-0.5).then_inc(done, 1)
                logarithms[0] += len(items)

            def norm_rstd(n):
                nc.scalar.activation(derived[0:1, 73:74], eps[0:1], ACT.Ln)
                act.wait_ge(s_nsum, 2 * n + 2)
                inverse_root([(rstd[:, half_of(h)], ps[:, 4 + h], 1.0 / D, s_rstd) for h in range(2)])

            def updated(stage):
                return lambda i, j: act.wait_ge(s_free[bank_of(stage, j, 1)], use_of(stage, i, j) + 1)

            act.dma_start(vec[:], a["vectors"]).then_inc(s_const, 16)
            act.dma_start(ident[:], a["identity"]).then_inc(s_const, 16)
            act.dma_start(ones[:], a["ones"]).then_inc(s_const, 16)
            act.dma_start(head_ones[:], a["head_ones"]).then_inc(s_bconst, 16)
            act.dma_start(far_mask[:], a["far_mask"]).then_inc(s_bconst, 16)
            act.wait_ge(s_const, 48)

            for m in range(DC):
                act.wait_ge(s_x[m // 2], 16)
                nc.scalar.activation(h1H[:, m], x1[:, m], ACT.Copy, scale=V(G_MIX + m)).then_inc(s_h, 1)
            for m in range(DC):
                await_at_least(act, s_sum0, m - 1)
                nc.scalar.activation(sq[:, m % 2], x1[:, m], ACT.Square).then_inc(s_sq0, 1)
            norm_rstd(0)

            nc.scalar.activation(derived[:, 21:31], V(V_LAM, RB), ACT.Abs).then_inc(s_ldone, 1)
            act.wait_ge(s_ldone, 1)
            nc.scalar.activation(derived[:, 31:41], derived[:, 21:31], ACT.Exp, scale=-1.0).then_inc(s_ldone, 1)
            nc.scalar.activation(ident_r[:], ident[:], ACT.Copy).then_inc(s_ldone, 1)
            act.wait_ge(s_bconst, 32)
            nc.scalar.activation(far_mask_r[:], far_mask[:], ACT.Copy).then_inc(s_ldone, 1)

            act.wait_ge(s_free[bank_of("zqk", 1, 1)], use_of("zqk", 3, 1) + 1)

            def head_squares(c):
                await_at_least(act, s_bsum, 2 * c)
                nc.scalar.activation(tmp[:], chunk_of(qk_b, c), ACT.Square).then_inc(s_bsq, 1)

            def head_rstd(c):
                act.wait_ge(s_bsum, 2 * c + 2)
                await_at_least(act, s_bn, c)
                for h in range(2):
                    nc.scalar.activation(acc[:, half_of(h)], ps[:, 4 + h], ACT.Ln, bias=eps, scale=1.0 / HD_B).then_inc(s_bln, 1)
                for h in range(2):
                    act.wait_ge(s_bln, 2 * c + h + 1)
                    nc.scalar.activation(acc[:, half_of(h)], acc[:, half_of(h)], ACT.Exp, scale=-0.5).then_inc(s_brstd, 1)

            def gate(i, j):
                act.wait_ge(s_gz, 2 * i + j + 1)
                nc.scalar.activation(sq[:, j], sq[:, j], ACT.Sigmoid).then_inc(s_gs, 1)
                act.wait_ge(s_gs, 2 * i + j + 1)
                act.dma_start(a["gates"][bass.ds(2 * i + j, 1)].rearrange("u p n -> p (u n)"), sq[:, j]).then_inc(s_gst[j], 16)

            def gate_and_head(i, j):
                if j == 0:
                    head_squares(i + 2)
                gate(i, j)
                if j == 1:
                    if isinstance(i, int):
                        for t in range(NT):
                            act.wait_ge(s_vT, t + 1)
                            nc.scalar.activation(v_tok[:, t], ps[:, 6 + t % 2], ACT.Copy).then_inc(s_vt, 1)
                    head_rstd(i + 2)
                    if isinstance(i, int):
                        act.dma_start(bias[:], a["bias"]).then_inc(s_bconst, 16)
                        act.wait_ge(s_bias, 2 * HEADS_B)
                        nc.scalar.activation(biasH[:], bias[:], ACT.Copy).then_inc(s_biasH, 1)

            for c in range(2):
                head_squares(c)
                head_rstd(c)
            items_of(act, 12, gate_and_head)
            items_of(act, 14, gate, 12)
            gate(7, 0)

            def band_high(m):
                h, j, _ = band.items[m]
                if h == HEADS_B - 1:
                    act.wait_ge(band.outT, m // HEADS_B + 1)
                    nc.scalar.activation(obH[:, :, j * P:(j + 1) * P], ps[:, 6 + m % 2].rearrange("p (c t) -> p c t", c=4), ACT.Copy).then_inc(s_bandH, 1)

            attention_scalar(act, band, band_high, between=lambda: gate(7, 1))

            parts = [slice(k * S, (k + 1) * S) for k in range(4)]
            act.wait_ge(s_free[bank_of("za", 1, 1)], use_of("za", 1, 1) + 1)
            for step, (f, src, scale, bias_) in enumerate(((ACT.Abs, zf, 1.0, 0.0), (ACT.Exp, zq, -1.0, 0.0), (ACT.Ln, zq, 1.0, 1.0))):
                for k, part in enumerate(parts):
                    await_at_least(act, s_ha, 4 * (step - 1) + k + 1)
                    nc.scalar.activation(zq[:, part], src[:, part], f, scale=scale, bias=bias_).then_inc(s_ha, 1)
            for k, part in enumerate(parts):
                act.wait_ge(s_hp, 2 * k + 2)
                nc.scalar.activation(zf[:, part], zq[:, part], ACT.Exp).then_inc(s_hk, 1)
            act.wait_ge(s_free[bank_of("za", 1, 1)], use_of("za", 3, 1) + 1)
            for part in parts:
                nc.scalar.activation(zg[:, part], zg[:, part], ACT.Silu).then_inc(s_hg, 1)
            act.wait_ge(s_free[bank_of("za", 1, 1)], use_of("za", 7, 1) + 1)
            act.dma_start(masks[:], a["masks"]).then_inc(s_hm, 16)

            def decays(n):
                size = LEVELS[n // 2]
                d = hd[:, (n % 2) * 4 * CH:(n % 2 + 1) * 4 * CH].rearrange("p (n two s) -> p n two s", two=2, s=size)
                if n < 2:
                    act.wait_ge(s_lD0, n + 1)
                else:
                    act.wait_ge(s_lD, n - 1)
                nc.scalar.activation(d[:, :, 1], d[:, :, 1], ACT.Exp)
                nc.scalar.activation(d[:, :, 0], d[:, :, 0], ACT.Exp, scale=-1.0).then_inc(s_lE, 1)

            def k_end_decays(k):
                part = slice(k * 4 * CH, (k + 1) * 4 * CH)
                act.wait_ge(s_kb, k + 1)
                nc.scalar.activation(k_end[:, part], k_end[:, part], ACT.Exp, scale=-1.0).then_inc(s_ke, 1)

            for k in range(2):
                decays(k)
                for c in range(4 * k, 4 * k + 4):
                    act.wait_ge(s_iT, c + 1)
                    nc.scalar.activation(zi[:, c * CH:(c + 1) * CH], ps[:, 4 + c % 4], ACT.Copy).then_inc(s_iTe, 1)
            k_end_decays(0)
            for n in range(2, 14):
                decays(n)
            for k in range(2):
                part = slice(k * 4 * CH, (k + 1) * 4 * CH)
                act.wait_ge(s_lQ, 13 + k)
                nc.scalar.activation(hd[:, part], hb[:, part], ACT.Exp).then_inc(s_eb, 1)
            nc.scalar.activation(chunk_decay[:], hb[:].rearrange("p (n t) -> p n t", t=P)[:, :, P - 1], ACT.Exp).then_inc(s_eb, 1)
            k_end_decays(1)

            def keys_copied(c):
                act.wait_ge(s_hT, c + 1)
                nc.scalar.activation(k_end[:, c * CH:(c + 1) * CH], ps[:, c % 2], ACT.Copy).then_inc(s_hTe, 1)

            def o_rstds(m):
                act.wait_ge(s_hn, m + 2)
                await_at_least(act, s_hw, m - 2)
                inverse_root([(o_rstd[:, c % 4], ps[:, 2 + c % 2], 1.0 / P, s_hrstd) for c in (m, m + 1)])

            def oa_high(c):
                act.wait_ge(s_hout, c + 1)
                nc.scalar.activation(oaH[:, :, c * P:(c + 1) * P], o_h[:, c * CH:(c + 1) * CH].rearrange("p (h t) -> p h t", h=4), ACT.Copy).then_inc(s_hoh, 1)

            keys_copied(0)
            for c in range(NT):
                part = slice(c * CH, (c + 1) * CH)
                if c + 1 < NT:
                    keys_copied(c + 1)
                act.wait_ge(s_hO, c + 1)
                nc.scalar.activation(o_h[:, part], ps[:, 4 + c % 2], ACT.Copy, scale=float(P ** -0.5)).then_inc(s_hOe, 1)
                act.wait_ge(s_hOe, c + 1)
                await_at_least(act, s_hn, c - 1)
                nc.scalar.activation(o_sq[:, c % 2], o_h[:, part], ACT.Square).then_inc(s_h2, 1)
                if c in (2, 4, 6):
                    o_rstds(c - 2)
                if c in (4, 6):
                    oa_high(c - 4)
                    oa_high(c - 3)
            o_rstds(6)
            for c in range(4, NT):
                oa_high(c)
            act.wait_ge(s_hol, NT)

            def gates_in(m, j):
                act.dma_start(gate_in[:, j], a["gates"].rearrange("(g m) p n -> m p g n", g=2)[bass.ds(m, 1)].rearrange("m p g n -> p (m g) n")).then_inc(s_gin[j], 16)

            for j in range(2):
                gates_in(j, j)
            act.dma_start(x2[:], a["xT"]).then_inc(s_x2, 16)

            def merged_high(i, j):
                m = 2 * i + j
                act.wait_ge(s_mg, m + 1)
                nc.scalar.activation(chunk_of(mgH, m), gate_in[:, j, 0], ACT.Copy).then_inc(s_mgh, 1)
                act.wait_ge(s_mgl, m + 1)

            for i in range(4):
                for j in range(2):
                    merged_high(i, j)
                    if i < 3:
                        gates_in(2 * i + j + 2, j)
            split_x(1, x2, h2H, G_FFN, updated("wout"))
            norm_rstd(1)
            for g, n in enumerate(FF_GROUPS):
                p0 = sum(FF_GROUPS[:g])
                u0 = f"gu{g}"

                def pair(i, j, p0=p0, u0=u0):
                    m = 2 * i + j
                    act.wait_ge(s_free[bank_of(u0, 0, 1)], m + (STAGE[u0][1] // 2 + 1))
                    nc.scalar.activation(sq[:, 0], sq[:, 0], ACT.Silu).then_inc(s_silu, 1)
                    act.wait_ge(s_act, m + (p0 + 1))
                    nc.scalar.activation(chunk_of(actH, m), tmp[:], ACT.Copy).then_inc(s_acth, 1)

                items_of(act, n, pair)
            act.wait_ge(s_mm, mm_count("dn1", 7, 1))
            act.dma_start(p_in[:], a["pT"]).then_inc(s_x2, 16)
            act.wait_ge(s_x2, 32)
            for c in range(2):
                nc.scalar.activation(pH[:, c], p_in[:, c], ACT.Copy).then_inc(s_ph, 1)
            split_x(2, x2, h2H, G_PLE, updated("dn2"))
            norm_rstd(2)

            def ple(i, j):
                m = 2 * i + j
                act.wait_ge(s_free[bank_of("pleg", j, 1)], use_of("pleg", i, j) + 1)
                nc.scalar.activation(tmp[:], tmp[:], ACT.Sigmoid).then_inc(s_sig, 1)
                act.wait_ge(s_pz, m + 1)
                await_at_least(act, s_l, m + (8 * 3 - 1))
                nc.scalar.activation(sq[:, j], chunk_of(x2, m), ACT.Square)
                nc.scalar.activation(chunk_of(h4H, m), chunk_of(x2, m), ACT.Copy, scale=vec[:, bass.ds(m + G_A, 1)]).then_inc(s_h, 1)
                act.dma_start(chunk_of(a["x_spill_rnn"], m), chunk_of(x2, m)).then_inc(s_xs3, 16)

            items_of(act, DC, ple)
            norm_rstd(3)

            act.wait_ge(s_xs3, DC * 16)
            act.dma_start(w_ri[:], a["rnn_gate_weights"]).then_inc(s_wri, 16)
            act.wait_ge(s_wri, 16)

            def y_high(n):
                act.wait_ge(s_yg, n + 1)
                nc.scalar.activation(chunk_of(yH, n), chunk_of(rgate, n), ACT.Copy).then_inc(s_yh, 1)

            def rnn_block(n, last=False):
                static = isinstance(n, int)
                of = lambda column: vec[:, bass.ds(n + column, 1)]
                derived_of = lambda column: derived[:, bass.ds(n + column, 1)]
                await_at_least(act, s_ri, 4 * n)
                nc.scalar.activation(w_riH[:], w_ri[:, n] if static else w_ri[:, bass.ds(n, 1)], ACT.Copy).then_inc(s_wrh, 1)
                act.wait_ge(s_cv, 4 * n + 4)
                nc.scalar.activation(convH[:], conv[:], ACT.Copy).then_inc(s_ch, 1)
                if not static or n > 0:
                    y_high(n - 1)
                act.wait_ge(s_free[bank_of("xg", 1, 1)], use_of("xg", n, 1) + 1)
                nc.scalar.activation(chunk_of(rgate, n), chunk_of(rgate, n), ACT.Silu).then_inc(s_rg, 1)
                if last:
                    for k in range(4):
                        act.dma_start(x4[:, 2 * k:2 * k + 2], a["x_spill_rnn"][:, 2 * k:2 * k + 2]).then_inc(s_x[k], 16)
                for g, (buf, b) in enumerate(((r_buf, V_BR), (i_buf, V_BI))):
                    act.wait_ge(s_ri, 4 * n + (2 * g + 2))
                    nc.scalar.activation(buf[:], ps[:, 4 + 2 * g:6 + 2 * g].rearrange("p b n -> p (b n)"), ACT.Sigmoid, bias=of(b)).then_inc(s_sg, 1)
                act.wait_ge(s_sg, 2 * n + 2)
                nc.scalar.activation(chunk_of(xb, n), r_buf[:], ACT.Exp, scale=derived_of(1)).then_inc(s_a, 1)
                act.wait_ge(s_a, n + 1)
                nc.scalar.activation(r_buf[:], r_buf[:], ACT.Tanh, scale=derived_of(11)).then_inc(s_T, 1)
                act.wait_ge(s_T, n + 1)
                nc.scalar.activation(r_buf[:], r_buf[:], ACT.Sqrt).then_inc(s_rs, 1)

            rnn_block(0)
            with act.Fori(1, RB - 1) as n:
                rnn_block(n)
            rnn_block(RB - 1, last=True)
            y_high(RB - 1)
            split_x(4, x4, None, 0, updated("wo2"))
            split_x(5, x4, h5H, G_KV, None, False)
            norm_rstd(4)
            split_x(6, x4, h6H, G_B, None, False)
            act.dma_start(a["x_spill_mla"], x4[:]).then_inc(s_xs5, 16)
            n = 0
            for k, (stage, chunks, width, src, H) in enumerate((("dkv", 2, 256, ckv, ckvH), ("cq", 3, 384, cq, cqH))):
                act.wait_ge(s_free[bank_of(stage, 2, 1)], use_of(stage, 0, 2) + 1)
                if k == 0:
                    act.dma_start(rotate[:], a["rotate"]).then_inc(s_cconst, 16)
                    act.dma_start(causal[:], a["causal"]).then_inc(s_cconst, 16)
                else:
                    act.wait_ge(s_cwl, 2)
                for c in range(chunks):
                    await_at_least(act, s_cs, 2 * n)
                    nc.scalar.activation(acc[:], src[:, c], ACT.Square).then_inc(s_c2, 1)
                    n += 1
                act.wait_ge(s_cs, 2 * n)
                inverse_root([(acc[:, half_of(h)], ps[:, 4 + h], 1.0 / width, s_crstd) for h in range(2)])
                for c in range(chunks):
                    act.wait_ge(s_cw, 2 * k + c + 1)
                    nc.scalar.activation(H[:, c], src[:, c], ACT.Copy).then_inc(s_cwh, 1)
            act.wait_ge(s_cwl, 5)
            act.wait_ge(s_cconst, 32)
            act.dma_start(cos_sin[:], a["cos_sin"]).then_inc(s_cconst, 16)
            nc.scalar.activation(causal_r[:], causal[:], ACT.Copy).then_inc(s_ldone, 1)

            def mla_gate(i, j):
                act.wait_ge(s_free[bank_of("cgate", j, 1)], use_of("cgate", i, j) + 1)
                nc.scalar.activation(chunk_of(cgate, 2 * i + j), chunk_of(cgate, 2 * i + j), ACT.Silu).then_inc(s_cg, 1)

            items_of(act, DC, mla_gate)
            for g in range(2):
                attention_scalar(act, mla[g], lambda m: None)
            act.wait_ge(mla[1].outL, len(mla[1].items))
            act.dma_start(x5[:], a["x_spill_mla"]).then_inc(s_xld5, 16)
            for m in range(DC):
                nc.scalar.activation(y7H[:, m], cgate[:, m], ACT.Copy).then_inc(s_y7h, 1)
            split_x(7, x5, None, 0, updated("wob"))
            norm_rstd(5)

        @block.vector
        def _(dve):
            def low_of(L, source, H):
                return nc.vector.tensor_tensor(L, source, f32(H), ALU.subtract)

            def split_x(q, x, H, L, gain, before=None, after_h=True, squares=True):
                def chunk(i, j):
                    m = 2 * i + j
                    if before:
                        before(i, j)
                    dve.wait_ge(s_h, m + (8 * q + 1))
                    if squares:
                        if isinstance(i, int) and m == 0:
                            last = nc.vector.tensor_copy(acc[:], sq[:, j])
                        else:
                            dve.wait_ge(s_l, m + 8 * q)
                            last = nc.vector.tensor_tensor(acc[:], acc[:], sq[:, j], ALU.add)
                    if H is not None:
                        last = nc.vector.scalar_tensor_tensor(out=chunk_of(L, m), in0=chunk_of(x, m), scalar=vec[:, bass.ds(m + gain, 1)],
                                                              in1=f32(chunk_of(H, m)), op0=ALU.mult, op1=ALU.subtract)
                    last.then_inc(s_l, 1)
                items_of(dve, DC, chunk)

            def norm_rstd(n):
                dve.wait_ge(s_rstd, 2 * n + 2)

            def read(stage, i, j, h, operation):
                dve.wait_ge(s_mm, mm_count(stage, 2 * i + j, h))
                bank = bank_of(stage, j, h)
                operation(ps[:, bank]).then_inc(s_free[bank], 1)

            def scaled(stage, destination, start=0, signal=None):
                def one(i, j):
                    for h in range(2):
                        read(stage, i, j, h, lambda p: nc.vector.tensor_tensor(
                            chunk_of(destination, 2 * i + j)[..., half_of(h)], p, rstd[:, half_of(h)], ALU.mult))
                items_of(dve, STAGE[stage][2], one)

            def add_to(stage, x):
                def one(i, j):
                    for h in range(2):
                        xm = chunk_of(x, 2 * i + j)[..., half_of(h)]
                        read(stage, i, j, h, lambda p: nc.vector.tensor_tensor(xm, p, xm, ALU.add))
                return one

            dve.wait_ge(s_const, 48)
            split_x(0, x1, h1H, h1L, G_MIX, squares=False)
            for m in range(DC):
                dve.wait_ge(s_sq0, m + 1)
                if m == 0:
                    nc.vector.tensor_copy(acc[:], sq[:, 0]).then_inc(s_sum0, 1)
                else:
                    dve.wait_ge(s_sum0, m)
                    nc.vector.tensor_tensor(acc[:], acc[:], sq[:, m % 2], ALU.add).then_inc(s_sum0, 1)
            norm_rstd(0)

            scaled("zqk", qk_b)

            chain = [0]

            def link(instruction):
                chain[0] += 1
                instruction.then_inc(s_vchain, 1)
                dve.wait_ge(s_vchain, chain[0])

            
            dve.wait_ge(s_ldone, 2)
            e, s_, s2, poly = derived[:, 31:41], derived[:, 41:51], derived[:, 51:61], derived[:, 61:71]
            link(nc.vector.tensor_scalar(s2, e, 2.0, None, ALU.add))
            link(nc.vector.reciprocal(s_, s2))
            link(nc.vector.tensor_tensor(s_, e, s_, ALU.mult))
            link(nc.vector.tensor_tensor(s2, s_, s_, ALU.mult))
            link(nc.vector.tensor_scalar(poly, s2, 1.0 / 15, 1.0 / 13, ALU.mult, ALU.add))
            for k in (11, 9, 7, 5, 3, 1):
                link(nc.vector.tensor_tensor(poly, poly, s2, ALU.mult))
                link(nc.vector.tensor_scalar(poly, poly, 1.0 / k, None, ALU.add))
            link(nc.vector.tensor_tensor(poly, poly, s_, ALU.mult))
            link(nc.vector.tensor_scalar(s2, V(V_LAM, RB), -1.0, 0.0, ALU.mult, ALU.max))
            link(nc.vector.scalar_tensor_tensor(out=s2, in0=poly, scalar=2.0, in1=s2, op0=ALU.mult, op1=ALU.add))
            link(nc.vector.tensor_scalar(derived[:, 1:11], s2, -8.0, None, ALU.mult))
            link(nc.vector.tensor_scalar(derived[:, 11:21], s2, 4.0, None, ALU.mult))
            for c in range(DC):
                link(nc.vector.tensor_scalar(qk_gains[:, c:c + 1], V(V_QN if c < 4 else V_KN), float(HD_B ** -0.5) if c < 4 else 1.0,
                                             None, ALU.mult))


            def head_normed(c):
                dve.wait_ge(s_brstd, 2 * c + 2)
                nc.vector.scalar_tensor_tensor(out=chunk_of(qk_b, c), in0=chunk_of(qk_b, c), scalar=derived[:, bass.ds(c + 41, 1)],
                                               in1=acc[:], op0=ALU.mult, op1=ALU.mult).then_inc(s_bn, 1)

            for i in range(2):
                for j in range(2):
                    for h in range(2):
                        read("zv", i, j, h, lambda p: nc.vector.tensor_tensor(v_raw[:, 2 * i + j, half_of(h)], p, rstd[:, half_of(h)], ALU.mult))
                head_normed(i)

            def bias_prepared():
                dve.wait_ge(s_bconst, 48)
                for h in range(HEADS_B):
                    nc.vector.tensor_scalar(bias[:, h], bias[:, h], V(V_CFAR + h), None, ALU.subtract).then_inc(s_bias, 1)
                dve.wait_ge(s_bias, HEADS_B)
                for h in range(HEADS_B):
                    nc.vector.memset(bias[0:64, h, 192:256], NEG).then_inc(s_bias, 1)
                dve.wait_ge(s_biasH, 1)
                low_of(biasL[:], bias[:], biasH[:]).then_inc(s_biasL, 1)

            def gate(i, j):
                if not (isinstance(i, int) and i == 0):
                    dve.wait_ge(s_gst[j], i * 16)
                for h in range(2):
                    read("gates", i, j, h, lambda p: nc.vector.tensor_tensor(sq[:, j, half_of(h)], p, rstd[:, half_of(h)], ALU.mult))
                dve.wait_ge(s_free[bank_of("gates", j, 1)], use_of("gates", i, j) + 1)
                dve.nop().then_inc(s_gz, 1)

            def gate_and_head(i, j):
                gate(i, j)
                if j == 1:
                    head_normed(i + 2)
                    if isinstance(i, int):
                        bias_prepared()

            items_of(dve, 12, gate_and_head)
            items_of(dve, 14, gate, 12)
            gate(7, 0)
            def band_destination(m, o, inverse):
                h, j, _ = band.items[m]
                if h == 0:
                    await_at_least(dve, band.outT, m // HEADS_B - 1)
                return nc.vector.tensor_scalar(o_tok[m // HEADS_B % 2][:, h * HD_B:(h + 1) * HD_B], o, inverse, None, ALU.mult)

            def band_low(m):
                h, j, _ = band.items[m]
                if h == HEADS_B - 1:
                    dve.wait_ge(s_bandH, m // HEADS_B + 1)
                    low_of(obL[:, :, j * P:(j + 1) * P], ps[:, 6 + m % 2].rearrange("p (c t) -> p c t", c=4),
                           obH[:, :, j * P:(j + 1) * P]).then_inc(band.outL, 1)

            attention_vector(dve, band, band_destination, band_low, between=lambda: gate(7, 1),
                             buffer_free=lambda m: dve.wait_ge(s_gst[m], 8 * 16))

            for t in range(16):
                w, head = "fgiq"[t // 4], t % 4
                if w == "i" and head == 0:
                    dve.wait_ge(s_hscan, 1)
                if w == "q" and head == 0:
                    dve.wait_ge(s_hk, 4)
                for h in range(2):
                    read("za", t // 2, t % 2, h, lambda p: nc.vector.tensor_tensor(
                        za[w][:, 4 * h:4 * h + 4, head], p.rearrange("p (c t) -> p c t", c=4),
                        rstd[:, half_of(h)].rearrange("p (c t) -> p c t", c=4), ALU.mult))
                if w == "g":
                    part = slice(head * S, (head + 1) * S)
                    dve.wait_ge(s_ha, 9 + head)
                    nc.vector.scalar_tensor_tensor(out=zi[:, part], in0=zf[:, part], scalar=0.0, in1=zq[:, part],
                                                   op0=ALU.min, op1=ALU.subtract).then_inc(s_hp, 1)
                    dve.wait_ge(s_hp, 2 * head + 1)
                    nc.vector.tensor_tensor(zq[:, part], zi[:, part], zf[:, part], ALU.subtract).then_inc(s_hp, 1)
                if t == 7:
                    for n in range(NT * A_HEADS):
                        last = nc.vector.tensor_tensor_scan(out=hb[:, n * P:(n + 1) * P], data0=ones[:], data1=zi[:, n * P:(n + 1) * P],
                                                            initial=0.0, op0=ALU.mult, op1=ALU.add)
                    last.then_inc(s_hscan, 1)
            dve.wait_ge(s_free[bank_of("za", 1, 1)], use_of("za", 7, 1) + 1)
            for n in range(2):
                level_difference(nc.vector, n).then_inc(s_lD0, 1)
            nc.vector.memset(attn[:], 0.0).then_inc(s_hscan, 1)
            dve.wait_ge(s_hscan, 2)
            dve.wait_ge(s_hm, 16)

            def place(m):
                level = 7 if m < 2 else m // 2 - 1
                for k in range(4):
                    c = 4 * (m % 2) + k
                    dve.wait_ge(s_lS, 4 * m + k + 1)
                    nc.vector.copy_predicated(attn[:, c * CH:(c + 1) * CH].rearrange("p (h t) -> p h t", h=A_HEADS),
                                              masks[:, level:level + 1, :].bitcast(mybir.dt.int32).broadcast_to([P, A_HEADS, P]),
                                              ps[:, c].rearrange("p (h t) -> p h t", h=A_HEADS)).then_inc(s_lP, 1)

            def k_to_end(k):
                part = slice(k * 4 * CH, (k + 1) * 4 * CH)
                dve.wait_ge(s_ke, k + 1)
                nc.vector.tensor_tensor(k_end[:, part], k_end[:, part], zf[:, part], ALU.mult).then_inc(s_kd, 1)

            for n in range(14):
                place(n)
                size = LEVELS[n // 2]
                part = slice((n % 2) * 4 * CH, (n % 2 + 1) * 4 * CH)
                two = lambda t: t[:, part].rearrange("p (n two s) -> p n two s", two=2, s=size)
                dve.wait_ge(s_lE, n + 1)
                if n >= 2:
                    dve.wait_ge(s_lS, 4 * n + 4)
                nc.vector.tensor_tensor(two(hqk)[:, :, 1], two(hd)[:, :, 1], two(zq)[:, :, 1], ALU.mult)
                nc.vector.tensor_tensor(two(hqk)[:, :, 0], two(hd)[:, :, 0], two(zf)[:, :, 0], ALU.mult).then_inc(s_lQ, 1)
                if n == 4:
                    k_to_end(0)
            place(14)
            for k in range(2):
                part = slice(k * 4 * CH, (k + 1) * 4 * CH)
                dve.wait_ge(s_eb, k + 1)
                nc.vector.tensor_tensor(hd[:, part], hd[:, part], zq[:, part], ALU.mult).then_inc(s_qe, 1)
                if k == 0:
                    place(15)
            k_to_end(1)
            dve.wait_ge(s_eb, 3)

            def oa_gated(c):
                part = slice(c * CH, (c + 1) * CH)
                dve.wait_ge(s_hrstd, c + 1)
                nc.vector.scalar_tensor_tensor(out=o_h[:, part], in0=o_h[:, part], scalar=V(V_ONORM), in1=o_rstd[:, c % 4],
                                               op0=ALU.mult, op1=ALU.mult).then_inc(s_hw, 1)
                dve.wait_ge(s_hw, c + 1)
                dve.wait_ge(s_hg, 4)
                nc.vector.tensor_tensor(o_h[:, part], o_h[:, part], zg[:, part], ALU.mult).then_inc(s_hout, 1)

            def oa_low(m):
                dve.wait_ge(s_hoh, m + 1)
                low_of(oaL[:, :, m * P:(m + 1) * P], o_h[:, m * CH:(m + 1) * CH].rearrange("p (h t) -> p h t", h=A_HEADS),
                       oaH[:, :, m * P:(m + 1) * P]).then_inc(s_hol, 1)

            for c in range(NT - 1):
                dve.wait_ge(s_hU, c + 1)
                if c == 0:
                    nc.vector.tensor_copy(states[:, 0], ps[:, 6]).then_inc(s_hst, 1)
                else:
                    dve.wait_ge(s_hst, c)
                    dve.wait_ge(s_hO, c)
                    for h in range(A_HEADS):
                        hs = slice(h * P, (h + 1) * P)
                        last = nc.vector.scalar_tensor_tensor(out=states[:, c % 2, hs], in0=states[:, (c - 1) % 2, hs],
                                                              scalar=chunk_decay[:, c * A_HEADS + h:c * A_HEADS + h + 1],
                                                              in1=ps[:, 6 + c % 2, hs], op0=ALU.mult, op1=ALU.add)
                    last.then_inc(s_hst, 1)
                if c in (3, 5):
                    oa_gated(c - 3)
                    oa_gated(c - 2)
                if c == 5:
                    oa_low(0)
                    oa_low(1)
            for c in range(4, NT):
                oa_gated(c)
                oa_low(c - 2)
            for c in range(NT - 2, NT):
                oa_low(c)

            def merge(i, j):
                m = 2 * i + j
                dve.wait_ge(s_gin[j], i * 16 + 16)
                for part in range(2):
                    for h in range(2):
                        dve.wait_ge(s_mm, mm_count("merge", m * 2 + part, h))
                        g = gate_in[:, j, part, half_of(h)]
                        nc.vector.tensor_tensor(g, ps[:, 2 * part + h], g, ALU.mult).then_inc(s_free[2 * part + h], 1)
                dve.wait_ge(s_free[3], m + (STAGE["merge"][1] // 2 + 1))
                nc.vector.tensor_tensor(gate_in[:, j, 0], gate_in[:, j, 0], gate_in[:, j, 1], ALU.add).then_inc(s_mg, 1)
                dve.wait_ge(s_mgh, m + 1)
                low_of(chunk_of(mgL, m), gate_in[:, j, 0], chunk_of(mgH, m)).then_inc(s_mgl, 1)

            items_of(dve, DC, merge)
            dve.wait_ge(s_x2, 16)
            split_x(1, x2, h2H, h2L, G_FFN, add_to("wout", x2))
            norm_rstd(1)
            for g, n in enumerate(FF_GROUPS):
                p0 = sum(FF_GROUPS[:g])
                stage = f"gu{g}"

                def pair(i, j, p0=p0, stage=stage):
                    m = 2 * i + j
                    for part in range(2):
                        for h in range(2):
                            read(stage, m, part, h, lambda p: nc.vector.tensor_tensor(sq[:, part, half_of(h)], p, rstd[:, half_of(h)], ALU.mult))
                    dve.wait_ge(s_silu, m + (p0 + 1))
                    dve.wait_ge(s_free[bank_of(stage, 1, 1)], m + (STAGE[stage][1] // 2 + 1))
                    nc.vector.tensor_tensor(tmp[:], sq[:, 0], sq[:, 1], ALU.mult).then_inc(s_act, 1)
                    dve.wait_ge(s_acth, m + (p0 + 1))
                    low_of(chunk_of(actL, m), tmp[:], chunk_of(actH, m)).then_inc(s_actl, 1)

                items_of(dve, n, pair)
                if g < 2:
                    items_of(dve, DC, add_to(f"dn{g}", x2))
            for c in range(2):
                dve.wait_ge(s_ph, c + 1)
                low_of(pL[:, c], p_in[:, c], pH[:, c]).then_inc(s_pl, 1)
            split_x(2, x2, h2H, h2L, G_PLE, add_to("dn2", x2))
            for t in range(DC):
                if t == 6:
                    dve.wait_ge(s_mm, mm_count("proj", 7, 1))
                for h in range(2):
                    read("proj", t // 2, t % 2, h, lambda p: nc.vector.tensor_copy(proj[:, t, half_of(h)], p))
            norm_rstd(2)

            def ple_add(i, j):
                m = 2 * i + j
                for h in range(2):
                    read("pleg", i, j, h, lambda p: nc.vector.tensor_tensor(tmp[:, half_of(h)], p, rstd[:, half_of(h)], ALU.mult))
                dve.wait_ge(s_sig, m + 1)
                nc.vector.tensor_tensor(tmp[:], tmp[:], chunk_of(proj, m), ALU.mult).then_inc(s_pc, 1)
                dve.wait_ge(s_pc, m + 1)
                nc.vector.tensor_tensor(chunk_of(x2, m), chunk_of(x2, m), tmp[:], ALU.add).then_inc(s_pz, 1)

            split_x(3, x2, h4H, h4L, G_A, ple_add)
            norm_rstd(3)
            dve.wait_ge(s_xs3, DC * 16)

            def project(n, j, destination):
                for h in range(2):
                    read("xg", n, j, h, lambda p: nc.vector.tensor_tensor(
                        chunk_of(destination, n)[..., half_of(h)], p, rstd[:, half_of(h)], ALU.mult))

            def recurrence(n):
                dve.wait_ge(s_rs, n + 1)
                nc.vector.scalar_tensor_tensor(out=r_buf[:], in0=chunk_of(xb, n), scalar=1.0, in1=r_buf[:],
                                               op0=ALU.add, op1=ALU.mult).then_inc(s_rw, 1)
                dve.wait_ge(s_rw, 3 * n + 1)
                nc.vector.tensor_tensor(i_buf[:], i_buf[:], r_buf[:], ALU.mult).then_inc(s_rw, 1)
                dve.wait_ge(s_rw, 3 * n + 2)
                nc.vector.tensor_tensor_scan(out=r_buf[:], data0=xb[:].rearrange("p c t -> p (c t)")[:, bass.ds(n * S, S)], data1=i_buf[:], initial=0.0,
                                             op0=ALU.mult, op1=ALU.add).then_inc(s_rw, 1)
                dve.wait_ge(s_rw, 3 * n + 3)
                dve.wait_ge(s_rg, n + 1)
                nc.vector.tensor_tensor(chunk_of(rgate, n), r_buf[:], chunk_of(rgate, n), ALU.mult).then_inc(s_yg, 1)

            def y_low(n):
                dve.wait_ge(s_yh, n + 1)
                low_of(chunk_of(yL, n), chunk_of(rgate, n), chunk_of(yH, n)).then_inc(s_yl, 1)

            def rnn_block(n):
                first = isinstance(n, int)
                w = lambda k: vec[:, bass.ds(4 * n + (V_CW + k), 1)]
                project(n, 0, xb)
                dve.wait_ge(s_free[bank_of("xg", 0, 1)], use_of("xg", n, 0) + 1)
                await_at_least(dve, s_ix, n)
                x = chunk_of(xb, n)
                nc.vector.tensor_scalar(conv[:], x, w(3), vec[:, bass.ds(n + V_CB, 1)], ALU.mult, ALU.add).then_inc(s_cv, 1)
                for k in (1, 2, 3):
                    dve.wait_ge(s_cv, 4 * n + k)
                    nc.vector.scalar_tensor_tensor(out=conv[:, k:], in0=x[..., 0:S - k], scalar=w(3 - k), in1=conv[:, k:],
                                                   op0=ALU.mult, op1=ALU.add).then_inc(s_cv, 1)
                dve.wait_ge(s_wrh, n + 1)
                low_of(w_riL[:], w_ri[:, n] if first else w_ri[:, bass.ds(n, 1)], w_riH[:]).then_inc(s_wrl, 1)
                dve.wait_ge(s_ch, n + 1)
                low_of(convL[:], conv[:], convH[:]).then_inc(s_cl, 1)
                if not first:
                    recurrence(n - 1)
                project(n, 1, rgate)
                if not first:
                    y_low(n - 1)
                dve.wait_ge(s_sg, 2 * n + 2)
                nc.vector.tensor_tensor(i_buf[:], i_buf[:], conv[:], ALU.mult).then_inc(s_ix, 1)

            rnn_block(0)
            with dve.Fori(1, RB) as n:
                rnn_block(n)
            for j in range(2):
                dve.wait_ge(s_x[0], 32)
                add_to("wo1", x4)(0, j)
            dve.wait_ge(s_ix, RB)
            recurrence(RB - 1)
            y_low(RB - 1)
            for k in range(1, 4):
                dve.wait_ge(s_x[k], 32)
                for j in range(2):
                    add_to("wo1", x4)(k, j)
            split_x(4, x4, None, None, 0, add_to("wo2", x4))
            split_x(5, x4, h5H, h5L, G_KV, squares=False)
            norm_rstd(4)
            split_x(6, x4, h6H, h6L, G_B, squares=False)
            for k, (stage, chunks, src, H, L, gain) in enumerate((("dkv", 2, ckv, ckvH, ckvL, V_KVN), ("cq", 3, cq, cqH, cqL, V_CQN))):
                for t in range(3):
                    for h in range(2):
                        dst = src[:, t, half_of(h)] if t < chunks else tmp[:, half_of(h)]
                        read(stage, t // 2, t % 2, h, lambda p: nc.vector.tensor_tensor(dst, p, rstd[:, half_of(h)], ALU.mult))
                dve.wait_ge(s_crstd, 2 * k + 2)
                for c in range(chunks):
                    nc.vector.scalar_tensor_tensor(out=src[:, c], in0=src[:, c], scalar=V(gain + c), in1=acc[:],
                                                   op0=ALU.mult, op1=ALU.mult).then_inc(s_cw, 1)
                for c in range(chunks):
                    dve.wait_ge(s_cwh, 2 * k + c + 1)
                    low_of(L[:, c], src[:, c], H[:, c]).then_inc(s_cwl, 1)
            dve.wait_ge(s_xs5, 16)
            scaled("cgate", cgate)
            for h in range(2):
                dve.wait_ge(s_rot, h + 1)
                nc.vector.tensor_tensor(sq[:, 0, half_of(h)], ps[:, 6 + h], cos_sin[:, 1, half_of(h)], ALU.mult).then_inc(s_kr, 1)
            nc.vector.tensor_tensor(k_rope[:], tmp[:], cos_sin[:, 0], ALU.mult).then_inc(s_kr, 1)
            dve.wait_ge(s_kr, 3)
            nc.vector.tensor_tensor(k_rope[:], k_rope[:], sq[:, 0], ALU.add).then_inc(s_kr, 1)
            for t in range(DC):
                for h in range(2):
                    read("uk", t // 2, t % 2, h, lambda p: nc.vector.tensor_copy(k_nope[:, t, half_of(h)], p))
            for t in range(DC):
                v, r = t // 4, t % 4
                for h in range(2):
                    read("uv", t // 2, t % 2, h, lambda p: nc.vector.tensor_copy(v_mla[:, 2 * r + h, v * HALF:(v + 1) * HALF], p))
            for g in range(2):
                at_ = mla[g]

                def queries_read(t, dst):
                    for h in range(2):
                        read(f"uq{g}", t // 2, t % 2, h, lambda p: nc.vector.tensor_copy(dst[:, half_of(h)], p))

                for t in range(2):
                    queries_read(t, q_rope[:, t])
                dve.wait_ge(s_free[bank_of(f"uq{g}", 1, 1)], use_of(f"uq{g}", 0, 1) + 1)
                dve.nop().then_inc(s_rq, 1)
                for t in range(2, 4):
                    queries_read(t, q_nope[:, t - 2])
                for n in range(4):
                    t, h = n // 2, n % 2
                    x = q_rope[:, t, half_of(h)]
                    dve.wait_ge(s_rotq, 4 * g + n + 1)
                    nc.vector.tensor_tensor(sq[:, 0, half_of(h)], ps[:, 4 + n], cos_sin[:, 1, half_of(h)], ALU.mult).then_inc(s_rqe, 1)
                    nc.vector.tensor_tensor(x, x, cos_sin[:, 0, half_of(h)], ALU.mult).then_inc(s_rqe, 1)
                    dve.wait_ge(s_rqe, 8 * g + 2 * n + 2)
                    nc.vector.tensor_tensor(x, x, sq[:, 0, half_of(h)], ALU.add).then_inc(s_qready, 1)
                for t in range(4, 6):
                    queries_read(t, q_nope[:, t - 2])
                if g == 0:
                    dve.wait_ge(s_cg, DC)

                def mla_destination(m, o, inverse):
                    await_at_least(dve, at_.outT, m - 1)
                    return nc.vector.tensor_scalar(o_mla[:, m % 2], o, inverse, None, ALU.mult)

                def mla_gated(m):
                    h, j, _ = at_.items[m]
                    dve.wait_ge(at_.outT, m + 1)
                    y = cgate[:, h, j * P:(j + 1) * P]
                    nc.vector.tensor_tensor(y, ps[:, 6 + m % 2, 0:P], y, ALU.mult).then_inc(at_.outL, 1)

                attention_vector(dve, at_, mla_destination, mla_gated)
            for m in range(DC):
                dve.wait_ge(s_y7h, m + 1)
                low_of(y7L[:, m], cgate[:, m], y7H[:, m]).then_inc(s_y7l, 1)
            dve.wait_ge(s_xld5, 16)
            split_x(7, x5, None, None, 0, add_to("wob", x5))
            norm_rstd(5)
            for m in range(DC):
                nc.vector.scalar_tensor_tensor(out=out_sb[:, m], in0=x5[:, m], scalar=V(G_FIN + m), in1=rstd[:],
                                               op0=ALU.mult, op1=ALU.mult).then_inc(s_fin, 1)


def _feature_major(x):
    return np.ascontiguousarray(x.T.reshape(-1, P, x.shape[0]).transpose(1, 0, 2))


def _unit(w):
    u = w.reshape(-1, P, w.shape[1]).transpose(1, 0, 2).reshape(P, -1)
    return np.concatenate([u, np.zeros((P, 1024 - u.shape[1]), np.float32)], axis=1)


def _stream(x):
    col = lambda w, t, n=P: w[:, t * n:(t + 1) * n]
    w_in, wa, wb = x["w_in"][0], x["w_branch_a"][0], x["w_branch_b"][0]
    units = [_unit(col(w_in, t)) for t in list(range(16, 44)) + list(range(4, 8)) + list(range(12, 16)) + list(range(8, 12)) + list(range(4))]
    units += [_unit(np.concatenate([col(wa, m), col(wb, m)])) for m in range(DC)]
    units += [_unit(col(x["w_out"][0], m)) for m in range(DC)]
    f0 = 0
    for n in FF_GROUPS:
        for f in range(f0, f0 + n):
            units += [_unit(col(x["w_ffn_gate"][0], f)), _unit(col(x["w_ffn_up"][0], f))]
        units += [_unit(col(x["w_ffn_down"][0], m)[f0 * P:(f0 + n) * P]) for m in range(DC)]
        f0 += n
    units += [_unit(col(x["w_ple_proj"][0], v, 512)) for v in range(2)]
    units += [_unit(col(x["w_ple_gate"][0], m)) for m in range(DC)]
    units += [_unit(col(x["w_in_a_2"][0], part * RB + n)) for n in range(RB) for part in range(2)]
    for k in range(2):
        units += [_unit(col(x["w_out_a_2"][0], m)[k * 640:(k + 1) * 640]) for m in range(DC)]
    dkv, wb_ = x["w_dkv_2"], x["w_in_b_2"][0]
    units += [_unit(dkv[:, 0:P]), _unit(dkv[:, P:2 * P]), _unit(np.concatenate([dkv[:, 256:320]] * 2, axis=1))]
    units += [_unit(col(wb_, m)) for m in range(11)]
    units += [_unit(col(x["w_uk_2"].reshape(256, 1024), v, 512)) for v in range(2)]
    units += [_unit(col(x["w_uv_2"].reshape(256, 1024), v, 512)) for v in range(2)]
    uq = x["w_uq_2"][0]
    for g in range(2):
        units.append(_unit(uq[:, 4 * g:4 * g + 4, P:].reshape(384, 256)))
        for h in (4 * g, 4 * g + 2):
            units.append(_unit(uq[:, h:h + 2, 0:P].reshape(384, 256)))
    units += [_unit(col(x["w_out_b_2"][0], m)) for m in range(DC)]
    assert len(units) == UNITS
    return np.stack(units)


def _vectors(x):
    cols = lambda v: v.reshape(-1, P).T
    twice = lambda v: np.concatenate([v, v])[:, None]
    parts = [cols(x[n].reshape(-1)) for n in ("norm_mix_g", "norm_ffn_g", "norm_ple_g", "norm_a_2", "norm_kv_2", "norm_b_2", "final_norm_2")]
    parts += [cols(x["hgrn_onorm_g"][0]), twice(x["attn_qnorm_g"][0]), twice(x["attn_knorm_g"][0])]
    parts += [cols(x[n][0]) for n in ("conv_b_2", "lru_lambda_2", "b_rg_2", "b_ig_2")]
    parts.append(x["conv_w_2"][0].reshape(4, RB, P).transpose(2, 1, 0).reshape(P, 4 * RB))
    parts += [cols(x["kv_norm_2"]), cols(x["q_norm_2"][0]), np.full((P, 1), EPS, np.float32)]
    parts.append(np.broadcast_to(x["attn_rel_bias"][0, :, 256], (P, HEADS_B)))
    parts.append(np.ones((P, 1), np.float32))
    return np.ascontiguousarray(np.concatenate(parts, axis=1))


def _constants():
    i = np.arange(P)
    s, t = i[:, None], i[None, :]
    levels = [(s // (2 * n) == t // (2 * n)) & (s % (2 * n) < n) & (t % (2 * n) >= n) for n in LEVELS] + [s == t]
    rotate = np.zeros((P, P), np.float32)
    for b in (0, 64):
        for k in range(32):
            rotate[b + 32 + k, b + k] = -1.0
            rotate[b + k, b + 32 + k] = 1.0
    inv = np.float32(10000.0) ** (-np.arange(0, 64, 2, dtype=np.float32) / np.float32(64))
    angle = np.arange(S, dtype=np.float32)[None, :] * inv[i % 32][:, None]
    return {
        "identity": np.eye(P, dtype=np.float32),
        "ones": np.ones((P, P), np.float32),
        "head_ones": (s // 64 == t // 64).astype(np.float32),
        "far_mask": np.ascontiguousarray(np.broadcast_to(np.where(s >= 64, np.float32(NEG), np.float32(0)), (P, 64))),
        "masks": np.ascontiguousarray(np.stack(levels, axis=1).astype(np.float32)),
        "rotate": rotate,
        "causal": np.where(t > s, np.float32(NEG), np.float32(0)),
        "cos_sin": np.ascontiguousarray(np.stack([np.cos(angle), np.sin(angle)], axis=1).astype(np.float32)),
    }


def _arrays(x):
    t, k = np.arange(P)[:, None], np.arange(256)[None, :]
    arrays = {
        "xT": _feature_major(x["x"][0]),
        "pT": _feature_major(x["p"][0, 0]),
        "weights": _stream(x),
        "vectors": _vectors(x),
        "rnn_gate_weights": np.ascontiguousarray(np.concatenate([x["w_rg_2"][0], x["w_ig_2"][0]], axis=2).transpose(1, 0, 2)),
        "bias": np.ascontiguousarray(x["attn_rel_bias"][0][:, np.clip(t + P - k, -128, 128) + 128].transpose(1, 0, 2)),
    }
    arrays.update(_constants())
    return arrays


def _build(nc, arrays):
    aps = {}
    for name, v in arrays.items():
        aps[name] = nc.dram_tensor(name + "_in", v.shape, mybir.dt.from_np(v.dtype), kind="ExternalInput").ap()
    for name, shape in (("gates", (16, P, S)), ("x_spill_rnn", (P, DC, S)), ("x_spill_mla", (P, DC, S))):
        aps[name] = nc.dram_tensor(name, shape, F32, kind="Internal").ap()
    aps["outT"] = nc.dram_tensor("outT", (P, DC, S), F32, kind="ExternalOutput").ap()
    fused_kernel(nc, aps)


def kernel(**inputs):
    import concourse.bacc as bacc
    from concourse.bass_utils import run_bass_kernel_spmd

    arrays = _arrays({name: np.asarray(v) for name, v in inputs.items()})
    nc = bacc.Bacc("TRN2", target_bir_lowering=False, num_devices=1)
    _build(nc, arrays)
    r = run_bass_kernel_spmd(nc, [{name + "_in": v for name, v in arrays.items()}], core_ids=[0])
    out = np.asarray(r.results[0]["outT"])
    return np.ascontiguousarray(out.transpose(1, 0, 2).reshape(D, S).T)[None]
```
